# Optimizing a Trainium2 kernel written in Bass

```python
import math
import jax, jax.numpy as jnp
from jax import lax
import numpy as np

D_MODEL = 1024
BATCH = 1
SEQ = 256
DEPTH = 2

N_MIXERS = 2
N_META = 16
D_FF = 2816
CONV_WIDTH = 3
HEAD_DIM = 64
V_DIM = 2 * HEAD_DIM
N_HEADS = D_MODEL // (2 * HEAD_DIM)
ROT_DIM = HEAD_DIM // 4
ROPE_THETA = 500000.0
Q_BLOCK = 128
FRONT_PAD = Q_BLOCK - N_META
N_CONV_LAYERS = (DEPTH + N_MIXERS - 1) // N_MIXERS
N_ATTN_LAYERS = DEPTH // N_MIXERS
NORM_EPS = 1e-6
SUBLN_EPS = 1e-5
NEG_INF = -1e30


def rms_norm(t, g, eps=NORM_EPS):
    t32 = t.astype(jnp.float32)
    t32 = t32 * lax.rsqrt(jnp.mean(t32 * t32, axis=-1, keepdims=True) + eps)
    return t32.astype(t.dtype) * g.astype(t.dtype)

def swiglu(h, w_gu, w_down):
    g, u = jnp.split(h @ w_gu, 2, axis=-1)
    return (jax.nn.silu(g) * u) @ w_down

def short_conv_mixer(h, w_in, conv_w, w_out):
    b, c, xt = jnp.split(h @ w_in, 3, axis=-1)
    u = c * xt
    u = lax.conv_general_dilated(
        u, conv_w[:, None, :].astype(u.dtype),
        window_strides=(1,), padding=((CONV_WIDTH - 1, 0),),
        dimension_numbers=('NWC', 'WIO', 'NWC'),
        feature_group_count=u.shape[-1])
    return (b * u) @ w_out

def partial_rope(t, cos, sin):
    half = ROT_DIM // 2
    t1 = t[..., :half]
    t2 = t[..., half:ROT_DIM]
    c = cos[None, :, None, None, :]
    s = sin[None, :, None, None, :]
    return jnp.concatenate([t1 * c - t2 * s, t1 * s + t2 * c, t[..., ROT_DIM:]], axis=-1)

def diff_attention_mixer(h, w_qkv, lam_p, subln_g, w_o, lambda_init):
    bsz, seq_len, d = h.shape
    dt = h.dtype
    q, k, v = jnp.split(h @ w_qkv, 3, axis=-1)
    q = q.reshape(bsz, seq_len, N_HEADS, 2, HEAD_DIM)
    k = k.reshape(bsz, seq_len, N_HEADS, 2, HEAD_DIM)
    v = v.reshape(bsz, seq_len, N_HEADS, V_DIM)
    pos = jnp.arange(seq_len, dtype=jnp.float32)
    inv_freq = ROPE_THETA ** (-jnp.arange(0, ROT_DIM, 2, dtype=jnp.float32) / ROT_DIM)
    ang = pos[:, None] * inv_freq[None, :]
    cos = jnp.cos(ang).astype(dt)
    sin = jnp.sin(ang).astype(dt)
    q = partial_rope(q, cos, sin)
    k = partial_rope(k, cos, sin)
    q = jnp.pad(q, ((0, 0), (FRONT_PAD, 0), (0, 0), (0, 0), (0, 0))).transpose(0, 2, 3, 1, 4)
    k = jnp.pad(k, ((0, 0), (FRONT_PAD, 0), (0, 0), (0, 0), (0, 0))).transpose(0, 2, 3, 1, 4)
    v = jnp.pad(v, ((0, 0), (FRONT_PAD, 0), (0, 0), (0, 0))).transpose(0, 2, 1, 3)
    lp = seq_len + FRONT_PAD
    lam32 = lam_p.astype(jnp.float32)
    lam = (jnp.exp(jnp.sum(lam32[0] * lam32[1])) - jnp.exp(jnp.sum(lam32[2] * lam32[3]))
           + lambda_init)
    scale = HEAD_DIM ** -0.5
    outs = []
    for j in range(lp // Q_BLOCK):
        q0, q1 = j * Q_BLOCK, (j + 1) * Q_BLOCK
        qb = q[:, :, :, q0:q1]
        kb = k[:, :, :, :q1]
        vb = v[:, :, :q1]
        s = jnp.einsum('bhcqd,bhckd->bhcqk', qb, kb).astype(jnp.float32) * scale
        qi = jnp.arange(q0, q1)[:, None]
        ki = jnp.arange(q1)[None, :]
        mask = (ki <= qi) & (ki >= FRONT_PAD)
        p = jax.nn.softmax(jnp.where(mask, s, NEG_INF), axis=-1)
        a = p[:, :, 0] - lam * p[:, :, 1]
        outs.append(jnp.einsum('bhqk,bhkv->bhqv', a.astype(dt), vb))
    o = jnp.concatenate(outs, axis=2)[:, :, FRONT_PAD:]
    o = rms_norm(o, subln_g, SUBLN_EPS) * (1.0 - lambda_init)
    o = o.transpose(0, 2, 1, 3).reshape(bsz, seq_len, d)
    return o @ w_o

def first_inputs(seed: int = 0) -> dict:
    key = jax.random.key(seed)
    ks = jax.random.split(key, 20)

    def nrm(k, shape, scale):
        return jax.random.normal(k, shape, jnp.float32) * scale

    def gains(k, shape):
        return 1.0 + nrm(k, shape, 0.02)

    D = D_MODEL
    return {
        'x': nrm(ks[0], (BATCH, SEQ, D), 1.0),
        'meta_tokens': nrm(ks[1], (N_META, D), 1.0),
        'ln_ffn1': gains(ks[2], (DEPTH, 2, D)),
        'ffn1_w_gu': nrm(ks[3], (DEPTH, D, 2 * D_FF), D ** -0.5),
        'ffn1_w_down': nrm(ks[4], (DEPTH, D_FF, D), D_FF ** -0.5),
        'ln_mix': gains(ks[5], (DEPTH, 2, D)),
        'conv_w_in': nrm(ks[6], (N_CONV_LAYERS, D, 3 * D), D ** -0.5),
        'conv_w': nrm(ks[7], (N_CONV_LAYERS, CONV_WIDTH, D), CONV_WIDTH ** -0.5),
        'conv_w_out': nrm(ks[8], (N_CONV_LAYERS, D, D), D ** -0.5),
        'attn_w_qkv': nrm(ks[9], (N_ATTN_LAYERS, D, 3 * D), D ** -0.5),
        'attn_lambda': nrm(ks[10], (N_ATTN_LAYERS, 4, HEAD_DIM), 0.1),
        'attn_subln_g': gains(ks[11], (N_ATTN_LAYERS, V_DIM)),
        'attn_w_o': nrm(ks[12], (N_ATTN_LAYERS, D, D), D ** -0.5),
        'ln_ffn2': gains(ks[13], (DEPTH, 2, D)),
        'ffn2_w_gu': nrm(ks[14], (DEPTH, D, 2 * D_FF), D ** -0.5),
        'ffn2_w_down': nrm(ks[15], (DEPTH, D_FF, D), D_FF ** -0.5),
    }

def first_block(x, meta_tokens, ln_ffn1, ffn1_w_gu, ffn1_w_down, ln_mix,
              conv_w_in, conv_w, conv_w_out, attn_w_qkv, attn_lambda,
              attn_subln_g, attn_w_o, ln_ffn2, ffn2_w_gu, ffn2_w_down):
    bsz = x.shape[0]
    meta = jnp.broadcast_to(meta_tokens.astype(x.dtype)[None], (bsz, N_META, x.shape[-1]))
    h = jnp.concatenate([meta, x], axis=1)
    for i in range(DEPTH):
        f = swiglu(rms_norm(h, ln_ffn1[i, 0]), ffn1_w_gu[i], ffn1_w_down[i])
        h = h + 0.5 * rms_norm(f, ln_ffn1[i, 1])
        hn = rms_norm(h, ln_mix[i, 0])
        j = i // N_MIXERS
        if i % N_MIXERS == 0:
            m = short_conv_mixer(hn, conv_w_in[j], conv_w[j], conv_w_out[j])
        else:
            lambda_init = 0.8 - 0.6 * math.exp(-0.3 * i)
            m = diff_attention_mixer(hn, attn_w_qkv[j], attn_lambda[j],
                                     attn_subln_g[j], attn_w_o[j], lambda_init)
        h = h + rms_norm(m, ln_mix[i, 1])
        f = swiglu(rms_norm(h, ln_ffn2[i, 0]), ffn2_w_gu[i], ffn2_w_down[i])
        h = h + 0.5 * rms_norm(f, ln_ffn2[i, 1])
    return h[:, N_META:]


DEPTH_2 = 1

HEAD_DIM_2 = 128
DSA_HEADS = 4
MOBA_HEADS = 4
IDX_HEADS = 8
IDX_DIM = 64
DSA_TOPK_MAX = 256
MOBA_BLOCK = 256
MOBA_TOPK = 3
D_FF_2 = -(-8 * D_MODEL // 768) * 256
ROPE_THETA_2 = 10000.0
EPS = 1e-6
NEG = -1e30
DSA_Q_BLOCK = 128
MOBA_Q_BLOCK = 32
DSA_W = DSA_HEADS * HEAD_DIM_2
MOBA_W = MOBA_HEADS * HEAD_DIM_2
IN_SIZES = (DSA_W, DSA_W, DSA_W, IDX_HEADS * IDX_DIM, IDX_DIM, IDX_HEADS,
            MOBA_W, MOBA_W, MOBA_W, D_MODEL, D_MODEL)
IN_W = sum(IN_SIZES)
N_MOD = 6


def rms_norm_2(x, gain):
    xf = x.astype(jnp.float32)
    y = xf * lax.rsqrt(jnp.mean(xf * xf, axis=-1, keepdims=True) + EPS)
    return (y * gain.astype(jnp.float32)).astype(x.dtype)

def rope_tables(seq, dim):
    inv = ROPE_THETA_2 ** (-jnp.arange(0, dim, 2, dtype=jnp.float32) / dim)
    ang = jnp.arange(seq, dtype=jnp.float32)[:, None] * inv[None, :]
    return jnp.cos(ang)[:, None, :], jnp.sin(ang)[:, None, :]

def apply_rope(x, cos, sin):
    x1, x2 = jnp.split(x.astype(jnp.float32), 2, axis=-1)
    return jnp.concatenate([x1 * cos - x2 * sin, x2 * cos + x1 * sin], axis=-1).astype(x.dtype)

def dsa_attention(q, k, v, qi, ki, wi):
    B, S, H, Dh = q.shape
    topk = min(DSA_TOPK_MAX, S // 4)
    nq = S // DSA_Q_BLOCK
    scale = Dh ** -0.5
    key_pos = jnp.arange(S)
    bi = jnp.arange(B)[:, None, None]

    def chunks(a):
        return jnp.moveaxis(a.reshape(a.shape[0], nq, DSA_Q_BLOCK, *a.shape[2:]), 1, 0)

    def block(args):
        qb, qib, wib, t = args
        logits = jnp.einsum('bqhd,bsd->bqhs', qib, ki).astype(jnp.float32)
        score = jnp.einsum('bqh,bqhs->bqs', wib.astype(jnp.float32), jax.nn.relu(logits))
        score = jnp.where((key_pos[None, :] <= t[:, None])[None], score, NEG)
        _, sel = lax.top_k(score, topk)
        ks = k[bi, sel]
        vs = v[bi, sel]
        s = jnp.einsum('bqhd,bqkhd->bhqk', qb, ks).astype(jnp.float32) * scale
        valid = sel <= t[None, :, None]
        s = jnp.where(valid[:, None], s, NEG)
        p = jax.nn.softmax(s, axis=-1).astype(v.dtype)
        return jnp.einsum('bhqk,bqkhd->bqhd', p, vs)

    t_c = jnp.arange(S).reshape(nq, DSA_Q_BLOCK)
    out = lax.map(block, (chunks(q), chunks(qi), chunks(wi), t_c))
    return jnp.moveaxis(out, 0, 1).reshape(B, S, H * Dh)

def moba_attention(q, k, v):
    B, S, H, Dh = q.shape
    nb = -(-S // MOBA_BLOCK)
    pad = nb * MOBA_BLOCK - S
    scale = Dh ** -0.5
    qh = q.transpose(0, 2, 1, 3)
    padw = ((0, 0), (0, 0), (0, pad), (0, 0))
    kh = jnp.pad(k.transpose(0, 2, 1, 3), padw).reshape(B, H, nb, MOBA_BLOCK, Dh)
    vh = jnp.pad(v.transpose(0, 2, 1, 3), padw).reshape(B, H, nb, MOBA_BLOCK, Dh)
    own = (jnp.arange(S) // MOBA_BLOCK).astype(jnp.int32)
    own_b = jnp.broadcast_to(own[:, None], (B, H, S, 1))
    n_sel = min(MOBA_TOPK, nb - 1)
    if n_sel > 0:
        kmean = jnp.mean(kh.astype(jnp.float32), axis=3)
        gate = jnp.einsum('bhsd,bhnd->bhsn', qh.astype(jnp.float32), kmean)
        past = jnp.arange(nb)[None, :] < own[:, None]
        gate = jnp.where(past, gate, NEG)
        _, sel = lax.top_k(gate, n_sel)
        blocks = jnp.concatenate([sel.astype(jnp.int32), own_b], axis=-1)
        bvalid = jnp.concatenate([sel < own[:, None], jnp.ones((B, H, S, 1), bool)], axis=-1)
    else:
        blocks = own_b
        bvalid = jnp.ones((B, H, S, 1), bool)
    nq = S // MOBA_Q_BLOCK
    bi = jnp.arange(B)[:, None, None, None]
    hi = jnp.arange(H)[None, :, None, None]
    offs = jnp.arange(MOBA_BLOCK)

    def chunks(a):
        return jnp.moveaxis(a.reshape(B, H, nq, MOBA_Q_BLOCK, *a.shape[3:]), 2, 0)

    def block(args):
        qb, bl, bv, t = args
        kg = kh[bi, hi, bl]
        vg = vh[bi, hi, bl]
        s = jnp.einsum('bhqd,bhqnkd->bhqnk', qb, kg).astype(jnp.float32) * scale
        kpos = bl[..., None] * MOBA_BLOCK + offs
        mask = bv[..., None] & (kpos <= t[:, None, None])
        s = jnp.where(mask, s, NEG)
        shp = s.shape
        p = jax.nn.softmax(s.reshape(shp[0], shp[1], shp[2], -1), axis=-1).reshape(shp).astype(v.dtype)
        return jnp.einsum('bhqnk,bhqnkd->bhqd', p, vg)

    t_c = jnp.arange(S).reshape(nq, MOBA_Q_BLOCK)
    out = lax.map(block, (chunks(qh), chunks(blocks), chunks(bvalid), t_c))
    out = jnp.moveaxis(out, 0, 2).reshape(B, H, S, Dh)
    return out.transpose(0, 2, 1, 3).reshape(B, S, H * Dh)

def second_inputs(seed: int = 0) -> dict:
    key = jax.random.key(seed)
    ks = jax.random.split(key, 16)
    f32 = jnp.float32

    def w(k, shape, fan_in):
        return jax.random.normal(k, shape, f32) * fan_in ** -0.5

    def gain(k, shape):
        return 1.0 + 0.02 * jax.random.normal(k, shape, f32)

    return {
        "x": jax.random.normal(ks[0], (BATCH, SEQ, D_MODEL), f32),
        "c": jax.random.normal(ks[1], (BATCH, D_MODEL), f32),
        "w_mod": w(ks[2], (DEPTH_2, D_MODEL, N_MOD * D_MODEL), D_MODEL),
        "b_mod": 0.02 * jax.random.normal(ks[3], (DEPTH_2, N_MOD * D_MODEL), f32),
        "g_mix_norm": gain(ks[4], (DEPTH_2, D_MODEL)),
        "g_ffn_norm": gain(ks[5], (DEPTH_2, D_MODEL)),
        "w_in": w(ks[6], (DEPTH_2, D_MODEL, IN_W), D_MODEL),
        "g_q_dsa": gain(ks[7], (DEPTH_2, HEAD_DIM_2)),
        "g_k_dsa": gain(ks[8], (DEPTH_2, HEAD_DIM_2)),
        "g_q_moba": gain(ks[9], (DEPTH_2, HEAD_DIM_2)),
        "g_k_moba": gain(ks[10], (DEPTH_2, HEAD_DIM_2)),
        "w_br_dsa": w(ks[11], (DEPTH_2, DSA_W, D_MODEL), DSA_W),
        "w_br_moba": w(ks[12], (DEPTH_2, MOBA_W, D_MODEL), MOBA_W),
        "w_out": w(ks[13], (DEPTH_2, D_MODEL, D_MODEL), D_MODEL),
        "w_gate_up": w(ks[14], (DEPTH_2, D_MODEL, 2 * D_FF_2), D_MODEL),
        "w_down": w(ks[15], (DEPTH_2, D_FF_2, D_MODEL), D_FF_2),
    }

def second_block(x, c, w_mod, b_mod, g_mix_norm, g_ffn_norm, w_in, g_q_dsa, g_k_dsa,
              g_q_moba, g_k_moba, w_br_dsa, w_br_moba, w_out, w_gate_up, w_down):
    B, S, _ = x.shape
    cos_h, sin_h = rope_tables(S, HEAD_DIM_2)
    cos_i, sin_i = rope_tables(S, IDX_DIM)
    split_at = np.cumsum(IN_SIZES)[:-1].tolist()
    idx_w_scale = (IDX_HEADS ** -0.5) * (IDX_DIM ** -0.5)
    for l in range(DEPTH_2):
        mod = jax.nn.silu(c) @ w_mod[l] + b_mod[l]
        sh_m, sc_m, gt_m, sh_f, sc_f, gt_f = [m[:, None, :] for m in jnp.split(mod, N_MOD, axis=-1)]

        h = rms_norm_2(x, g_mix_norm[l]) * (1.0 + sc_m) + sh_m
        proj = h @ w_in[l]
        (q_a, k_a, v_a, q_i, k_i, w_i, q_b, k_b, v_b, gate_a, gate_b) = jnp.split(proj, split_at, axis=-1)
        q_a = apply_rope(rms_norm_2(q_a.reshape(B, S, DSA_HEADS, HEAD_DIM_2), g_q_dsa[l]), cos_h, sin_h)
        k_a = apply_rope(rms_norm_2(k_a.reshape(B, S, DSA_HEADS, HEAD_DIM_2), g_k_dsa[l]), cos_h, sin_h)
        v_a = v_a.reshape(B, S, DSA_HEADS, HEAD_DIM_2)
        q_i = apply_rope(q_i.reshape(B, S, IDX_HEADS, IDX_DIM), cos_i, sin_i)
        k_i = apply_rope(k_i[:, :, None, :], cos_i, sin_i)[:, :, 0, :]
        w_i = w_i * idx_w_scale
        o_a = dsa_attention(q_a, k_a, v_a, q_i, k_i, w_i)

        q_b = apply_rope(rms_norm_2(q_b.reshape(B, S, MOBA_HEADS, HEAD_DIM_2), g_q_moba[l]), cos_h, sin_h)
        k_b = apply_rope(rms_norm_2(k_b.reshape(B, S, MOBA_HEADS, HEAD_DIM_2), g_k_moba[l]), cos_h, sin_h)
        v_b = v_b.reshape(B, S, MOBA_HEADS, HEAD_DIM_2)
        o_b = moba_attention(q_b, k_b, v_b)

        merged = (jax.nn.sigmoid(gate_a) * (o_a @ w_br_dsa[l])
                  + jax.nn.sigmoid(gate_b) * (o_b @ w_br_moba[l]))
        x = x + gt_m * (merged @ w_out[l])

        h = rms_norm_2(x, g_ffn_norm[l]) * (1.0 + sc_f) + sh_f
        g_ff, u_ff = jnp.split(h @ w_gate_up[l], 2, axis=-1)
        x = x + gt_f * ((jax.nn.silu(g_ff) * u_ff) @ w_down[l])
    return x


def setup_inputs(seed=0):
    out = dict(first_inputs(seed))
    for name, value in second_inputs(seed + 1).items():
        if name != "x":
            out[name + "_2"] = value
    return out


def reference(
    x, meta_tokens, ln_ffn1, ffn1_w_gu, ffn1_w_down, ln_mix, conv_w_in, conv_w, conv_w_out,
    attn_w_qkv, attn_lambda, attn_subln_g, attn_w_o, ln_ffn2, ffn2_w_gu, ffn2_w_down, c_2,
    w_mod_2, b_mod_2, g_mix_norm_2, g_ffn_norm_2, w_in_2, g_q_dsa_2, g_k_dsa_2, g_q_moba_2,
    g_k_moba_2, w_br_dsa_2, w_br_moba_2, w_out_2, w_gate_up_2, w_down_2,
):
    x = first_block(
        x, meta_tokens, ln_ffn1, ffn1_w_gu, ffn1_w_down, ln_mix, conv_w_in, conv_w, conv_w_out,
        attn_w_qkv, attn_lambda, attn_subln_g, attn_w_o, ln_ffn2, ffn2_w_gu, ffn2_w_down,
    )
    return second_block(
        x, c_2, w_mod_2, b_mod_2, g_mix_norm_2, g_ffn_norm_2, w_in_2, g_q_dsa_2, g_k_dsa_2,
        g_q_moba_2, g_k_moba_2, w_br_dsa_2, w_br_moba_2, w_out_2, w_gate_up_2, w_down_2,
    )


_drawn_inputs = setup_inputs


def setup_inputs(seed=0):
    import zlib

    import numpy as np

    out = dict(_drawn_inputs(seed))
    spreads = {}
    factors = {'attn_subln_g': 4.648,
     'ln_ffn2': 3.121,
     'b_mod_2': 3.16,
     'g_mix_norm_2': 8.0,
     'g_ffn_norm_2': 6.875,
     'g_q_dsa_2': 8.0,
     'g_k_dsa_2': 8.0,
     'g_q_moba_2': 8.0,
     'g_k_moba_2': 8.0}
    for name, (base, spread) in spreads.items():
        noise = np.random.default_rng([zlib.crc32(name.encode()), seed]).standard_normal(out[name].shape)
        drawn = base * np.exp(spread * noise) if base else spread * noise
        out[name] = __import__('jax').numpy.asarray(drawn.astype(out[name].dtype))
    for name, factor in factors.items():
        out[name] = (out[name] * factor).astype(out[name].dtype)
    return out
```

```python
import math
from contextlib import ExitStack

import numpy as np

import concourse.bass as bass
from concourse import mybir

F32, F32R, BF16 = mybir.dt.float32, mybir.dt.float32r, mybir.dt.bfloat16
ACT = mybir.ActivationFunctionType
ALU = mybir.AluOpType
AX = mybir.AxisListType

P = 128
D = 1024
KT = D // P
SEQ, META = 256, 16
TOK = SEQ + META
FF = 2816
FT = FF // P
UNIT = 2048
RING = 4
GROUP = 4
NEG = -1e30
TAKEN = -3e38
LAMBDA_INIT = 0.8 - 0.6 * math.exp(-0.3)
EPS, SUBLN_EPS = 1e-6, 1e-5
HEADS1, HEADS2, IDX_HEADS = 8, 4, 8
TOPK = min(256, SEQ // 4)
IDX_SCALE = (IDX_HEADS ** -0.5) * (64 ** -0.5)
MOD_UNITS = 24
MOD_PARTS = 4
MOD_PER = MOD_UNITS // MOD_PARTS

V_LN = 0
V_CONV = V_LN + 96
V_BMOD = V_CONV + 24
V_GMIX = V_BMOD + 48
V_GFFN = V_GMIX + 8
V_GQK = V_GFFN + 8
V_SUB = V_GQK + 4
V_C = V_SUB + 1
V_LAM = V_C + 8
V_ALL = V_LAM + 4
C_ONES, C_IDENT, C_ROT1, C_ROT2, C_ROTI, C_COS1, C_SIN1, C_MASK = 0, 128, 256, 384, 512, 640, 912, 1184
C_ALL = C_MASK + TOK


class Stage:

    def __init__(self, plan, name, units, tiles, tokens, k_outer, quad_banks=False):
        self.name, self.units, self.tiles, self.T = name, units, tiles, tokens
        self.u0, self.t0 = plan["u"], plan["t"]
        self.quad = quad_banks
        self.first_fresh = plan["quad"] or quad_banks
        plan["u"] += units
        plan["t"] += tiles
        plan["quad"] = quad_banks
        done = self.t0
        for n in range(units):
            if k_outer:
                last = n == units - 1
            elif name == "w_in":
                last = n % 2 == 0
            else:
                last = n % 2 == 1
            if last:
                done += 8 if k_outer else GROUP
                plan["used"].append(("tile_done", done))
            else:
                plan["mid"] += 1
                plan["used"].append(("weights_used", plan["mid"]))

    def bank(self, t):
        return (t - self.t0) % 4 if self.quad else t % 8


def build(nc, w_units, mod_units, x_in, vectors, constants, tables2, out):
    ctx = ExitStack()
    with ctx:
        def sb(name, shape, dt=F32):
            return ctx.enter_context(nc.sbuf_tensor(name, shape, dt))

        def sem(name):
            return ctx.enter_context(nc.semaphore(name))

        plan = {"u": 0, "t": 0, "quad": False, "mid": 0, "used": []}
        stages = {}

        def stage(name, key, units, tiles, tokens, k_outer, quad=False):
            stages[key] = Stage(plan, name, units, tiles, tokens, k_outer, quad)

        for layer in range(2):
            stage("gate_up", ("up", 2 * layer), 22, 44, TOK, False)
            stage("down", ("down", 2 * layer), 11, 8, TOK, True)
            if layer == 0:
                stage("conv_in", "conv_in", 12, 24, TOK, False)
                stage("proj", "conv_out", 4, 8, TOK, True)
                stage("gate_up", ("up", 1), 22, 44, TOK, False)
                stage("down", ("down", 1), 11, 8, TOK, True)
            else:
                stage("qkv", "qkv", 12, 24, TOK, False, True)
                stage("proj", "attn_out", 4, 8, SEQ, True)
                stage("gate_up", ("up", 3), 22, 44, SEQ, False)
                stage("down", ("down", 3), 11, 8, SEQ, True)
        stage("w_in", "w_in", 23, 48, SEQ, False, True)
        stage("proj", "br_dsa", 2, 8, SEQ, True)
        stage("proj", "br_moba", 2, 8, SEQ, True)
        stage("proj", "w_out", 4, 8, SEQ, True)
        stage("gate_up", ("up", 4), 22, 44, SEQ, False)
        stage("down", ("down", 4), 11, 8, SEQ, True)
        n_units = plan["u"]
        assert n_units % RING == 0
        S0, I0, E0, A0, X0 = {}, {}, {}, {}, {}
        silus = given = events = a_tiles = x_tiles = 0
        for key, n_silu, n_event, n_tiles, x in (
                (("up", 0), 11, 11, FT, 8), ("conv_in", 0, 4, 8, 8), (("up", 1), 11, 11, FT, 8),
                (("up", 2), 11, 11, FT, 8), ("qkv", 0, 2, 8, 8), (("up", 3), 11, 11, FT, 8),
                ("w_in", 0, 2, 8, 8), ("br", 0, 4, 8, 0), (("up", 4), 11, 11, FT, 8)):
            S0[key], I0[key], E0[key], A0[key], X0[key] = silus, given, events, a_tiles, x_tiles
            given += n_event if key != "w_in" else 0
            silus, events, a_tiles, x_tiles = silus + n_silu, events + n_event, a_tiles + n_tiles, x_tiles + x
        used_by = plan["used"]

        a_bytes = FT * TOK * 4
        mod_bytes = 8 * 256 * 4
        acc_bytes = MOD_PER * 256 * 4
        arena_at = -(-nc.sbuf_base // 32) * 32
        sb("arena", [P, (2 * a_bytes + mod_bytes + acc_bytes + 64) // 4])

        def at(name, offset, shape, dt=F32):
            return nc.alloc_sbuf_tensor_at(name, shape, dt, offset=arena_at + offset)

        a_hi = at("a_hi", 0, [P, FT, TOK], F32R)
        a_lo = at("a_lo", a_bytes, [P, FT, TOK], F32R)
        mod_w = at("mod_w", 2 * a_bytes, [P, 8, 256])
        mod_acc = at("mod_acc", 2 * a_bytes + mod_bytes, [P, MOD_PER, 256])
        free1, free2 = 8 * TOK * 4, a_bytes + 8 * TOK * 4
        v1_T = at("v1_T", free1, [P, 4, TOK])
        qk1 = at("qk1", free1 + 4 * TOK * 4, [P, 2, 4, TOK])
        pT1 = at("pT1", free1 + 12 * TOK * 4, [P, 3, P])
        v1 = at("v1", free2, [P, 3, HEADS1, P])
        o1 = at("o1", 2 * a_bytes, [P, HEADS1, SEQ])
        KB = 1024
        qkv2 = {n: at(n, i * 4 * KB, [P, 4, SEQ]) for i, n in enumerate(("q_a", "k_a"))}
        v_a = at("v_a", 8 * KB, [P, 2, HEADS2, P])
        qkv2["q_b"] = at("q_b", 16 * KB, [P, 4, SEQ])
        qkv2["k_b"] = at("k_b", 20 * KB, [P, 4, SEQ])
        v_b = at("v_b", 24 * KB, [P, 2, HEADS2, P])
        v2_T = at("v2_T", 12 * KB, [P, 4, SEQ])
        qi = at("qi", 28 * KB, [P, 4, SEQ])
        gates = at("gates", 32 * KB, [P, 16, SEQ])
        work1 = at("work1", 48 * KB, [P, 4, SEQ])
        work2 = at("work2", 52 * KB, [P, 4, SEQ])
        tab = at("tab", 56 * KB, [P, 4, SEQ])
        o2_hi = at("o2_hi", 0, [P, 8, SEQ], F32R)
        o2_lo = at("o2_lo", 8 * KB, [P, 8, SEQ], F32R)
        z_hi = at("z_hi", 16 * KB, [P, 8, SEQ], F32R)
        z_lo = at("z_lo", 24 * KB, [P, 8, SEQ], F32R)

        raw = sb("raw_weights", [P, RING, UNIT])
        w_hi = sb("w_hi", [P, RING, UNIT], F32R)
        w_lo = sb("w_lo", [P, RING, UNIT], F32R)
        h = sb("h", [P, KT, TOK])
        x_hi = sb("x_hi", [P, KT, TOK], F32R)
        x_lo = sb("x_lo", [P, KT, TOK], F32R)
        f = sb("f", [P, KT, TOK])
        pair_a = sb("pair_a", [P, 2, TOK])
        pair_b = sb("pair_b", [P, 2, TOK])
        norm_at = -(-nc.sbuf_base // 32) * 32
        sb("norm_area", [P, 5 * TOK])

        def norm_part(name, offset, shape, dt=F32):
            return nc.alloc_sbuf_tensor_at(name, shape, dt, offset=norm_at + offset)

        sq = norm_part("sq", 0, [P, 2, TOK])
        sq_sum = norm_part("sq_sum", 8 * TOK, [P, TOK])
        std = norm_part("std", 12 * TOK, [P, TOK])
        rstd = norm_part("rstd", 16 * TOK, [P, TOK])
        ki = norm_part("ki", 0, [P, SEQ])
        wi_T = norm_part("wi_T", KB, [P, SEQ])
        score = norm_part("score", 2 * KB, [P, 2, SEQ])
        pT2 = norm_part("pT2", 2 * KB, [P, 4, P])
        sel = norm_part("sel", 4 * KB, [P, 2, SEQ], BF16)
        vec = sb("vec", [P, V_ALL])
        g_out = sb("g_out", [P, 49])
        mod = sb("mod", [P, 48])
        gain2 = sb("gain2", [P, 16])
        silu_c = sb("silu_c", [P, KT])
        eps = sb("eps", [P, 2])
        small = sb("small", [P, 4, 8])
        lam = sb("lam", [P, 8])
        con = sb("con", [P, C_MASK])
        mask = sb("mask", [P, TOK], BF16)
        ident_b = sb("ident_b", [P, P], BF16)
        wi = sb("wi", [P, 2, 8])
        top8 = sb("top8", [P, 8])
        ones, ident = con[:, C_ONES:C_ONES + P], con[:, C_IDENT:C_IDENT + P]
        rot1, rot2, rot_i = (con[:, c:c + P] for c in (C_ROT1, C_ROT2, C_ROTI))
        cos1, sin1 = con[:, C_COS1:C_COS1 + TOK], con[:, C_SIN1:C_SIN1 + TOK]
        ps = ctx.enter_context(nc.psum_tensor("ps", [P, 8, 512], F32))

        raw_loaded = [sem(f"raw_loaded{i}") for i in range(RING)]
        inputs_loaded, mask_loaded, tables_loaded = sem("inputs_loaded"), sem("mask_loaded"), sem("tables_loaded")
        mod_loaded, out_stored = sem("mod_loaded"), sem("out_stored")
        S = {n: sem(n) for n in (
            "hi_ready", "lo_ready", "weights_used", "tile_done", "tile_evicted",
            "x_hi_ready", "x_ready", "act_in_ready", "a_hi_ready", "a_ready", "silu_done",
            "sq_ready", "sq_used", "sumsq_ready", "stats_done", "std_ready", "h_ready", "full_ready",
            "silu_c_ready", "mod_used", "mod_psum", "mod_evicted", "setup_done", "lam_in", "lam_sums", "lam_exp",
            "turned", "v_stored", "rotated", "normed_heads", "roped", "qk_ready",
            "head_sq", "head_sums", "head_std",
            "scored", "max_ready", "probs_ready", "weights_ready", "p_turned", "pT_ready", "pv_done", "o_evicted",
            "idx_scored", "idx_relu", "idx_used", "w_turned", "wi_ready", "sel_ready", "gate_ready",
            "vec_chain")}

        class Count:

            def __init__(self):
                self.n = {}

            def up(self, name, k=1):
                self.n[name] = self.n.get(name, 0) + k
                return self.n[name]

            def now(self, name):
                return self.n.get(name, 0)

        def used_wait(eng, u):
            if u >= RING:
                name, n = used_by[u - RING]
                eng.wait_ge(S[name], n)

        ups = [("up", i) for i in range(5)]

        def end_of(st):
            return st.u0 + st.units

        block = ctx.enter_context(nc.Block())

        @block.sync
        def _(sp):
            for s in range(RING):
                sp.dma_start(raw[:, s, :], w_units[s]).then_inc(raw_loaded[s], 16)
            with sp.Fori(1, n_units // RING) as i:
                for s in range(RING):
                    sp.wait_ge(S["lo_ready"], RING * i + (s - RING + 1))
                    sp.dma_start(raw[:, s, :], w_units[RING * i + s]).then_inc(raw_loaded[s], 16)
            sp.wait_ge(out_stored, 16 * KT)

        @block.gpsimd
        def _(gp):
            gp.dma_start(h[:, :, :], x_in).then_inc(inputs_loaded, 16)
            gp.dma_start(vec[:, :], vectors).then_inc(inputs_loaded, 16)
            gp.dma_start(con[:, :], constants[:, 0:C_MASK]).then_inc(inputs_loaded, 16)
            gp.dma_start(f[:, 0, :], constants[:, C_MASK:C_ALL]).then_inc(mask_loaded, 16)
            for u in range(MOD_UNITS):
                if u:
                    gp.wait_ge(S["mod_used"], u)
                if u == 3 * MOD_PER:
                    gp.wait_ge(S["a_ready"], A0["up", 3])
                gp.dma_start(mod_w[:, :, :], mod_units[u]).then_inc(mod_loaded, 16)
            gp.wait_ge(S["mod_evicted"], MOD_PARTS)
            gp.dma_start(tab[:, :, :], tables2).then_inc(tables_loaded, 16)

        @block.tensor
        def _(pe):
            c = Count()

            def three_pass(dst, slot, col, hi, lo, start, stop):
                wh, wl = w_hi[:, slot, col:col + P], w_lo[:, slot, col:col + P]
                pe.matmul(dst, wh, hi, start=start, stop=False)
                pe.matmul(dst, wh, lo, start=False, stop=False)
                return pe.matmul(dst, wl, hi, start=False, stop=stop)

            def wait_bank(st, t, shift=0):
                n = t - (3 if st.quad else 7)
                if st.first_fresh and t < st.t0 + (4 if st.quad else 8):
                    n = st.t0
                if n > 0:
                    pe.wait_ge(S["tile_evicted"], n + shift)

            def group(st, g, xs, i=0, x_base=None, bank_busy=None):
                for half in range(2):
                    u = st.u0 + 2 * g + half + (1 if st.name == "w_in" else 0)
                    pe.wait_ge(S["lo_ready"], u + 1 + 4 * i)
                    for kk in range(4):
                        k = 4 * half + kk
                        if x_base is not None:
                            pe.wait_ge(S["x_ready"], x_base + k + 1)
                        for m in range(GROUP):
                            t = st.t0 + GROUP * g + m + (4 if st.name == "w_in" else 0)
                            if k == 0:
                                wait_bank(st, t, 8 * i)
                                if bank_busy is not None:
                                    bank_busy(m)
                            ins = three_pass(ps[:, st.bank(t), 0:st.T], u % RING, (kk * GROUP + m) * P,
                                             xs[0][:, k, 0:st.T], xs[1][:, k, 0:st.T], k == 0, k == KT - 1)
                            if k == KT - 1:
                                ins.then_inc(S["tile_done"], 1)
                    if half == 0:
                        ins.then_inc(S["weights_used"], 1)

            def k_outer(st, xs, a_base):
                for n in range(st.units):
                    u = st.u0 + n
                    pe.wait_ge(S["lo_ready"], u + 1)
                    last = n == st.units - 1
                    order = [(kk, m) for kk in range(2) for m in range(8)]
                    if last:
                        order = [(kk, m) for m in range(8) for kk in range(2)]
                    for kk, m in order:
                        k = 2 * n + kk
                        if m == 0:
                            pe.wait_ge(S["a_ready"], a_base + k + 1)
                        if k == 0:
                            wait_bank(st, st.t0 + m)
                        ins = three_pass(ps[:, st.bank(st.t0 + m), 0:st.T], u % RING, (kk * 8 + m) * P,
                                         xs[0][:, k, 0:st.T], xs[1][:, k, 0:st.T], k == 0, k == 2 * st.units - 1)
                        if k == 2 * st.units - 1:
                            ins.then_inc(S["tile_done"], 1)
                    if not last:
                        ins.then_inc(S["weights_used"], 1)

            def stats(T, bank):
                pe.wait_ge(S["sumsq_ready"], c.up("sumsq_ready"))
                pe.matmul(ps[:, bank, 0:T], ones, sq_sum[:, 0:T], start=True, stop=True).then_inc(S["stats_done"], 1)
                c.up("std_ready")

            def side_bank(st):
                return 7 if st.quad else st.bank(st.t0 + 7)

            def mod_bank(st):
                return st.bank(st.t0 + 6)

            def mod_sums(part, bank):
                pe.wait_ge(S["mod_used"], MOD_PER * (part + 1))
                for n in range(2 * MOD_PER):
                    ins = pe.matmul(ps[:, bank, 288 + n:289 + n], mod_acc[:, n // 2, (n % 2) * P:(n % 2) * P + P],
                                    ones[:, 0:1], start=True, stop=True)
                ins.then_inc(S["mod_psum"], 1)

            def wait_side(part, m=None):
                if part is not None and m in (None, 2):
                    pe.wait_ge(S["mod_evicted"], part + 1)
                if m in (None, 3):
                    pe.wait_ge(S["std_ready"], c.now("std_ready"))

            def first_groups(st, x_base, part=None):
                group(st, 0, (x_hi, x_lo), x_base=x_base)
                stats(st.T, side_bank(st))
                group(st, 1, (x_hi, x_lo), bank_busy=lambda m: wait_side(part, m))

            def gate_up(n, x_base, part=None, deferred=True):
                st = stages["up", n]
                if deferred:
                    first_groups(st, x_base, part)
                else:
                    group(st, 0, (x_hi, x_lo), x_base=x_base)
                    group(st, 1, (x_hi, x_lo), bank_busy=lambda m: wait_side(part, m))
                with pe.Fori(0, 4) as i:
                    group(st, 2, (x_hi, x_lo), i)
                    group(st, 3, (x_hi, x_lo), i)
                group(st, 10, (x_hi, x_lo))

            pe.wait_ge(S["lam_in"], 1)
            pe.matmul(ps[:, 7, 0:2], ones, lam[:, 0:2], start=True, stop=True).then_inc(S["lam_sums"], 1)
            pe.wait_ge(S["lam_exp"], 1)

            gate_up(0, 0)
            k_outer(stages["down", 0], (a_hi, a_lo), A0["up", 0])
            conv = stages["conv_in"]
            stats(TOK, side_bank(conv))
            mod_sums(0, mod_bank(conv))
            first_groups(conv, X0["conv_in"], 0)
            with pe.Fori(0, 2) as i:
                group(conv, 2, (x_hi, x_lo), i)
                group(conv, 3, (x_hi, x_lo), i)
            k_outer(stages["conv_out"], (a_hi, a_lo), A0["conv_in"])
            stats(TOK, side_bank(stages["up", 1]))
            gate_up(1, X0["up", 1])
            k_outer(stages["down", 1], (a_hi, a_lo), A0["up", 1])
            stats(TOK, side_bank(stages["up", 2]))
            mod_sums(1, mod_bank(stages["up", 2]))
            gate_up(2, X0["up", 2], 1)
            k_outer(stages["down", 2], (a_hi, a_lo), A0["up", 2])
            qkv = stages["qkv"]
            stats(TOK, 7)
            mod_sums(2, 6)

            def turn_v1(g):
                pe.wait_ge(S["tile_evicted"], qkv.t0 + GROUP * (g + 1))
                for w, at_token in enumerate((0, META, META + P)):
                    for m in range(4):
                        ins = pe.transpose(ps[:, 4 + w, m * P:(m + 1) * P], v1_T[:, m, at_token:at_token + P], ident)
                ins.then_inc(S["turned"], 1)

            def rope1(g):
                pe.wait_ge(S["tile_evicted"], qkv.t0 + GROUP * (g + 3))
                for m in range(4):
                    ins = pe.matmul(ps[:, 4 + m, 0:TOK], rot1, qk1[:, g % 2, m, :], start=True, stop=True)
                ins.then_inc(S["rotated"], 1)

            def attend1(g, j, qt):
                head = 2 * g + j
                n = META + P * (qt + 1)
                pe.wait_ge(S["qk_ready"], g + 1)
                if c.now("scored"):
                    pe.wait_ge(S["probs_ready"], 2 * c.now("scored"))
                for comp in range(2):
                    rows = slice(64 * comp, 64 * comp + 64)
                    at_q = META + P * qt
                    pe.matmul(ps[:, 4 + comp, 0:n], qk1[rows, g % 2, j, at_q:at_q + P],
                              qk1[rows, g % 2, 2 + j, 0:n], start=True, stop=False)
                    ins = pe.matmul(ps[:, 4 + comp, 0:n], ident_b[:, :], mask[:, P - P * qt:P - P * qt + n],
                                    start=False, stop=True)
                ins.then_inc(S["scored"], 1)
                c.up("scored")
                pe.wait_ge(S["weights_ready"], c.up("weights_ready"))
                if c.now("p_turned"):
                    pe.wait_ge(S["pT_ready"], c.now("p_turned"))
                windows = (0, META, META + P)[:qt + 2]
                for w, at_key in enumerate(windows):
                    ins = pe.transpose(ps[:, 6, w * P:(w + 1) * P], pair_b[:, 0, at_key:at_key + P], ident)
                ins.then_inc(S["p_turned"], 1)
                c.up("p_turned")
                pe.wait_ge(S["pT_ready"], c.now("p_turned"))
                if qt == 0 and head:
                    pe.wait_ge(S["o_evicted"], head)
                for w in range(len(windows)):
                    rows = slice(0, META if w == 0 else P)
                    ins = pe.matmul(ps[:, 7, P * qt:P * qt + P], v1[rows, w, head, :], pT1[rows, w, :],
                                    start=w == 0, stop=w == len(windows) - 1)
                if qt == 1:
                    ins.then_inc(S["pv_done"], 1)
                    c.up("pv_done")

            def subln_sums():
                pe.wait_ge(S["head_sq"], c.up("head_sq"))
                for m in range(2):
                    ins = pe.matmul(ps[:, 4 + m, :], ones, f[:, 2 * m:2 * m + 2, 0:SEQ], start=True, stop=True)
                ins.then_inc(S["head_sums"], 1)

            xs = (x_hi, x_lo)
            group(qkv, 0, xs, x_base=X0["qkv"])
            stats(TOK, 7)
            group(qkv, 1, xs)
            wait_side(2)
            turn_v1(0)
            group(qkv, 2, xs)
            pe.wait_ge(S["v_stored"], c.up("v_stored"))
            turn_v1(1)
            for g in range(4):
                if g < 3:
                    group(qkv, 3 + g, xs)
                if g == 0:
                    pe.wait_ge(S["v_stored"], c.up("v_stored"))
                else:
                    pe.wait_ge(S["o_evicted"], 2 * g)
                    if g == 2:
                        pe.wait_ge(S["head_std"], 1)
                rope1(g)
                for j in range(2):
                    for qt in range(2):
                        attend1(g, j, qt)
                if g % 2 == 1:
                    subln_sums()
            attn_out = stages["attn_out"]
            pe.wait_ge(S["head_std"], 2)
            k_outer(attn_out, (a_hi, a_lo), A0["qkv"])
            stats(SEQ, side_bank(stages["up", 3]))
            gate_up(3, X0["up", 3])
            k_outer(stages["down", 3], (a_hi, a_lo), A0["up", 3])
            w_in = stages["w_in"]
            stats(SEQ, 7)
            mod_sums(3, 6)
            stats(SEQ, 7)

            def small_group():
                u = w_in.u0
                pe.wait_ge(S["lo_ready"], u + 1)
                for k in range(KT):
                    pe.wait_ge(S["x_ready"], X0["w_in"] + k + 1)
                    for m in range(2):
                        if k == 0:
                            wait_bank(w_in, w_in.t0 + m)
                        ins = three_pass(ps[:, m, 0:SEQ], u % RING, (k * 2 + m) * P, x_hi[:, k, 0:SEQ],
                                         x_lo[:, k, 0:SEQ], k == 0, k == KT - 1)
                        if k == KT - 1:
                            ins.then_inc(S["tile_done"], 2)

            def rotate(matrix, src, tiles, bank):
                if tiles == 1:
                    ins = pe.matmul(ps[:, bank, 0:SEQ], matrix, src[:, :], start=True, stop=True)
                else:
                    for m in range(2):
                        ins = pe.matmul(ps[:, bank + m, :], matrix, src[:, 2 * m:2 * m + 2, :], start=True, stop=True)
                ins.then_inc(S["rotated"], 1)
                c.up("roped")

            def head_norm_sums():
                pe.wait_ge(S["head_sq"], c.up("head_sq"))
                for m in range(2):
                    ins = pe.matmul(ps[:, 4 + m, :], ones, work1[:, 2 * m:2 * m + 2, :], start=True, stop=True)
                ins.then_inc(S["head_sums"], 1)
                c.up("head_std")

            def idx_scores(qt, batch):
                n = P * (qt + 1)
                if c.now("idx_scored"):
                    pe.wait_ge(S["idx_relu"], c.now("idx_scored"))
                for b in range(4):
                    i = 4 * batch + b
                    rows = slice(64 * (i % 2), 64 * (i % 2) + 64)
                    ins = pe.matmul(ps[:, 4 + b, 0:n], qi[rows, i // 2, P * qt:P * qt + P], ki[rows, 0:n],
                                    start=True, stop=True)
                ins.then_inc(S["idx_scored"], 1)
                c.up("idx_scored")

            def turn_v2(g):
                pe.wait_ge(S["tile_evicted"], w_in.t0 + GROUP * (g + 2))
                for kt in range(2):
                    for m in range(4):
                        ins = pe.transpose(ps[:, 4 + kt, m * P:(m + 1) * P], v2_T[:, m, kt * P:(kt + 1) * P], ident)
                ins.then_inc(S["turned"], 1)
                c.up("v_stored")

            def attend2(which, pair, qt):
                q, k, v = (qkv2["q_a"], qkv2["k_a"], v_a) if which == 0 else (qkv2["q_b"], qkv2["k_b"], v_b)
                n = P * (qt + 1)
                bias = sel[:, qt, 0:n] if which == 0 else mask[:, META + P - P * qt:META + P - P * qt + n]
                pe.wait_ge(S["probs_ready"], 2 * c.now("scored"))
                for comp in range(2):
                    head = 2 * pair + comp
                    pe.matmul(ps[:, 4 + comp, 0:n], q[:, head, P * qt:P * qt + P], k[:, head, 0:n],
                              start=True, stop=False)
                    ins = pe.matmul(ps[:, 4 + comp, 0:n], ident_b[:, :], bias, start=False, stop=True)
                ins.then_inc(S["scored"], 1)
                c.up("scored")
                pe.wait_ge(S["weights_ready"], c.up("weights_ready"))
                pe.wait_ge(S["pT_ready"], c.now("p_turned"))
                for comp in range(2):
                    for kt in range(qt + 1):
                        col = (comp * (qt + 1) + kt) * P
                        ins = pe.transpose(ps[:, 6, col:col + P], pair_b[:, comp, kt * P:(kt + 1) * P], ident)
                ins.then_inc(S["p_turned"], 1)
                c.up("p_turned")
                pe.wait_ge(S["pT_ready"], c.now("p_turned"))
                if qt == 0:
                    pe.wait_ge(S["o_evicted"], c.now("pv_done"))
                for comp in range(2):
                    for kt in range(qt + 1):
                        ins = pe.matmul(ps[:, 7, comp * SEQ + P * qt:comp * SEQ + P * qt + P],
                                        v[:, kt, 2 * pair + comp, :], pT2[:, comp * (qt + 1) + kt, :],
                                        start=kt == 0, stop=kt == qt)
                if qt == 1:
                    ins.then_inc(S["pv_done"], 1)
                    c.up("pv_done")

            def side_free():
                for name, n in (("roped", c.now("roped")), ("head_std", 2 + c.now("head_std")),
                                ("v_stored", c.now("v_stored")), ("idx_relu", c.now("idx_scored")),
                                ("probs_ready", 2 * c.now("scored")), ("pT_ready", c.now("p_turned")),
                                ("o_evicted", c.now("pv_done"))):
                    pe.wait_ge(S[name], n)

            def qk2_job(name):
                side_free()
                head_norm_sums()
                pe.wait_ge(S["normed_heads"], c.up("normed_heads"))
                rotate(rot2, qkv2[name], 4, 6)

            small_group()
            group(w_in, 0, xs)
            pe.wait_ge(S["std_ready"], c.now("std_ready"))
            pe.wait_ge(S["mod_evicted"], 4)
            pe.wait_ge(S["tile_evicted"], w_in.t0 + GROUP)
            rotate(rot_i, ki, 1, 4)
            for qt in range(2):
                ins = pe.transpose(ps[:, 5, qt * P:(qt + 1) * P], wi_T[:, qt * P:(qt + 1) * P], ident)
            ins.then_inc(S["w_turned"], 1)
            group(w_in, 1, xs)
            pe.wait_ge(S["tile_evicted"], w_in.t0 + 2 * GROUP)
            rotate(rot_i, qi, 4, 6)
            side_free()
            pe.wait_ge(S["wi_ready"], 1)
            for qt in range(2):
                for batch in range(2):
                    idx_scores(qt, batch)
            group(w_in, 2, xs)
            qk2_job("q_a")
            group(w_in, 3, xs)
            qk2_job("k_a")
            group(w_in, 4, xs)
            side_free()
            turn_v2(3)
            group(w_in, 5, xs)
            qk2_job("q_b")
            side_free()
            pe.wait_ge(S["sel_ready"], 2)
            attend2(0, 0, 0)
            attend2(0, 0, 1)
            group(w_in, 6, xs)
            qk2_job("k_b")
            side_free()
            attend2(0, 1, 0)
            attend2(0, 1, 1)
            group(w_in, 7, xs)
            side_free()
            turn_v2(6)
            group(w_in, 8, xs)
            side_free()
            attend2(1, 0, 0)
            attend2(1, 0, 1)
            group(w_in, 9, xs)
            attend2(1, 1, 0)
            attend2(1, 1, 1)
            group(w_in, 10, xs)
            side_free()
            k_outer(stages["br_dsa"], (o2_hi, o2_lo), A0["w_in"])
            k_outer(stages["br_moba"], (o2_hi[:, 4:8, :], o2_lo[:, 4:8, :]), A0["w_in"] + 4)
            k_outer(stages["w_out"], (z_hi, z_lo), A0["br"])
            stats(SEQ, side_bank(stages["up", 4]))
            gate_up(4, X0["up", 4], deferred=False)
            k_outer(stages["down", 4], (a_hi, a_lo), A0["up", 4])

        @block.vector
        def _(dve):
            c = Count()
            nxt = [0]

            def chain(ins):
                ins.then_inc(S["vec_chain"], 1)
                dve.wait_ge(S["vec_chain"], c.up("vec_chain"))

            def low_part(u, i=0):
                dve.wait_ge(S["hi_ready"], u + 1 + 4 * i)
                dve.tensor_tensor(w_lo[:, u % RING, :], raw[:, u % RING, :], w_hi[:, u % RING, :].bitcast(F32),
                                  ALU.subtract).then_inc(S["lo_ready"], 1)

            def split_to(u_end):
                while nxt[0] < min(u_end, n_units):
                    low_part(nxt[0])
                    nxt[0] += 1

            def bcast(row, T, n=2):
                return row[:, 0:T].unsqueeze(1).broadcast_to([P, n, T])

            def gated_eviction(n, g, i=0):
                st = stages["up", n]
                T, t, e = st.T, st.t0 + GROUP * g, E0["up", n] + g
                b = t % 8
                gate, up = pair_a[:, :, 0:T], pair_b[:, :, 0:T]
                if A0["up", n] + g > 0:
                    dve.wait_ge(S["a_ready"], A0["up", n] + 2 * g + 4 * i)
                dve.wait_ge(S["tile_done"], t + 2 + 8 * i)
                if n < 4:
                    dve.tensor_tensor(gate, ps[:, b:b + 2, 0:T], bcast(rstd, T), ALU.mult).then_inc(S["tile_evicted"], 2)
                else:
                    dve.tensor_copy(gate, ps[:, b:b + 2, 0:T]).then_inc(S["tile_evicted"], 2)
                dve.wait_ge(S["tile_done"], t + 4 + 8 * i)
                if n < 4:
                    dve.tensor_tensor(up, ps[:, b + 2:b + 4, 0:T], bcast(rstd, T), ALU.mult).then_inc(S["tile_evicted"], 2)
                else:
                    dve.tensor_copy(up, ps[:, b + 2:b + 4, 0:T]).then_inc(S["tile_evicted"], 2)
                dve.wait_ge(S["tile_evicted"], t + 4 + 8 * i)
                dve.wait_ge(S["silu_done"], S0["up", n] + g + 1 + 2 * i)
                dve.tensor_tensor(up, gate, up, ALU.mult).then_inc(S["act_in_ready"], 1)
                dve.wait_ge(S["a_hi_ready"], e + 1 + 2 * i)
                k = bass.ds(2 * g + 4 * i, 2)
                dve.tensor_tensor(a_lo[:, k, 0:T], up, a_hi[:, k, 0:T].bitcast(F32), ALU.subtract).then_inc(S["a_ready"], 2)

            def gate_up(n):
                st = stages["up", n]
                for g in range(2):
                    split_to(st.u0 + 2 * g + 5)
                    gated_eviction(n, g)
                split_to(st.u0 + 9)
                with dve.Fori(0, 4) as i:
                    u = st.u0 + 9
                    gated_eviction(n, 2, i)
                    low_part(u, i)
                    low_part(u + 1, i)
                    gated_eviction(n, 3, i)
                    low_part(u + 2, i)
                    low_part(u + 3, i)
                nxt[0] = st.u0 + 25
                gated_eviction(n, 10)

            def mod_part(part):
                for n in range(MOD_PER):
                    dve.wait_ge(mod_loaded, 16 * (MOD_PER * part + n + 1))
                    if part == 0 and n == 0:
                        dve.wait_ge(S["silu_c_ready"], 1)
                    elif n == 0:
                        dve.wait_ge(S["mod_psum"], part)
                    acc = mod_acc[:, n, :]
                    chain(dve.tensor_scalar(acc, mod_w[:, 0, :], silu_c[:, 0:1], None, ALU.mult))
                    for j in range(1, 8):
                        ins = dve.scalar_tensor_tensor(acc, mod_w[:, j, :], silu_c[:, j:j + 1], acc, ALU.mult, ALU.add)
                        if j < 7:
                            chain(ins)
                    ins.then_inc(S["mod_used"], 1)
                    yield

            def mod_evict(part, bank):
                cols = slice(2 * MOD_PER * part, 2 * MOD_PER * (part + 1))
                dve.wait_ge(S["mod_psum"], part + 1)
                dve.tensor_tensor(mod[:, cols], ps[:, bank, 288:288 + 2 * MOD_PER],
                                  vec[:, V_BMOD + 2 * MOD_PER * part:V_BMOD + 2 * MOD_PER * (part + 1)],
                                  ALU.add).then_inc(S["mod_evicted"], 1)

            def down(n, part=None):
                st = stages["down", n]
                work = mod_part(part) if part is not None else iter(())
                for u in range(nxt[0], end_of(st)):
                    split_to(u + 1)
                    next(work, None)
                for _ in work:
                    pass

            def add_square(m, T):
                if m == 0:
                    return
                dve.wait_ge(S["sq_ready"], c.now("sq_ready") + m + 1)
                first = sq[:, 0, 0:T] if m == 1 else sq_sum[:, 0:T]
                if m > 1:
                    dve.wait_ge(S["sq_used"], c.now("sq_used") + m - 1)
                dve.tensor_tensor(sq_sum[:, 0:T], first, sq[:, m % 2, 0:T], ALU.add)\
                   .then_inc(S["sq_used" if m < 7 else "sumsq_ready"], 1)

            def squares_done():
                c.up("sq_ready", 8)
                c.up("sq_used", 6)

            def root(T):
                dve.wait_ge(S["std_ready"], c.up("std_ready"))
                chain(dve.reciprocal(rstd[:, 0:T], std[:, 0:T]))

            def tail(st, gain, nx, next_gain, shift=None, normed=True, part=None, bank=None):
                T = st.T
                off = TOK - T
                if nx is not None:
                    split_to(nx.u0 + 3)
                t0 = st.t0 if st is not None else 0
                for m in range(8):
                    dve.wait_ge(S["tile_done"], t0 + m + 1)
                    dve.tensor_copy(f[:, m, 0:T], ps[:, st.bank(t0 + m), 0:T]).then_inc(S["tile_evicted"], 1)
                    if normed and m >= 1:
                        add_square(m - 1, T)
                if normed:
                    add_square(7, T)
                    squares_done()
                    root(T)
                if part == MOD_PARTS - 1:
                    mod_evict(part, bank)
                    dve.wait_ge(S["mod_evicted"], MOD_PARTS)
                    for w in range(2):
                        chain(dve.tensor_scalar(gain2[:, 8 * w:8 * w + 8], mod[:, 8 + 24 * w:16 + 24 * w], 1.0, None, ALU.add))
                        chain(dve.tensor_tensor(gain2[:, 8 * w:8 * w + 8], gain2[:, 8 * w:8 * w + 8],
                                                vec[:, V_GMIX + 8 * w:V_GMIX + 8 * w + 8], ALU.mult))
                if not normed:
                    dve.wait_ge(S["tile_evicted"], t0 + 8)
                update_and_prepare(T, off, gain, next_gain, shift, normed, nx)
                if nx is not None and shift is None and part is not None:
                    mod_evict(part, bank)

            def update_and_prepare(T, off, gain, next_gain, shift, normed, nx, update=True):
                n_h = c.now("h_ready")
                n_v = c.now("vec_chain")
                deferred = shift is None
                for m in range(8 + 2):
                    if update and m < 8:
                        if normed:
                            if m >= 2:
                                dve.wait_ge(S["h_ready"], n_h + m - 1)
                            dve.tensor_tensor(pair_a[:, m % 2, 0:T], f[:, m, 0:T], rstd[:, 0:T], ALU.mult)\
                               .then_inc(S["vec_chain"], 1)
                            c.up("vec_chain")
                    k = m - 1
                    if update and 0 <= k < 8:
                        src = f[:, k, 0:T]
                        if normed:
                            src = pair_a[:, k % 2, 0:T]
                            dve.wait_ge(S["vec_chain"], n_v + k + 1)
                        dve.scalar_tensor_tensor(h[:, k, off:off + T], src, gain[:, k:k + 1], h[:, k, off:off + T],
                                                 ALU.mult, ALU.add).then_inc(S["h_ready"], 1)
                    k = m - 2
                    if k >= 0 and nx is not None:
                        if deferred:
                            dve.wait_ge(S["x_hi_ready"], c.up("x_hi_ready"))
                            dve.scalar_tensor_tensor(x_lo[:, k, 0:T], h[:, k, off:off + T], next_gain[:, k:k + 1],
                                                     x_hi[:, k, 0:T].bitcast(F32), ALU.mult, ALU.subtract)\
                               .then_inc(S["x_ready"], 1)
                        add_square(k, T)
                if update:
                    c.up("h_ready", 8)
                if nx is None:
                    return
                squares_done()
                if deferred:
                    return
                root(T)
                for m in range(8 + 2):
                    if m < 8:
                        dve.tensor_tensor(f[:, m, 0:T], h[:, m, off:off + T], rstd[:, 0:T], ALU.mult)\
                           .then_inc(S["vec_chain"], 1)
                        c.up("vec_chain")
                    k = m - 1
                    if 0 <= k < 8:
                        dve.wait_ge(S["vec_chain"], c.now("vec_chain") - (1 if m < 8 else 0))
                        dve.tensor_scalar(f[:, k, 0:T], f[:, k, 0:T], next_gain[:, k:k + 1], shift[:, k:k + 1],
                                          ALU.mult, ALU.add).then_inc(S["full_ready"], 1)
                    k = m - 2
                    if k >= 0:
                        dve.wait_ge(S["x_hi_ready"], c.up("x_hi_ready"))
                        dve.tensor_tensor(x_lo[:, k, 0:T], f[:, k, 0:T], x_hi[:, k, 0:T].bitcast(F32),
                                          ALU.subtract).then_inc(S["x_ready"], 1)

            def before_evictions(nx, deferred=True):
                split_to(nx.u0 + 5)
                if deferred:
                    root(nx.T)

            def ln(layer, which):
                at_col = V_LN + 8 * (6 * layer + which)
                return vec[:, at_col:at_col + 8]

            dve.memset(eps[:, 0:1], EPS)
            dve.memset(eps[:, 1:2], SUBLN_EPS)
            dve.wait_ge(inputs_loaded, 48)
            for n in range(4):
                dve.tensor_scalar(g_out[:, 8 * n:8 * n + 8], ln(n // 2, 1 + 4 * (n % 2)), 0.5, None, ALU.mult)
            dve.tensor_scalar(g_out[:, 48:49], vec[:, V_SUB:V_SUB + 1], 1.0 - LAMBDA_INIT, None, ALU.mult)
            chain(dve.tensor_tensor(lam[:, 0:2], vec[:, V_LAM:V_LAM + 4:2], vec[:, V_LAM + 1:V_LAM + 4:2], ALU.mult))
            dve.wait_ge(mask_loaded, 16)
            dve.tensor_copy(ident_b[:, :], ident)
            dve.tensor_copy(mask[:, :], f[:, 0, :]).then_inc(S["lam_in"], 1)
            dve.wait_ge(S["lam_in"], 1)
            dve.wait_ge(S["lam_exp"], 1)
            chain(dve.tensor_tensor(lam[:, 4:5], lam[:, 2:3], lam[:, 3:4], ALU.subtract))
            chain(dve.tensor_scalar(lam[:, 5:6], lam[:, 4:5], LAMBDA_INIT, None, ALU.add))

            split_to(3)
            update_and_prepare(TOK, 0, None, ln(0, 0), None, False, stages["up", 0], update=False)
            before_evictions(stages["up", 0])
            gate_up(0)
            down(0, 0)
            conv = stages["conv_in"]
            conv_bank = conv.bank(conv.t0 + 6)
            tail(stages["down", 0], g_out[:, 0:8], conv, ln(0, 2), part=0, bank=conv_bank)
            before_evictions(conv)
            for g in range(6):
                split_to(conv.u0 + 2 * g + 5)
                t = conv.t0 + GROUP * g
                b = t % 8
                if g < 4:
                    for q, dst in enumerate((pair_a, pair_b)):
                        dve.wait_ge(S["tile_done"], t + 2 + 2 * q)
                        dve.tensor_tensor(dst[:, :, :], ps[:, b + 2 * q:b + 2 * q + 2, 0:TOK], bcast(rstd, TOK),
                                          ALU.mult).then_inc(S["tile_evicted"], 2)
                    dve.wait_ge(S["tile_evicted"], t + 4)
                    chain(dve.tensor_tensor(pair_a[:, :, :], pair_a[:, :, :], pair_b[:, :, :], ALU.mult))
                    taps = [V_CONV + 8 * j + 2 * g for j in range(3)]
                    for back in range(3):
                        for m in range(2):
                            y, w = f[:, 2 * g + m, back:TOK], vec[:, taps[2 - back] + m:taps[2 - back] + m + 1]
                            if back == 0:
                                ins = dve.tensor_scalar(y, pair_a[:, m, :], w, None, ALU.mult)
                            else:
                                ins = dve.scalar_tensor_tensor(y, pair_a[:, m, 0:TOK - back], w, y, ALU.mult, ALU.add)
                            if m == 0:
                                ins.then_inc(S["vec_chain"], 1)
                                c.up("vec_chain")
                            else:
                                chain(ins)
                else:
                    for q, dst in enumerate((pair_a, pair_b)):
                        k = 4 * (g - 4) + 2 * q
                        e = E0["conv_in"] + 2 * (g - 4) + q
                        dve.wait_ge(S["tile_done"], t + 2 + 2 * q)
                        if g == 5:
                            dve.wait_ge(S["a_ready"], A0["conv_in"] + 2 * q + 2)
                        dve.tensor_tensor(dst[:, :, :], ps[:, b + 2 * q:b + 2 * q + 2, 0:TOK], bcast(rstd, TOK),
                                          ALU.mult).then_inc(S["tile_evicted"], 2)
                        dve.wait_ge(S["tile_evicted"], t + 2 + 2 * q)
                        dve.tensor_tensor(dst[:, :, :], dst[:, :, :], f[:, k:k + 2, :], ALU.mult)\
                           .then_inc(S["act_in_ready"], 1)
                    for q, src in enumerate((pair_a, pair_b)):
                        k = 4 * (g - 4) + 2 * q
                        dve.wait_ge(S["a_hi_ready"], E0["conv_in"] + 2 * (g - 4) + q + 1)
                        dve.tensor_tensor(a_lo[:, k:k + 2, :], src[:, :, :], a_hi[:, k:k + 2, :].bitcast(F32),
                                          ALU.subtract).then_inc(S["a_ready"], 2)
            tail(stages["conv_out"], ln(0, 3), stages["up", 1], ln(0, 4))
            before_evictions(stages["up", 1])
            gate_up(1)
            down(1, 1)
            up2 = stages["up", 2]
            tail(stages["down", 1], g_out[:, 8:16], up2, ln(1, 0), part=1, bank=up2.bank(up2.t0 + 6))

            before_evictions(up2)
            gate_up(2)
            down(2, 2)
            qkv = stages["qkv"]
            tail(stages["down", 2], g_out[:, 16:24], qkv, ln(1, 2), part=2, bank=6)
            before_evictions(qkv)

            def evict4(st, g, dst, T, scaled):
                t = st.t0 + GROUP * g + (4 if st.name == "w_in" else 0)
                dve.wait_ge(S["tile_done"], t + 4)
                if scaled:
                    ins = dve.tensor_tensor(dst, ps[:, 0:4, 0:T], bcast(rstd, T, 4), ALU.mult)
                else:
                    ins = dve.tensor_copy(dst, ps[:, 0:4, 0:T])
                ins.then_inc(S["tile_evicted"], 4)
                dve.wait_ge(S["tile_evicted"], t + 4)

            def soften(n, scale):
                s = c.now("scored")
                c.up("scored")
                col = small[:, s % 4, :]
                dve.wait_ge(S["scored"], s + 1)
                chain(dve.tensor_reduce(col[:, 0:2], ps[:, 4:6, 0:n], AX.X, ALU.max))
                dve.tensor_scalar(col[:, 2:4], col[:, 0:2], -scale, None, ALU.mult).then_inc(S["max_ready"], 1)
                dve.wait_ge(S["probs_ready"], 2 * s + 2)
                chain(dve.reciprocal(col[:, 6:8], col[:, 4:6]))
                return col

            def attend1(g, j, qt):
                n = META + P * (qt + 1)
                col = soften(n, 64 ** -0.5)
                chain(dve.tensor_scalar(col[:, 7:8], col[:, 7:8], lam[:, 5:6], None, ALU.mult))
                chain(dve.tensor_scalar(pair_a[:, 1, 0:n], pair_a[:, 1, 0:n], col[:, 7:8], None, ALU.mult))
                if c.now("p_turned"):
                    dve.wait_ge(S["p_turned"], c.now("p_turned"))
                dve.scalar_tensor_tensor(pair_b[:, 0, 0:n], pair_a[:, 0, 0:n], col[:, 6:7], pair_a[:, 1, 0:n],
                                         ALU.mult, ALU.subtract).then_inc(S["weights_ready"], 1)
                c.up("p_turned")
                if qt == 1:
                    dve.wait_ge(S["pv_done"], c.up("pv_done"))
                    dve.tensor_copy(o1[:, 2 * g + j, :], ps[:, 7, 0:SEQ]).then_inc(S["o_evicted"], 1)

            def rope1(g):
                x = qk1[:, g % 2, :, :]
                dve.wait_ge(S["rotated"], c.up("rotated"))
                if g:
                    dve.wait_ge(S["qk_ready"], g)
                dve.tensor_tensor(f[:, 0:4, :], ps[:, 4:8, 0:TOK], bcast(sin1, TOK, 4), ALU.mult)
                chain(dve.tensor_tensor(x, x, bcast(cos1, TOK, 4), ALU.mult))
                dve.tensor_tensor(x, x, f[:, 0:4, :], ALU.add).then_inc(S["qk_ready"], 1)

            def subln(half):
                e = E0["qkv"] + half
                heads = slice(4 * half, 4 * half + 4)
                dve.wait_ge(S["head_std"], half + 1)
                chain(dve.reciprocal(f[:, 4:8, 0:SEQ], f[:, 4:8, 0:SEQ]))
                dve.scalar_tensor_tensor(o1[:, heads, :], o1[:, heads, :], g_out[:, 48:49], f[:, 4:8, 0:SEQ],
                                         ALU.mult, ALU.mult).then_inc(S["act_in_ready"], 1)
                dve.wait_ge(S["a_hi_ready"], e + 1)
                dve.tensor_tensor(a_lo[:, heads, 0:SEQ], o1[:, heads, :], a_hi[:, heads, 0:SEQ].bitcast(F32),
                                  ALU.subtract).then_inc(S["a_ready"], 4)

            split_to(qkv.u0 + 5)
            evict4(qkv, 0, v1_T[:, :, :], TOK, True)
            for g in range(1, 6):
                split_to(qkv.u0 + 2 * g + 5)
                if g == 1:
                    dve.wait_ge(S["turned"], 1)
                    evict4(qkv, 1, v1_T[:, :, :], TOK, True)
                else:
                    evict4(qkv, g, qk1[:, g % 2, :, :], TOK, True)
                split_to(qkv.u0 + 2 * g + 6)
                if g >= 3:
                    rope1(g - 3)
                    for j in range(2):
                        for qt in range(2):
                            attend1(g - 3, j, qt)
                    if g == 4:
                        subln(0)
            rope1(3)
            for j in range(2):
                for qt in range(2):
                    attend1(3, j, qt)
            subln(1)
            tail(stages["attn_out"], ln(1, 3), stages["up", 3], ln(1, 4))
            before_evictions(stages["up", 3])
            gate_up(3)
            down(3, 3)
            w_in = stages["w_in"]
            tail(stages["down", 3], g_out[:, 24:32], w_in, gain2[:, 0:8], shift=mod[:, 0:8], part=3, bank=6)

            def rope2(x, which, tiles, bank):
                cos, sin = tab[:, 2 * which, :], tab[:, 2 * which + 1, :]
                dve.wait_ge(S["rotated"], c.up("rotated"))
                if c.now("roped"):
                    dve.wait_ge(S["roped"], c.now("roped"))
                c.up("roped")
                if tiles == 1:
                    dve.tensor_tensor(work1[:, 0, :], ps[:, bank, 0:SEQ], sin, ALU.mult)
                    chain(dve.tensor_tensor(x, x, cos, ALU.mult))
                    ins = dve.tensor_tensor(x, x, work1[:, 0, :], ALU.add)
                else:
                    for m in range(2):
                        dve.tensor_tensor(work1[:, 2 * m:2 * m + 2, :], ps[:, bank + m, :].rearrange("p (a n) -> p a n", a=2),
                                          bcast(sin, SEQ, 2), ALU.mult)
                    chain(dve.tensor_tensor(x, x, bcast(cos, SEQ, 4), ALU.mult))
                    ins = dve.tensor_tensor(x, x, work1[:, :, :], ALU.add)
                ins.then_inc(S["roped"], 1)

            def qk2_job(n, name):
                x = qkv2[name][:, :, :]
                dve.wait_ge(S["head_std"], 2 + n + 1)
                chain(dve.reciprocal(work2[:, :, :], work2[:, :, :]))
                dve.scalar_tensor_tensor(x, x, vec[:, V_GQK + n:V_GQK + n + 1], work2[:, :, :], ALU.mult, ALU.mult)\
                   .then_inc(S["normed_heads"], 1)
                rope2(x, 0, 4, 6)

            def idx_scores(qt, batch):
                n = P * (qt + 1)
                e = c.up("idx_relu")
                dve.wait_ge(S["idx_relu"], e)
                src = (work1, work2)[(e - 1) % 2]
                for b in range(4):
                    i = 4 * batch + b
                    before = mask[:, META + P - P * qt:META + P - P * qt + n] if i == 0 else score[:, qt, 0:n]
                    ins = dve.scalar_tensor_tensor(score[:, qt, 0:n], src[:, b, 0:n], wi[:, qt, i:i + 1], before,
                                                   ALU.mult, ALU.add)
                    if b < 3:
                        chain(ins)
                ins.then_inc(S["idx_used"], 1)
                dve.wait_ge(S["idx_used"], e)

            def select(qt):
                n = P * (qt + 1)
                x = score[:, qt, 0:n]
                for _ in range(TOPK // 8):
                    chain(dve.max(top8[:, :], x))
                    chain(dve.match_replace(x, top8[:, :], x, TAKEN))
                chain(dve.tensor_scalar(x, x, TAKEN / 2, NEG, ALU.is_gt, ALU.mult))
                dve.tensor_tensor(sel[:, qt, 0:n], x, mask[:, META + P - P * qt:META + P - P * qt + n],
                                  ALU.add).then_inc(S["sel_ready"], 1)

            def attend2(which, pair, qt):
                n = P * (qt + 1)
                col = soften(n, P ** -0.5)
                dve.wait_ge(S["p_turned"], c.now("p_turned"))
                for comp in range(2):
                    ins = dve.tensor_scalar(pair_b[:, comp, 0:n], pair_a[:, comp, 0:n], col[:, 6 + comp:7 + comp],
                                            None, ALU.mult)
                ins.then_inc(S["weights_ready"], 1)
                c.up("p_turned")
                if qt == 1:
                    dve.wait_ge(S["pv_done"], c.up("pv_done"))
                    head = 4 * which + 2 * pair
                    dve.tensor_copy(f[:, head:head + 2, 0:SEQ], ps[:, 7, :].rearrange("p (a n) -> p a n", a=2))\
                       .then_inc(S["o_evicted"], 1)

            u0 = w_in.u0
            split_to(u0 + 5)
            dve.wait_ge(S["tile_done"], w_in.t0 + 4)
            dve.tensor_copy(ki[:, :], ps[:, 0, 0:SEQ])
            dve.tensor_copy(wi_T[:, :], ps[:, 1, 0:SEQ]).then_inc(S["tile_evicted"], 4)
            dve.wait_ge(S["tile_evicted"], w_in.t0 + 4)
            dests = [qi, qkv2["q_a"], qkv2["k_a"], v2_T, qkv2["q_b"], qkv2["k_b"], v2_T]
            dve.wait_ge(tables_loaded, 16)
            for g in range(11):
                split_to(u0 + 2 * g + 6)
                if g < 7:
                    if g == 6:
                        dve.wait_ge(S["turned"], 3)
                    evict4(w_in, g, dests[g][:, :, :], SEQ, False)
                else:
                    k = 4 * (g - 7)
                    evict4(w_in, g, gates[:, k:k + 4, :], SEQ, False)
                split_to(u0 + 2 * g + 7)
                if g == 0:
                    rope2(ki[:, :], 1, 1, 4)
                    dve.wait_ge(S["w_turned"], 1)
                    for qt in range(2):
                        ins = dve.tensor_scalar(wi[:, qt, :], ps[:, 5, qt * P:qt * P + 8], IDX_SCALE, None, ALU.mult)
                    ins.then_inc(S["wi_ready"], 1)
                    dve.wait_ge(S["wi_ready"], 1)
                elif g == 1:
                    rope2(qi[:, :, :], 1, 4, 6)
                    for qt in range(2):
                        for batch in range(2):
                            idx_scores(qt, batch)
                elif g == 2:
                    qk2_job(0, "q_a")
                    select(0)
                elif g == 3:
                    qk2_job(1, "k_a")
                    select(1)
                elif g == 5:
                    qk2_job(2, "q_b")
                    attend2(0, 0, 0)
                    attend2(0, 0, 1)
                elif g == 6:
                    qk2_job(3, "k_b")
                    attend2(0, 1, 0)
                    attend2(0, 1, 1)
                elif g in (8, 9):
                    attend2(1, g - 8, 0)
                    attend2(1, g - 8, 1)
            for which in range(2):
                heads = slice(4 * which, 4 * which + 4)
                dve.wait_ge(S["a_hi_ready"], E0["w_in"] + which + 1)
                dve.tensor_tensor(o2_lo[:, heads, :], f[:, heads, 0:SEQ], o2_hi[:, heads, :].bitcast(F32),
                                  ALU.subtract).then_inc(S["a_ready"], 4)
            dsa, moba, w_out = stages["br_dsa"], stages["br_moba"], stages["w_out"]
            split_to(end_of(dsa) + 3)
            dve.wait_ge(S["gate_ready"], 4)
            for m in range(0, 8, 2):
                t = dsa.t0 + m
                dve.wait_ge(S["tile_done"], t + 2)
                dve.tensor_tensor(gates[:, m:m + 2, :], ps[:, t % 8:t % 8 + 2, 0:SEQ], gates[:, m:m + 2, :],
                                  ALU.mult).then_inc(S["tile_evicted"], 2)
            split_to(end_of(moba) + 3)
            for m in range(0, 8, 2):
                t, e = moba.t0 + m, E0["br"] + m // 2
                x = (pair_a, pair_b)[m // 2 % 2][:, :, 0:SEQ]
                dve.wait_ge(S["tile_done"], t + 2)
                if m >= 4:
                    dve.wait_ge(S["a_ready"], A0["br"] + m - 2)
                dve.tensor_tensor(x, ps[:, t % 8:t % 8 + 2, 0:SEQ], gates[:, 8 + m:10 + m, :],
                                  ALU.mult).then_inc(S["tile_evicted"], 2)
                dve.wait_ge(S["tile_evicted"], t + 2)
                dve.tensor_tensor(x, x, gates[:, m:m + 2, :], ALU.add).then_inc(S["act_in_ready"], 1)
                dve.wait_ge(S["a_hi_ready"], e + 1)
                dve.tensor_tensor(z_lo[:, m:m + 2, :], x, z_hi[:, m:m + 2, :].bitcast(F32), ALU.subtract)\
                   .then_inc(S["a_ready"], 2)
            tail(w_out, mod[:, 16:24], stages["up", 4], gain2[:, 8:16], shift=mod[:, 24:32], normed=False)
            before_evictions(stages["up", 4], deferred=False)
            gate_up(4)
            down(4)
            last = stages["down", 4]
            for m in range(8):
                dve.wait_ge(S["tile_done"], last.t0 + m + 1)
                dve.scalar_tensor_tensor(h[:, m, META:TOK], ps[:, last.bank(last.t0 + m), 0:SEQ], mod[:, 40 + m:41 + m],
                                         h[:, m, META:TOK], ALU.mult, ALU.add).then_inc(S["h_ready"], 1)

        @block.scalar
        def _(act):
            c = Count()
            nxt = [0]

            def high_part(u, i=0):
                act.wait_ge(raw_loaded[u % RING], 16 * (u // RING + 1) + 16 * i)
                if u >= RING:
                    name, n = used_by[u - RING]
                    act.wait_ge(S[name], n + (8 if name == "tile_done" else 2) * i)
                act.activation(w_hi[:, u % RING, :], raw[:, u % RING, :], ACT.Copy).then_inc(S["hi_ready"], 1)

            def split_to(u_end):
                while nxt[0] < min(u_end, n_units):
                    high_part(nxt[0])
                    nxt[0] += 1

            def gated(n, g, i=0):
                st = stages["up", n]
                T, t = st.T, st.t0 + GROUP * g
                act.wait_ge(S["tile_evicted"], t + 2 + 8 * i)
                act.activation(pair_a[:, :, 0:T], pair_a[:, :, 0:T], ACT.Silu).then_inc(S["silu_done"], 1)
                act.wait_ge(S["act_in_ready"], I0["up", n] + g + 1 + 2 * i)
                act.activation(a_hi[:, bass.ds(2 * g + 4 * i, 2), 0:T], pair_b[:, :, 0:T], ACT.Copy)\
                   .then_inc(S["a_hi_ready"], 1)

            def gate_up(n):
                st = stages["up", n]
                for g in range(2):
                    split_to(st.u0 + 2 * g + 5)
                    gated(n, g)
                split_to(st.u0 + 9)
                with act.Fori(0, 4) as i:
                    u = st.u0 + 9
                    gated(n, 2, i)
                    high_part(u, i)
                    high_part(u + 1, i)
                    gated(n, 3, i)
                    high_part(u + 2, i)
                    high_part(u + 3, i)
                nxt[0] = st.u0 + 25
                gated(n, 10)

            def square(m, src, T):
                if m >= 2:
                    act.wait_ge(S["sq_used"], c.now("sq_used") + max(1, m - 2))
                act.activation(sq[:, m % 2, 0:T], src, ACT.Square).then_inc(S["sq_ready"], 1)

            def root(T, bank):
                act.wait_ge(S["stats_done"], c.up("stats_done"))
                act.activation(std[:, 0:T], ps[:, bank, 0:T], ACT.Sqrt, bias=eps[:, 0:1], scale=1.0 / D)\
                   .then_inc(S["std_ready"], 1)

            def tail(st, nx, next_gain, full=False, normed=True, bank=None):
                T = st.T
                off = TOK - T
                split_to(nx.u0 + 3)
                if normed:
                    for m in range(8):
                        act.wait_ge(S["tile_evicted"], st.t0 + m + 1)
                        square(m, f[:, m, 0:T], T)
                    c.up("sq_used", 6)
                    root(T, bank)
                prepare(T, off, next_gain, full, bank)

            def prepare(T, off, next_gain, full, bank, update=True):
                for m in range(8):
                    if update:
                        act.wait_ge(S["h_ready"], c.up("h_ready"))
                    if not full:
                        act.activation(x_hi[:, m, 0:T], h[:, m, off:off + T], ACT.Identity,
                                       scale=next_gain[:, m:m + 1]).then_inc(S["x_hi_ready"], 1)
                    square(m, h[:, m, off:off + T], T)
                c.up("sq_used", 6)
                if full:
                    root(T, bank)
                    for m in range(8):
                        act.wait_ge(S["full_ready"], c.up("full_ready"))
                        act.activation(x_hi[:, m, 0:T], f[:, m, 0:T], ACT.Copy).then_inc(S["x_hi_ready"], 1)

            def before_evictions(nx, bank):
                split_to(nx.u0 + 5)
                root(nx.T, bank)

            def ln(layer, which):
                at_col = V_LN + 8 * (6 * layer + which)
                return vec[:, at_col:at_col + 8]

            def side_bank(st):
                return 7 if st.quad else st.bank(st.t0 + 7)

            act.wait_ge(inputs_loaded, 48)
            act.activation(silu_c[:, :], vec[:, V_C:V_C + 8], ACT.Silu).then_inc(S["silu_c_ready"], 1)
            act.wait_ge(S["lam_sums"], 1)
            act.activation(lam[:, 2:4], ps[:, 7, 0:2], ACT.Exp).then_inc(S["lam_exp"], 1)

            split_to(3)
            prepare(TOK, 0, ln(0, 0), False, None, update=False)
            before_evictions(stages["up", 0], side_bank(stages["up", 0]))
            gate_up(0)
            conv = stages["conv_in"]
            tail(stages["down", 0], conv, ln(0, 2), bank=side_bank(conv))
            before_evictions(conv, side_bank(conv))
            for g in range(6):
                split_to(conv.u0 + 2 * g + 5)
                if g >= 4:
                    for q, src in enumerate((pair_a, pair_b)):
                        k = 4 * (g - 4) + 2 * q
                        act.wait_ge(S["act_in_ready"], I0["conv_in"] + 2 * (g - 4) + q + 1)
                        act.activation(a_hi[:, k:k + 2, :], src[:, :, :], ACT.Copy).then_inc(S["a_hi_ready"], 1)
            up1, up2, qkv, up3, w_in = (stages["up", 1], stages["up", 2], stages["qkv"], stages["up", 3], stages["w_in"])
            tail(stages["conv_out"], up1, ln(0, 4), bank=side_bank(up1))
            before_evictions(up1, side_bank(up1))
            gate_up(1)
            tail(stages["down", 1], up2, ln(1, 0), bank=side_bank(up2))

            before_evictions(up2, side_bank(up2))
            gate_up(2)
            tail(stages["down", 2], qkv, ln(1, 2), bank=7)
            before_evictions(qkv, 7)

            def soften(n, scale):
                s = c.now("scored")
                c.up("scored")
                col = small[:, s % 4, :]
                act.wait_ge(S["max_ready"], s + 1)
                if s:
                    act.wait_ge(S["weights_ready"], s)
                for comp in range(2):
                    act.activation(pair_a[:, comp, 0:n], ps[:, 4 + comp, 0:n], ACT.Exp, bias=col[:, 2 + comp:3 + comp],
                                   scale=scale, accum_out=col[:, 4 + comp:5 + comp]).then_inc(S["probs_ready"], 1)

            def attend1(qt):
                soften(META + P * (qt + 1), 64 ** -0.5)
                act.wait_ge(S["p_turned"], c.up("p_turned"))
                w = qt + 2
                act.activation(pT1[:, 0:w, :], ps[:, 6, 0:w * P].rearrange("p (w n) -> p w n", w=w), ACT.Copy)\
                   .then_inc(S["pT_ready"], 1)

            def subln(half):
                heads = slice(4 * half, 4 * half + 4)
                act.wait_ge(S["o_evicted"], 4 * half + 4)
                act.activation(f[:, 0:4, 0:SEQ], o1[:, heads, :], ACT.Square).then_inc(S["head_sq"], 1)
                act.wait_ge(S["head_sums"], half + 1)
                act.activation(f[:, 4:8, 0:SEQ], ps[:, 4:6, :].rearrange("p b (a n) -> p (b a) n", a=2), ACT.Sqrt,
                               bias=eps[:, 1:2], scale=1.0 / P).then_inc(S["head_std"], 1)
                act.wait_ge(S["act_in_ready"], I0["qkv"] + half + 1)
                act.activation(a_hi[:, heads, 0:SEQ], o1[:, heads, :], ACT.Copy).then_inc(S["a_hi_ready"], 1)

            def store_v1(g):
                act.wait_ge(S["turned"], g + 1)
                act.activation(v1[:, :, 4 * g:4 * g + 4, :], ps[:, 4:7, :].rearrange("p w (a n) -> p w a n", a=4),
                               ACT.Copy).then_inc(S["v_stored"], 1)

            for g in range(1, 6):
                split_to(qkv.u0 + 2 * g + 5)
                if g == 1:
                    store_v1(0)
                split_to(qkv.u0 + 2 * g + 6)
                if g == 2:
                    store_v1(1)
                if g >= 3:
                    for _ in range(2):
                        for qt in range(2):
                            attend1(qt)
                    if g == 4:
                        subln(0)
            for _ in range(2):
                for qt in range(2):
                    attend1(qt)
            subln(1)
            tail(stages["attn_out"], up3, ln(1, 4), bank=side_bank(up3))
            before_evictions(up3, side_bank(up3))
            gate_up(3)
            tail(stages["down", 3], w_in, None, full=True, bank=7)

            def qk2_job(n, name):
                act.wait_ge(S["tile_evicted"], w_in.t0 + GROUP * ((1, 2, 4, 5)[n] + 2))
                act.wait_ge(S["roped"], c.now("roped"))
                act.activation(work1[:, :, :], qkv2[name][:, :, :], ACT.Square).then_inc(S["head_sq"], 1)
                act.wait_ge(S["head_sums"], 2 + n + 1)
                act.activation(work2[:, :, :], ps[:, 4:6, :].rearrange("p b (a n) -> p (b a) n", a=2), ACT.Sqrt,
                               bias=eps[:, 0:1], scale=1.0 / P).then_inc(S["head_std"], 1)
                c.up("roped")

            def store_v2(n, dst):
                act.wait_ge(S["turned"], 2 + n + 1)
                act.activation(dst[:, :, :, :], ps[:, 4:6, :].rearrange("p k (a n) -> p k a n", a=4), ACT.Copy)\
                   .then_inc(S["v_stored"], 1)

            def attend2(qt):
                n = P * (qt + 1)
                soften(n, P ** -0.5)
                act.wait_ge(S["p_turned"], c.up("p_turned"))
                act.activation(pT2[:, 0:2 * (qt + 1), :], ps[:, 6, 0:2 * n].rearrange("p (w n) -> p w n", n=P),
                               ACT.Copy).then_inc(S["pT_ready"], 1)

            u0 = w_in.u0
            c.n["roped"] = 2
            split_to(u0 + 5)
            for g in range(11):
                split_to(u0 + 2 * g + 7)
                if g == 1:
                    act.wait_ge(S["roped"], 2)
                    for qt in range(2):
                        for _ in range(2):
                            e = c.up("idx_scored")
                            n = P * (qt + 1)
                            act.wait_ge(S["idx_scored"], e)
                            if e > 2:
                                act.wait_ge(S["idx_used"], e - 2)
                            act.activation((work1, work2)[(e - 1) % 2][:, :, 0:n], ps[:, 4:8, 0:n], ACT.Relu)\
                               .then_inc(S["idx_relu"], 1)
                elif g == 2:
                    act.wait_ge(S["idx_used"], 4)
                    qk2_job(0, "q_a")
                elif g == 3:
                    qk2_job(1, "k_a")
                elif g == 4:
                    store_v2(0, v_a)
                elif g == 5:
                    qk2_job(2, "q_b")
                    attend2(0)
                    attend2(1)
                elif g == 6:
                    qk2_job(3, "k_b")
                    attend2(0)
                    attend2(1)
                elif g == 7:
                    store_v2(1, v_b)
                elif g in (8, 9):
                    attend2(0)
                    attend2(1)
            for which in range(2):
                heads = slice(4 * which, 4 * which + 4)
                act.wait_ge(S["o_evicted"], 8 + 2 * which + 2)
                act.activation(o2_hi[:, heads, :], f[:, heads, 0:SEQ], ACT.Copy).then_inc(S["a_hi_ready"], 1)
            for k in range(4):
                act.wait_ge(S["tile_evicted"], w_in.t0 + GROUP * (k + 9))
                act.activation(gates[:, 4 * k:4 * k + 4, :], gates[:, 4 * k:4 * k + 4, :], ACT.Sigmoid)\
                   .then_inc(S["gate_ready"], 1)
            dsa, moba = stages["br_dsa"], stages["br_moba"]
            split_to(end_of(dsa) + 3)
            split_to(end_of(moba) + 3)
            for m in range(0, 8, 2):
                x = (pair_a, pair_b)[m // 2 % 2][:, :, 0:SEQ]
                act.wait_ge(S["act_in_ready"], I0["br"] + m // 2 + 1)
                act.activation(z_hi[:, m:m + 2, :], x, ACT.Copy).then_inc(S["a_hi_ready"], 1)
            up4 = stages["up", 4]
            tail(stages["w_out"], up4, None, full=True, normed=False, bank=side_bank(up4))
            split_to(up4.u0 + 5)
            gate_up(4)
            split_to(n_units)
            n_h = c.now("h_ready")
            for m in range(KT):
                act.wait_ge(S["h_ready"], n_h + m + 1)
                act.dma_start(out[:, m, :], h[:, m, META:TOK]).then_inc(out_stored, 16)


def _constants():
    f32 = np.float32
    con = np.zeros((P, C_ALL), f32)
    con[:, C_ONES:C_ONES + P] = 1
    con[:, C_IDENT:C_IDENT + P] = np.eye(P)

    def swap(block, half):
        r = np.zeros((P, P), f32)
        for b in range(0, P, block):
            for i in range(half):
                r[b + half + i, b + i] = -1
                r[b + i, b + half + i] = 1
        return r

    con[:, C_ROT1:C_ROT1 + P] = swap(64, 8)
    con[:, C_ROT2:C_ROT2 + P] = swap(128, 64)
    con[:, C_ROTI:C_ROTI + P] = swap(64, 32)

    def table(tokens, dim, theta, block):
        half = dim // 2
        inv = (f32(theta) ** (-np.arange(0, dim, 2, dtype=f32) / f32(dim))).astype(f32)
        ang = (np.arange(tokens, dtype=f32)[None, :] * inv[:, None]).astype(f32)
        cos, sin = np.ones((P, tokens), f32), np.zeros((P, tokens), f32)
        for b in range(0, P, block):
            for part in range(2):
                cos[b + part * half:b + (part + 1) * half] = np.cos(ang)
                sin[b + part * half:b + (part + 1) * half] = np.sin(ang)
        return cos, sin

    con[:, C_COS1:C_COS1 + TOK], con[:, C_SIN1:C_SIN1 + TOK] = table(TOK, 16, 500000.0, 64)
    con[:, C_MASK:] = np.where(np.arange(TOK)[None, :] <= META + P + np.arange(P)[:, None], 0, NEG)
    tables2 = np.stack([*table(SEQ, 128, 10000.0, 128), *table(SEQ, 64, 10000.0, 64)], axis=1)
    return con, tables2.astype(f32)


def _layout(a):
    def grouped(w):
        k, m = w.shape
        return w.reshape(k // 512, 4, P, m // 512, 512).transpose(3, 0, 2, 1, 4).reshape(-1, P, UNIT)

    def pairs(w, starts):
        return np.concatenate([w[:, s:s + 256] for s in starts], axis=1)

    def k_outer(w):
        return w.reshape(-1, 2, P, D).transpose(0, 2, 1, 3).reshape(-1, P, UNIT)

    def gate_up(w):
        return grouped(pairs(w, [s for g in range(FT // 2) for s in (256 * g, FF + 256 * g)]))

    units = []
    for i in range(2):
        units += [gate_up(a["ffn1_w_gu"][i]), k_outer(a["ffn1_w_down"][i])]
        if i == 0:
            w = a["conv_w_in"][0]
            units += [grouped(np.concatenate([pairs(w, [s for g in range(4) for s in (D + 256 * g, 2 * D + 256 * g)]),
                                              w[:, 0:D]], axis=1)),
                      k_outer(a["conv_w_out"][0])]
        else:
            w = a["attn_w_qkv"][0]
            units += [grouped(np.concatenate([w[:, 2 * D:], pairs(w, [s for g in range(4) for s in (256 * g, D + 256 * g)])],
                                             axis=1)),
                      k_outer(a["attn_w_o"][0])]
        units += [gate_up(a["ffn2_w_gu"][i]), k_outer(a["ffn2_w_down"][i])]
    w = a["w_in_2"][0]
    key = w[:, 2048:2112]
    small = np.concatenate([key, key, w[:, 2112:2120], np.zeros((D, 120), np.float32)], axis=1)
    units.append(small.reshape(KT, P, 256).transpose(1, 0, 2).reshape(1, P, UNIT))
    units.append(grouped(np.concatenate([w[:, 1536:2048], w[:, 0:1536], w[:, 2120:]], axis=1)))
    units += [k_outer(a["w_br_dsa_2"][0]), k_outer(a["w_br_moba_2"][0]), k_outer(a["w_out_2"][0]),
              gate_up(a["w_gate_up_2"][0]), k_outer(a["w_down_2"][0])]

    mod_units = a["w_mod_2"][0].reshape(P, 8, MOD_UNITS, 256).transpose(2, 0, 1, 3)
    x = np.concatenate([a["meta_tokens"], a["x"][0]], axis=0).reshape(TOK, KT, P).transpose(2, 1, 0)

    def columns(v):
        return v.reshape(-1, P).T

    cols = []
    for i in range(2):
        for name in ("ln_ffn1", "ln_mix", "ln_ffn2"):
            cols += [columns(a[name][i, 0]), columns(a[name][i, 1])]
    cols += [columns(a["conv_w"][0]), columns(a["b_mod_2"][0]), columns(a["g_mix_norm_2"][0]),
             columns(a["g_ffn_norm_2"][0])]
    cols += [columns(a[n][0]) for n in ("g_q_dsa_2", "g_k_dsa_2", "g_q_moba_2", "g_k_moba_2", "attn_subln_g")]
    cols.append(a["c_2"][0].reshape(P, 8))
    cols.append(np.concatenate([a["attn_lambda"][0].T, np.zeros((P - 64, 4), np.float32)], axis=0))
    return np.concatenate(units, axis=0), mod_units, x, np.concatenate(cols, axis=1)


def kernel(**inputs):
    import concourse.bacc as bacc
    from concourse.bass_utils import run_bass_kernel_spmd

    a = {name: np.asarray(value) for name, value in inputs.items()}
    names = ("w_units", "mod_units", "x_in", "vectors", "constants", "tables2")
    arrays = dict(zip(names, (*_layout(a), *_constants())))
    arrays = {name: np.ascontiguousarray(v) for name, v in arrays.items()}
    nc = bacc.Bacc("TRN2", target_bir_lowering=False, num_devices=1)
    args = [nc.dram_tensor(name, v.shape, F32, kind="ExternalInput").ap() for name, v in arrays.items()]
    out = nc.dram_tensor("out", (P, KT, SEQ), F32, kind="ExternalOutput").ap()
    build(nc, *args, out)
    r = run_bass_kernel_spmd(nc, [arrays], core_ids=[0])
    got = r.results[0]["out"]
    return np.ascontiguousarray(got.transpose(2, 1, 0)).reshape(1, SEQ, D)
```

```python
import math
from contextlib import ExitStack

import numpy as np

import concourse.bass as bass
from concourse import mybir

F32, F32R, BF16 = mybir.dt.float32, mybir.dt.float32r, mybir.dt.bfloat16
ACT = mybir.ActivationFunctionType
ALU = mybir.AluOpType
AX = mybir.AxisListType

P = 128
D = 1024
KT = D // P
SEQ, META = 256, 16
TOK = SEQ + META
FF = 2816
FT = FF // P
UNIT = 2048
RING = 4
GROUP = 4
NEG = -1e30
TAKEN = -3e38
LAMBDA_INIT = 0.8 - 0.6 * math.exp(-0.3)
EPS, SUBLN_EPS = 1e-6, 1e-5
HEADS1, HEADS2, IDX_HEADS = 8, 4, 8
TOPK = min(256, SEQ // 4)
IDX_SCALE = (IDX_HEADS ** -0.5) * (64 ** -0.5)
MOD_UNITS = 24
MOD_PARTS = 4
MOD_PER = MOD_UNITS // MOD_PARTS

V_LN = 0
V_CONV = V_LN + 96
V_BMOD = V_CONV + 24
V_GMIX = V_BMOD + 48
V_GFFN = V_GMIX + 8
V_GQK = V_GFFN + 8
V_SUB = V_GQK + 4
V_C = V_SUB + 1
V_LAM = V_C + 8
V_ALL = V_LAM + 4
C_ONES, C_IDENT, C_ROT1, C_ROT2, C_ROTI, C_COS1, C_SIN1, C_MASK = 0, 128, 256, 384, 512, 640, 912, 1184
C_ALL = C_MASK + TOK


class Stage:

    def __init__(self, plan, name, units, tiles, tokens, k_outer, quad_banks=False, tail=False):
        self.name, self.units, self.tiles, self.T = name, units, tiles, tokens
        self.u0, self.t0 = plan["u"], plan["t"]
        self.tail = tail
        self.e_shift = plan["tails"]
        if tail:
            plan["tails"] += tiles
        self.quad = quad_banks
        self.after_tail = plan["after_tail"]
        self.first_fresh = plan["quad"] or quad_banks
        plan["after_tail"] = tail
        plan["u"] += units
        plan["t"] += tiles
        plan["quad"] = quad_banks
        done = self.t0
        for n in range(units):
            if k_outer:
                last = n == units - 1
            elif name == "w_in":
                last = n % 2 == 0
            else:
                last = n % 2 == 1
            if last:
                done += 8 if k_outer else GROUP
                plan["used"].append(("tile_done", done))
            else:
                plan["mid"] += 1
                plan["used"].append(("weights_used", plan["mid"]))

    def evicted(self, t):
        return t - self.e_shift

    def bank(self, t):
        return (t - self.t0) % 4 if self.quad else t % 8


def build(nc, w_units, mod_units, x_in, vectors, constants, tables2, out):
    ctx = ExitStack()
    with ctx:
        def sb(name, shape, dt=F32):
            return ctx.enter_context(nc.sbuf_tensor(name, shape, dt))

        def sem(name):
            return ctx.enter_context(nc.semaphore(name))

        plan = {"u": 0, "t": 0, "quad": False, "mid": 0, "used": [], "tails": 0, "after_tail": True}
        stages = {}

        def stage(name, key, units, tiles, tokens, k_outer, quad=False):
            stages[key] = Stage(plan, name, units, tiles, tokens, k_outer, quad,
                                tail=k_outer and key not in ("br_dsa", "br_moba"))

        for layer in range(2):
            stage("gate_up", ("up", 2 * layer), 22, 44, TOK, False)
            stage("down", ("down", 2 * layer), 11, 8, TOK, True)
            if layer == 0:
                stage("conv_in", "conv_in", 12, 24, TOK, False)
                stage("proj", "conv_out", 4, 8, TOK, True)
                stage("gate_up", ("up", 1), 22, 44, TOK, False)
                stage("down", ("down", 1), 11, 8, TOK, True)
            else:
                stage("qkv", "qkv", 12, 24, TOK, False, True)
                stage("proj", "attn_out", 4, 8, SEQ, True)
                stage("gate_up", ("up", 3), 22, 44, SEQ, False)
                stage("down", ("down", 3), 11, 8, SEQ, True)
        stage("w_in", "w_in", 23, 48, SEQ, False, True)
        stage("proj", "br_dsa", 2, 8, SEQ, True)
        stage("proj", "br_moba", 2, 8, SEQ, True)
        stage("proj", "w_out", 4, 8, SEQ, True)
        stage("gate_up", ("up", 4), 22, 44, SEQ, False)
        stage("down", ("down", 4), 11, 8, SEQ, True)
        n_units = plan["u"]
        assert n_units % RING == 0
        S0, I0, E0, A0, X0 = {}, {}, {}, {}, {}
        silus = given = events = a_tiles = x_tiles = 0
        for key, n_silu, n_event, n_tiles, x in (
                (("up", 0), 11, 11, FT, 8), ("conv_in", 0, 4, 8, 8), (("up", 1), 11, 11, FT, 8),
                (("up", 2), 11, 11, FT, 8), ("qkv", 0, 4, 8, 8), (("up", 3), 11, 11, FT, 8),
                ("w_in", 0, 2, 8, 8), ("br", 0, 4, 8, 0), (("up", 4), 11, 11, FT, 8)):
            S0[key], I0[key], E0[key], A0[key], X0[key] = silus, given, events, a_tiles, x_tiles
            given += n_event if key != "w_in" else 0
            silus, events, a_tiles, x_tiles = silus + n_silu, events + n_event, a_tiles + n_tiles, x_tiles + x
        used_by = plan["used"]

        a_bytes = FT * TOK * 4
        mod_bytes = 8 * 256 * 4
        acc_bytes = MOD_PER * 256 * 4
        arena_at = -(-nc.sbuf_base // 32) * 32
        sb("arena", [P, (2 * a_bytes + mod_bytes + acc_bytes + 64) // 4])

        def at(name, offset, shape, dt=F32):
            return nc.alloc_sbuf_tensor_at(name, shape, dt, offset=arena_at + offset)

        a_hi = at("a_hi", 0, [P, FT, TOK], F32R)
        a_lo = at("a_lo", a_bytes, [P, FT, TOK], F32R)
        mod_w = at("mod_w", 2 * a_bytes, [P, 8, 256])
        mod_acc = at("mod_acc", 2 * a_bytes + mod_bytes, [P, MOD_PER, 256])
        free1, free2 = 8 * TOK * 4, a_bytes + 8 * TOK * 4
        v1_T = at("v1_T", free1, [P, 4, TOK])
        qk1 = at("qk1", free1 + 4 * TOK * 4, [P, 2, 4, TOK])
        pT1 = at("pT1", free1 + 12 * TOK * 4, [P, 3, P])
        v1 = at("v1", free2, [P, 3, HEADS1, P])
        o1 = at("o1", 2 * a_bytes, [P, HEADS1, SEQ])
        KB = 1024
        qkv2 = {n: at(n, i * 4 * KB, [P, 4, SEQ]) for i, n in enumerate(("q_a", "k_a"))}
        v_a = at("v_a", 8 * KB, [P, 2, HEADS2, P])
        qkv2["q_b"] = at("q_b", 16 * KB, [P, 4, SEQ])
        qkv2["k_b"] = at("k_b", 20 * KB, [P, 4, SEQ])
        v_b = at("v_b", 24 * KB, [P, 2, HEADS2, P])
        v2_T = at("v2_T", 12 * KB, [P, 4, SEQ])
        qi = at("qi", 28 * KB, [P, 4, SEQ])
        gates = at("gates", 32 * KB, [P, 16, SEQ])
        work1 = at("work1", 48 * KB, [P, 4, SEQ])
        work2 = at("work2", 52 * KB, [P, 4, SEQ])
        tab = at("tab", 56 * KB, [P, 4, SEQ])
        o2_hi = at("o2_hi", 0, [P, 8, SEQ], F32R)
        o2_lo = at("o2_lo", 8 * KB, [P, 8, SEQ], F32R)
        z_hi = at("z_hi", 16 * KB, [P, 8, SEQ], F32R)
        z_lo = at("z_lo", 24 * KB, [P, 8, SEQ], F32R)

        raw = sb("raw_weights", [P, RING, UNIT])
        w_hi = sb("w_hi", [P, RING, UNIT], F32R)
        w_lo = sb("w_lo", [P, RING, UNIT], F32R)
        h = sb("h", [P, KT, TOK])
        x_hi = sb("x_hi", [P, KT, TOK], F32R)
        x_lo = sb("x_lo", [P, KT, TOK], F32R)
        f = sb("f", [P, KT, TOK])
        pair_a = sb("pair_a", [P, 2, TOK])
        pair_b = sb("pair_b", [P, 2, TOK])
        norm_at = -(-nc.sbuf_base // 32) * 32
        sb("norm_area", [P, 5 * TOK])

        def norm_part(name, offset, shape, dt=F32):
            return nc.alloc_sbuf_tensor_at(name, shape, dt, offset=norm_at + offset)

        sq = norm_part("sq", 0, [P, 2, TOK])
        sq_sum = norm_part("sq_sum", 8 * TOK, [P, TOK])
        std_col = norm_part("std_col", 12 * TOK, [P, 4])
        r_col = norm_part("r_col", 12 * TOK + 32, [P, 4])
        rstd = norm_part("rstd", 16 * TOK, [P, TOK])
        ki = norm_part("ki", 0, [P, SEQ])
        wi_T = norm_part("wi_T", KB, [P, SEQ])
        score = norm_part("score", 2 * KB, [P, 2, SEQ])
        pT2 = norm_part("pT2", 2 * KB, [P, 4, P])
        sel = norm_part("sel", 4 * KB, [P, 2, SEQ], BF16)
        vec = sb("vec", [P, V_ALL])
        g_out = sb("g_out", [P, 49])
        mod = sb("mod", [P, 48])
        gain2 = sb("gain2", [P, 16])
        silu_c = sb("silu_c", [P, KT])
        eps = sb("eps", [P, 3])
        small = sb("small", [P, 4, 8])
        lam = sb("lam", [P, 8])
        head_col = sb("head_col", [P, 16])
        con = sb("con", [P, C_MASK])
        mask = sb("mask", [P, TOK], BF16)
        ident_b = sb("ident_b", [P, P], BF16)
        wi = sb("wi", [P, 2, 8])
        top8 = sb("top8", [P, 8])
        ones, ident = con[:, C_ONES:C_ONES + P], con[:, C_IDENT:C_IDENT + P]
        rot1, rot2, rot_i = (con[:, c:c + P] for c in (C_ROT1, C_ROT2, C_ROTI))
        cos1, sin1 = con[:, C_COS1:C_COS1 + TOK], con[:, C_SIN1:C_SIN1 + TOK]
        ps = ctx.enter_context(nc.psum_tensor("ps", [P, 8, 512], F32))

        raw_loaded = [sem(f"raw_loaded{i}") for i in range(RING)]
        inputs_loaded, mask_loaded, tables_loaded = sem("inputs_loaded"), sem("mask_loaded"), sem("tables_loaded")
        mod_loaded, out_stored = sem("mod_loaded"), sem("out_stored")
        S = {n: sem(n) for n in (
            "hi_ready", "lo_ready", "weights_used", "tile_done", "tile_evicted",
            "x_hi_ready", "x_ready", "act_in_ready", "a_hi_ready", "a_ready", "silu_done",
            "sq_ready", "sq_used", "sumsq_ready", "stats_done", "std_ready", "rstd_columns", "rstd_spread", "rstd_kept", "f_ready",
            "h_ready", "full_ready", "head_columns", "head_spread",
            "silu_c_ready", "mod_used", "mod_psum", "mod_evicted", "setup_done", "lam_in", "lam_sums", "lam_exp",
            "turned", "v_stored", "rotated", "rotation_read", "normed_heads", "roped", "qk_ready",
            "head_sq", "head_sums", "head_std",
            "scored", "max_ready", "probs_ready", "weights_ready", "p_turned", "pT_ready", "pv_done", "o_evicted",
            "idx_scored", "idx_relu", "idx_used", "w_turned", "wi_ready", "sel_ready", "gate_ready",
            "vec_chain")}

        class Count:

            def __init__(self):
                self.n = {}

            def up(self, name, k=1):
                self.n[name] = self.n.get(name, 0) + k
                return self.n[name]

            def now(self, name):
                return self.n.get(name, 0)

        def used_wait(eng, u):
            if u >= RING:
                name, n = used_by[u - RING]
                eng.wait_ge(S[name], n)

        QK_GROUP, V_GROUP = (0, 2, 3, 5), (1, 4)

        def end_of(st):
            return st.u0 + st.units

        block = ctx.enter_context(nc.Block())

        @block.sync
        def _(sp):
            for s in range(RING):
                sp.dma_start(raw[:, s, :], w_units[s]).then_inc(raw_loaded[s], 16)
            with sp.Fori(1, n_units // RING) as i:
                for s in range(RING):
                    sp.wait_ge(S["lo_ready"], RING * i + (s - RING + 1))
                    sp.dma_start(raw[:, s, :], w_units[RING * i + s]).then_inc(raw_loaded[s], 16)
            sp.wait_ge(out_stored, 16 * KT)

        @block.gpsimd
        def _(gp):
            gp.dma_start(h[:, :, :], x_in).then_inc(inputs_loaded, 16)
            gp.dma_start(vec[:, :], vectors).then_inc(inputs_loaded, 16)
            gp.dma_start(con[:, :], constants[:, 0:C_MASK]).then_inc(inputs_loaded, 16)
            gp.dma_start(f[:, 0, :], constants[:, C_MASK:C_ALL]).then_inc(mask_loaded, 16)
            for u in range(MOD_UNITS):
                if u:
                    gp.wait_ge(S["mod_used"], u)
                if u == 3 * MOD_PER:
                    gp.wait_ge(S["a_ready"], A0["up", 3])
                gp.dma_start(mod_w[:, :, :], mod_units[u]).then_inc(mod_loaded, 16)
            gp.wait_ge(S["mod_evicted"], MOD_PARTS)
            gp.dma_start(tab[:, :, :], tables2).then_inc(tables_loaded, 16)

        @block.tensor
        def _(pe):
            c = Count()

            def three_pass(dst, slot, col, hi, lo, start, stop):
                wh, wl = w_hi[:, slot, col:col + P], w_lo[:, slot, col:col + P]
                pe.matmul(dst, wh, hi, start=start, stop=False)
                pe.matmul(dst, wh, lo, start=False, stop=False)
                return pe.matmul(dst, wl, hi, start=False, stop=stop)

            def wait_bank(st, t, shift=0):
                n = st.evicted(t - (3 if st.quad else 7))
                if t < st.t0 + (4 if st.quad else 8):
                    if st.after_tail:
                        return
                    if st.first_fresh:
                        n = st.evicted(st.t0)
                pe.wait_ge(S["tile_evicted"], n + shift)

            def group(st, g, xs, i=0, x_base=None, bank_busy=None, between=None):
                for half in range(2):
                    u = st.u0 + 2 * g + half + (1 if st.name == "w_in" else 0)
                    pe.wait_ge(S["lo_ready"], u + 1 + 4 * i)
                    for kk in range(4):
                        k = 4 * half + kk
                        if x_base is not None:
                            pe.wait_ge(S["x_ready"], x_base + k + 1)
                        for m in range(GROUP):
                            t = st.t0 + GROUP * g + m + (4 if st.name == "w_in" else 0)
                            if k == 0:
                                wait_bank(st, t, 8 * i)
                                if bank_busy is not None:
                                    bank_busy(m)
                            ins = three_pass(ps[:, st.bank(t), 0:st.T], u % RING, (kk * GROUP + m) * P,
                                             xs[0][:, k, 0:st.T], xs[1][:, k, 0:st.T], k == 0, k == KT - 1)
                            if k == KT - 1:
                                ins.then_inc(S["tile_done"], 1)
                        if between is not None:
                            for job in between.get(k, ()):
                                job()
                    if half == 0:
                        ins.then_inc(S["weights_used"], 1)

            def k_outer(st, xs, a_base):
                for n in range(st.units):
                    u = st.u0 + n
                    pe.wait_ge(S["lo_ready"], u + 1)
                    last = n == st.units - 1
                    order = [(kk, m) for kk in range(2) for m in range(8)]
                    if last:
                        order = [(kk, m) for m in range(8) for kk in range(2)]
                    for kk, m in order:
                        k = 2 * n + kk
                        if m == 0:
                            pe.wait_ge(S["a_ready"], a_base + k + 1)
                        if k == 0:
                            wait_bank(st, st.t0 + m)
                        ins = three_pass(ps[:, st.bank(st.t0 + m), 0:st.T], u % RING, (kk * 8 + m) * P,
                                         xs[0][:, k, 0:st.T], xs[1][:, k, 0:st.T], k == 0, k == 2 * st.units - 1)
                        if k == 2 * st.units - 1:
                            ins.then_inc(S["tile_done"], 1)
                    if not last:
                        ins.then_inc(S["weights_used"], 1)

            def starts(T):
                return [0, P] if T == 2 * P else [0, P, T - P]

            def column_sums(T, bank):
                pe.wait_ge(S["sumsq_ready"], c.up("sumsq_ready"))
                for n, at_token in enumerate(starts(T)):
                    ins = pe.matmul(ps[:, bank, n:n + 1], sq_sum[:, at_token:at_token + P], ones[:, 0:1],
                                    start=True, stop=True)
                ins.then_inc(S["stats_done"], 1)

            def spread(T, bank):
                pe.wait_ge(S["rstd_columns"], c.up("rstd_columns"))
                for n, at_token in enumerate(starts(T)):
                    ins = pe.matmul(ps[:, bank, at_token:at_token + P], r_col[:, n:n + 1].broadcast_to([P, P]), ident,
                                    start=True, stop=True)
                ins.then_inc(S["rstd_spread"], 1)

            def stats(T, bank):
                column_sums(T, bank)
                spread(T, bank)

            def side_bank(st):
                return 7 if st.quad else st.bank(st.t0 + 7)

            def mod_bank(st):
                return 6 if st.quad else st.bank(st.t0 + 6)

            def mod_sums(part, bank):
                pe.wait_ge(S["mod_used"], MOD_PER * (part + 1))
                for n in range(2 * MOD_PER):
                    ins = pe.matmul(ps[:, bank, 288 + n:289 + n], mod_acc[:, n // 2, (n % 2) * P:(n % 2) * P + P],
                                    ones[:, 0:1], start=True, stop=True)
                ins.then_inc(S["mod_psum"], 1)

            def wait_side(part, m=None):
                if part is not None and m in (None, 2):
                    pe.wait_ge(S["mod_evicted"], part + 1)
                if m in (None, 3):
                    pe.wait_ge(S["rstd_kept"], c.now("rstd_kept"))

            def group_0(st, x_base, part=None):
                between = {KT - 2: [lambda: column_sums(st.T, side_bank(st))]}
                if part is not None:
                    between[3] = [lambda: mod_sums(part, mod_bank(st))]
                group(st, 0, (x_hi, x_lo), x_base=x_base, between=between)

            def first_groups(st, x_base, part=None):
                bank = side_bank(st)
                group_0(st, x_base, part)
                spread(st.T, bank)
                c.up("rstd_kept")
                group(st, 1, (x_hi, x_lo), bank_busy=lambda m: wait_side(part, m))

            def gate_up(n, x_base, part=None, deferred=True):
                st = stages["up", n]
                if deferred:
                    first_groups(st, x_base, part)
                else:
                    group(st, 0, (x_hi, x_lo), x_base=x_base)
                    group(st, 1, (x_hi, x_lo), bank_busy=lambda m: wait_side(part, m))
                with pe.Fori(0, 4) as i:
                    group(st, 2, (x_hi, x_lo), i)
                    group(st, 3, (x_hi, x_lo), i)
                group(st, 10, (x_hi, x_lo))

            pe.wait_ge(S["lam_in"], 1)
            pe.matmul(ps[:, 7, 0:2], ones, lam[:, 0:2], start=True, stop=True).then_inc(S["lam_sums"], 1)
            pe.wait_ge(S["lam_exp"], 1)

            gate_up(0, 0)
            k_outer(stages["down", 0], (a_hi, a_lo), A0["up", 0])
            conv = stages["conv_in"]
            stats(TOK, side_bank(conv))
            first_groups(conv, X0["conv_in"], 0)
            with pe.Fori(0, 2) as i:
                group(conv, 2, (x_hi, x_lo), i)
                group(conv, 3, (x_hi, x_lo), i)
            k_outer(stages["conv_out"], (a_hi, a_lo), A0["conv_in"])
            stats(TOK, side_bank(stages["up", 1]))
            gate_up(1, X0["up", 1])
            k_outer(stages["down", 1], (a_hi, a_lo), A0["up", 1])
            stats(TOK, side_bank(stages["up", 2]))
            gate_up(2, X0["up", 2], 1)
            k_outer(stages["down", 2], (a_hi, a_lo), A0["up", 2])
            qkv = stages["qkv"]
            stats(TOK, 7)

            def bank7_free():
                for name, n in (("v_stored", c.now("turned")), ("rotation_read", c.now("rotated")),
                                ("head_std", c.now("head_sums")), ("act_in_ready", I0["qkv"] + c.now("head_spread"))):
                    if n:
                        pe.wait_ge(S[name], n)

            def turn(g, w):
                at_token = (0, META, META + P)[w]
                bank7_free()
                pe.wait_ge(S["tile_evicted"], qkv.evicted(qkv.t0 + GROUP * (V_GROUP[g] + 1)))
                for m in range(4):
                    ins = pe.transpose(ps[:, 7, m * P:(m + 1) * P], v1_T[:, m, at_token:at_token + P], ident)
                ins.then_inc(S["turned"], 1)
                c.up("turned")

            def rot(g, m):
                bank7_free()
                pe.wait_ge(S["tile_evicted"], qkv.evicted(qkv.t0 + GROUP * (QK_GROUP[g] + 1)))
                pe.matmul(ps[:, 7, 0:TOK], rot1, qk1[:, g % 2, m, :], start=True, stop=True).then_inc(S["rotated"], 1)
                c.up("rotated")

            def scores(s):
                g, j, qt = s // 4, s // 2 % 2, s % 2
                n = META + P * (qt + 1)
                pe.wait_ge(S["qk_ready"], 4 * g + 2 + 2 * j)
                if s:
                    pe.wait_ge(S["probs_ready"], 2 * s)
                for comp in range(2):
                    rows = slice(64 * comp, 64 * comp + 64)
                    at_q = META + P * qt
                    pe.matmul(ps[:, 4 + comp, 0:n], qk1[rows, g % 2, j, at_q:at_q + P],
                              qk1[rows, g % 2, 2 + j, 0:n], start=True, stop=False)
                    ins = pe.matmul(ps[:, 4 + comp, 0:n], ident_b[:, :], mask[:, P - P * qt:P - P * qt + n],
                                    start=False, stop=True)
                ins.then_inc(S["scored"], 1)
                c.up("scored")

            def turn_p(s):
                pe.wait_ge(S["weights_ready"], c.up("weights_ready"))
                if s:
                    pe.wait_ge(S["head_sq"], s)
                for w, at_key in enumerate((0, META, META + P)[:s % 2 + 2]):
                    ins = pe.transpose(ps[:, 6, w * P:(w + 1) * P], pair_b[:, 0, at_key:at_key + P], ident)
                ins.then_inc(S["p_turned"], 1)
                c.up("p_turned")

            def values(s):
                pe.wait_ge(S["pT_ready"], s + 1)
                n = s % 2 + 2
                pe.wait_ge(S["v_stored"], 3 * (s // 8) + n)
                for w in range(n):
                    rows = slice(0, META if w == 0 else P)
                    ins = pe.matmul(ps[:, 6, 3 * P:4 * P], v1[rows, w, s // 2, :], pT1[rows, w, :],
                                    start=w == 0, stop=w == n - 1)
                ins.then_inc(S["pv_done"], 1)
                c.up("pv_done")

            def head_sums(squares, bank):
                for n in range(8):
                    ins = pe.matmul(ps[:, bank, n:n + 1], squares[:, n // 2, (n % 2) * P:(n % 2) * P + P], ones[:, 0:1],
                                    start=True, stop=True)
                ins.then_inc(S["head_sums"], 1)
                c.up("head_sums")

            def head_spread(heads, banks):
                pe.wait_ge(S["head_columns"], c.now("head_sums"))
                for h, bank in zip(heads, (b for b in banks for _ in range(2))):
                    for half in range(2):
                        n = 2 * h + half
                        ins = pe.matmul(ps[:, bank, (n % 4) * P:(n % 4) * P + P],
                                        head_col[:, 8 + n:9 + n].broadcast_to([P, P]), ident, start=True, stop=True)
                ins.then_inc(S["head_spread"], 1)
                c.up("head_spread")

            def subln_sums(half):
                bank7_free()
                pe.wait_ge(S["head_sq"], 8 * half + 8)
                c.n["head_sq"] = 8 * half + 8
                head_sums(f, 7)

            def subln_spread(r):
                bank7_free()
                head_spread((2 * r, 2 * r + 1), (7,))

            xs = (x_hi, x_lo)
            group_0(qkv, X0["qkv"], 2)
            spread(TOK, 7)
            c.up("rstd_kept")
            group(qkv, 1, xs, between={
                0: [lambda: wait_side(2)],
                1: [lambda: rot(0, 0)], 2: [lambda: rot(0, 2)], 3: [lambda: rot(0, 1)], 4: [lambda: rot(0, 3)],
                7: [lambda: scores(0)]})
            group(qkv, 2, xs, between={
                0: [lambda: turn(0, 0)],
                1: [lambda: turn(0, 1), lambda: scores(1), lambda: turn_p(0)],
                2: [lambda: turn(0, 2), lambda: values(0)],
                3: [lambda: scores(2), lambda: turn_p(1)], 4: [lambda: values(1)],
                5: [lambda: scores(3), lambda: turn_p(2)], 6: [lambda: values(2)],
                7: [lambda: turn_p(3)]})
            group(qkv, 3, xs, between={
                0: [lambda: values(3)],
                1: [lambda: rot(1, 0)], 2: [lambda: rot(1, 2)], 3: [lambda: rot(1, 1)],
                4: [lambda: rot(1, 3), lambda: scores(4)],
                6: [lambda: scores(5), lambda: turn_p(4)], 7: [lambda: values(4)]})
            group(qkv, 4, xs, between={
                0: [lambda: scores(6), lambda: turn_p(5)],
                1: [lambda: values(5), lambda: rot(2, 0)],
                2: [lambda: scores(7), lambda: turn_p(6), lambda: rot(2, 2)],
                3: [lambda: values(6), lambda: rot(2, 1)],
                4: [lambda: turn_p(7), lambda: rot(2, 3)],
                5: [lambda: values(7)], 6: [lambda: subln_sums(0)], 7: [lambda: scores(8)]})
            group(qkv, 5, xs, between={
                0: [lambda: turn(1, 0)],
                1: [lambda: turn(1, 1), lambda: scores(9), lambda: turn_p(8)],
                2: [lambda: turn(1, 2), lambda: values(8)],
                3: [lambda: scores(10), lambda: turn_p(9)],
                4: [lambda: values(9), lambda: subln_spread(0)],
                5: [lambda: scores(11), lambda: turn_p(10)],
                6: [lambda: values(10), lambda: subln_spread(1)],
                7: [lambda: turn_p(11)]})
            values(11)
            rot(3, 0)
            rot(3, 2)
            scores(12)
            rot(3, 1)
            rot(3, 3)
            for s in range(12, 16):
                if s < 15:
                    scores(s + 1)
                turn_p(s)
                values(s)
            subln_sums(1)
            subln_spread(0)
            subln_spread(1)
            attn_out = stages["attn_out"]
            pe.wait_ge(S["act_in_ready"], I0["qkv"] + 4)
            k_outer(attn_out, (a_hi, a_lo), A0["qkv"])
            stats(SEQ, side_bank(stages["up", 3]))
            gate_up(3, X0["up", 3])
            k_outer(stages["down", 3], (a_hi, a_lo), A0["up", 3])
            w_in = stages["w_in"]
            stats(SEQ, 7)
            mod_sums(3, 6)
            stats(SEQ, 7)

            def small_group():
                u = w_in.u0
                pe.wait_ge(S["lo_ready"], u + 1)
                for k in range(KT):
                    pe.wait_ge(S["x_ready"], X0["w_in"] + k + 1)
                    for m in range(2):
                        if k == 0:
                            wait_bank(w_in, w_in.t0 + m)
                        ins = three_pass(ps[:, m, 0:SEQ], u % RING, (k * 2 + m) * P, x_hi[:, k, 0:SEQ],
                                         x_lo[:, k, 0:SEQ], k == 0, k == KT - 1)
                        if k == KT - 1:
                            ins.then_inc(S["tile_done"], 2)

            def rotate(matrix, src, tiles, bank):
                if tiles == 1:
                    ins = pe.matmul(ps[:, bank, 0:SEQ], matrix, src[:, :], start=True, stop=True)
                else:
                    for m in range(2):
                        ins = pe.matmul(ps[:, bank + m, :], matrix, src[:, 2 * m:2 * m + 2, :], start=True, stop=True)
                ins.then_inc(S["rotated"], 1)
                c.up("roped")

            def idx_scores(qt, batch):
                n = P * (qt + 1)
                if c.now("idx_scored"):
                    pe.wait_ge(S["idx_relu"], c.now("idx_scored"))
                for b in range(4):
                    i = 4 * batch + b
                    rows = slice(64 * (i % 2), 64 * (i % 2) + 64)
                    ins = pe.matmul(ps[:, 4 + b, 0:n], qi[rows, i // 2, P * qt:P * qt + P], ki[rows, 0:n],
                                    start=True, stop=True)
                ins.then_inc(S["idx_scored"], 1)
                c.up("idx_scored")

            def turn_v2(g):
                pe.wait_ge(S["tile_evicted"], w_in.evicted(w_in.t0 + GROUP * (g + 2)))
                for kt in range(2):
                    for m in range(4):
                        ins = pe.transpose(ps[:, 4 + kt, m * P:(m + 1) * P], v2_T[:, m, kt * P:(kt + 1) * P], ident)
                ins.then_inc(S["turned"], 1)
                c.up("turned")

            def attend2(which, pair, qt):
                q, k, v = (qkv2["q_a"], qkv2["k_a"], v_a) if which == 0 else (qkv2["q_b"], qkv2["k_b"], v_b)
                n = P * (qt + 1)
                bias = sel[:, qt, 0:n] if which == 0 else mask[:, META + P - P * qt:META + P - P * qt + n]
                pe.wait_ge(S["probs_ready"], 2 * c.now("scored"))
                for comp in range(2):
                    head = 2 * pair + comp
                    pe.matmul(ps[:, 4 + comp, 0:n], q[:, head, P * qt:P * qt + P], k[:, head, 0:n],
                              start=True, stop=False)
                    ins = pe.matmul(ps[:, 4 + comp, 0:n], ident_b[:, :], bias, start=False, stop=True)
                ins.then_inc(S["scored"], 1)
                c.up("scored")
                pe.wait_ge(S["weights_ready"], c.up("weights_ready"))
                pe.wait_ge(S["pT_ready"], c.now("p_turned"))
                for comp in range(2):
                    for kt in range(qt + 1):
                        col = (comp * (qt + 1) + kt) * P
                        ins = pe.transpose(ps[:, 6, col:col + P], pair_b[:, comp, kt * P:(kt + 1) * P], ident)
                ins.then_inc(S["p_turned"], 1)
                c.up("p_turned")
                pe.wait_ge(S["pT_ready"], c.now("p_turned"))
                if qt == 0:
                    pe.wait_ge(S["o_evicted"], c.now("pv_done"))
                for comp in range(2):
                    for kt in range(qt + 1):
                        ins = pe.matmul(ps[:, 7, comp * SEQ + P * qt:comp * SEQ + P * qt + P],
                                        v[:, kt, 2 * pair + comp, :], pT2[:, comp * (qt + 1) + kt, :],
                                        start=kt == 0, stop=kt == qt)
                if qt == 1:
                    ins.then_inc(S["pv_done"], 1)
                    c.up("pv_done")

            def side_free():
                for name, n in (("roped", c.now("roped")),
                                ("v_stored", c.now("turned")), ("idx_relu", c.now("idx_scored")),
                                ("probs_ready", 2 * c.now("scored")), ("pT_ready", c.now("p_turned")),
                                ("o_evicted", c.now("pv_done"))):
                    pe.wait_ge(S[name], n)

            def qk2_job(name):
                side_free()
                pe.wait_ge(S["head_sq"], c.up("head_sq"))
                head_sums(work1, 4)
                head_spread(range(4), (5, 6))
                pe.wait_ge(S["normed_heads"], c.up("normed_heads"))
                rotate(rot2, qkv2[name], 4, 6)

            small_group()
            group(w_in, 0, xs)
            pe.wait_ge(S["mod_evicted"], 4)
            pe.wait_ge(S["tile_evicted"], w_in.evicted(w_in.t0 + GROUP))
            rotate(rot_i, ki, 1, 4)
            for qt in range(2):
                ins = pe.transpose(ps[:, 5, qt * P:(qt + 1) * P], wi_T[:, qt * P:(qt + 1) * P], ident)
            ins.then_inc(S["w_turned"], 1)
            group(w_in, 1, xs)
            pe.wait_ge(S["tile_evicted"], w_in.evicted(w_in.t0 + 2 * GROUP))
            rotate(rot_i, qi, 4, 6)
            side_free()
            pe.wait_ge(S["wi_ready"], 1)
            for qt in range(2):
                for batch in range(2):
                    idx_scores(qt, batch)
            group(w_in, 2, xs)
            qk2_job("q_a")
            group(w_in, 3, xs)
            qk2_job("k_a")
            group(w_in, 4, xs)
            side_free()
            turn_v2(3)
            group(w_in, 5, xs)
            qk2_job("q_b")
            side_free()
            pe.wait_ge(S["sel_ready"], 2)
            attend2(0, 0, 0)
            attend2(0, 0, 1)
            group(w_in, 6, xs)
            qk2_job("k_b")
            side_free()
            attend2(0, 1, 0)
            attend2(0, 1, 1)
            group(w_in, 7, xs)
            side_free()
            turn_v2(6)
            group(w_in, 8, xs)
            side_free()
            attend2(1, 0, 0)
            attend2(1, 0, 1)
            group(w_in, 9, xs)
            attend2(1, 1, 0)
            attend2(1, 1, 1)
            group(w_in, 10, xs)
            side_free()
            k_outer(stages["br_dsa"], (o2_hi, o2_lo), A0["w_in"])
            k_outer(stages["br_moba"], (o2_hi[:, 4:8, :], o2_lo[:, 4:8, :]), A0["w_in"] + 4)
            k_outer(stages["w_out"], (z_hi, z_lo), A0["br"])
            stats(SEQ, side_bank(stages["up", 4]))
            gate_up(4, X0["up", 4], deferred=False)
            k_outer(stages["down", 4], (a_hi, a_lo), A0["up", 4])

        @block.vector
        def _(dve):
            c = Count()
            nxt = [0]

            def chain(ins):
                ins.then_inc(S["vec_chain"], 1)
                dve.wait_ge(S["vec_chain"], c.up("vec_chain"))

            def low_part(u, i=0):
                dve.wait_ge(S["hi_ready"], u + 1 + 4 * i)
                dve.tensor_tensor(w_lo[:, u % RING, :], raw[:, u % RING, :], w_hi[:, u % RING, :].bitcast(F32),
                                  ALU.subtract).then_inc(S["lo_ready"], 1)

            def split_to(u_end):
                while nxt[0] < min(u_end, n_units):
                    low_part(nxt[0])
                    nxt[0] += 1

            def low_half(half):
                u, cols = nxt[0], slice(half * UNIT // 2, (half + 1) * UNIT // 2)
                if half == 0:
                    dve.wait_ge(S["hi_ready"], u + 1)
                ins = dve.tensor_tensor(w_lo[:, u % RING, cols], raw[:, u % RING, cols],
                                        w_hi[:, u % RING, cols].bitcast(F32), ALU.subtract)
                if half == 1:
                    ins.then_inc(S["lo_ready"], 1)
                    nxt[0] += 1

            def bcast(row, T, n=2):
                return row[:, 0:T].unsqueeze(1).broadcast_to([P, n, T])

            def gated_eviction(n, g, i=0):
                st = stages["up", n]
                T, t, e = st.T, st.t0 + GROUP * g, E0["up", n] + g
                b = t % 8
                gate, up = pair_a[:, :, 0:T], pair_b[:, :, 0:T]
                if A0["up", n] + g > 0:
                    dve.wait_ge(S["a_ready"], A0["up", n] + 2 * g + 4 * i)
                dve.wait_ge(S["tile_done"], t + 2 + 8 * i)
                if n < 4:
                    dve.tensor_tensor(gate, ps[:, b:b + 2, 0:T], bcast(rstd, T), ALU.mult).then_inc(S["tile_evicted"], 2)
                else:
                    dve.tensor_copy(gate, ps[:, b:b + 2, 0:T]).then_inc(S["tile_evicted"], 2)
                dve.wait_ge(S["tile_done"], t + 4 + 8 * i)
                if n < 4:
                    dve.tensor_tensor(up, ps[:, b + 2:b + 4, 0:T], bcast(rstd, T), ALU.mult).then_inc(S["tile_evicted"], 2)
                else:
                    dve.tensor_copy(up, ps[:, b + 2:b + 4, 0:T]).then_inc(S["tile_evicted"], 2)
                dve.wait_ge(S["tile_evicted"], st.evicted(t + 4) + 8 * i)
                dve.wait_ge(S["silu_done"], S0["up", n] + g + 1 + 2 * i)
                dve.tensor_tensor(up, gate, up, ALU.mult).then_inc(S["act_in_ready"], 1)
                dve.wait_ge(S["a_hi_ready"], e + 1 + 2 * i)
                k = bass.ds(2 * g + 4 * i, 2)
                dve.tensor_tensor(a_lo[:, k, 0:T], up, a_hi[:, k, 0:T].bitcast(F32), ALU.subtract).then_inc(S["a_ready"], 2)

            def gate_up(n):
                st = stages["up", n]
                for g in range(2):
                    split_to(st.u0 + 2 * g + 5)
                    gated_eviction(n, g)
                split_to(st.u0 + 9)
                with dve.Fori(0, 4) as i:
                    u = st.u0 + 9
                    gated_eviction(n, 2, i)
                    low_part(u, i)
                    low_part(u + 1, i)
                    gated_eviction(n, 3, i)
                    low_part(u + 2, i)
                    low_part(u + 3, i)
                nxt[0] = st.u0 + 25
                gated_eviction(n, 10)

            def mod_part(part):
                for n in range(MOD_PER):
                    dve.wait_ge(mod_loaded, 16 * (MOD_PER * part + n + 1))
                    if part == 0 and n == 0:
                        dve.wait_ge(S["silu_c_ready"], 1)
                    elif n == 0:
                        dve.wait_ge(S["mod_psum"], part)
                    acc = mod_acc[:, n, :]
                    chain(dve.tensor_scalar(acc, mod_w[:, 0, :], silu_c[:, 0:1], None, ALU.mult))
                    for j in range(1, 8):
                        ins = dve.scalar_tensor_tensor(acc, mod_w[:, j, :], silu_c[:, j:j + 1], acc, ALU.mult, ALU.add)
                        if j < 7:
                            chain(ins)
                    ins.then_inc(S["mod_used"], 1)
                    yield

            def mod_evict(part, bank):
                cols = slice(2 * MOD_PER * part, 2 * MOD_PER * (part + 1))
                dve.wait_ge(S["mod_psum"], part + 1)
                dve.tensor_tensor(mod[:, cols], ps[:, bank, 288:288 + 2 * MOD_PER],
                                  vec[:, V_BMOD + 2 * MOD_PER * part:V_BMOD + 2 * MOD_PER * (part + 1)],
                                  ALU.add).then_inc(S["mod_evicted"], 1)

            def down(n, part=None):
                st = stages["down", n]
                work = mod_part(part) if part is not None else iter(())
                for n, u in enumerate(range(nxt[0], end_of(st) + 3)):
                    split_to(u + 1)
                    if n in (0, 2, 3, 5, 6, 8):
                        next(work, None)

            def add_square(m, T):
                if m == 0:
                    return
                dve.wait_ge(S["sq_ready"], c.now("sq_ready") + m + 1)
                first = sq[:, 0, 0:T] if m == 1 else sq_sum[:, 0:T]
                if m > 1:
                    dve.wait_ge(S["sq_used"], c.now("sq_used") + m - 1)
                dve.tensor_tensor(sq_sum[:, 0:T], first, sq[:, m % 2, 0:T], ALU.add)\
                   .then_inc(S["sq_used" if m < 7 else "sumsq_ready"], 1)

            def squares_done():
                c.up("sq_ready", 8)
                c.up("sq_used", 6)

            def root(T):
                n = 2 if T == 2 * P else 3
                dve.wait_ge(S["std_ready"], c.up("std_ready"))
                dve.reciprocal(r_col[:, 0:n], std_col[:, 0:n]).then_inc(S["rstd_columns"], 1)
                dve.wait_ge(S["rstd_spread"], c.up("rstd_spread"))

            def tail(st, gain, nx, next_gain, shift=None, normed=True, part=None):
                T = st.T
                off = TOK - T
                split_to(nx.u0 + 3)
                if normed:
                    for m in range(8):
                        add_square(m, T)
                    squares_done()
                    root(T)
                if part is not None:
                    mod_evict(part, 6)
                    dve.wait_ge(S["mod_evicted"], MOD_PARTS)
                    for w in range(2):
                        chain(dve.tensor_scalar(gain2[:, 8 * w:8 * w + 8], mod[:, 8 + 24 * w:16 + 24 * w], 1.0, None, ALU.add))
                        chain(dve.tensor_tensor(gain2[:, 8 * w:8 * w + 8], gain2[:, 8 * w:8 * w + 8],
                                                vec[:, V_GMIX + 8 * w:V_GMIX + 8 * w + 8], ALU.mult))
                if not normed:
                    dve.wait_ge(S["f_ready"], 8 * 7)
                update_and_prepare(T, off, gain, next_gain, shift, normed, nx, spread=ps[:, side_bank(nx), :])

            def update_and_prepare(T, off, gain, next_gain, shift, normed, nx, update=True, spread=None):
                n_h = c.now("h_ready")
                n_v = c.now("vec_chain")
                deferred = shift is None
                for m in range(8 + 2):
                    if update and m < 8:
                        if normed:
                            if m >= 2:
                                dve.wait_ge(S["h_ready"], n_h + m - 1)
                            dve.tensor_tensor(pair_a[:, m % 2, 0:T], f[:, m, 0:T], spread[:, 0:T], ALU.mult)\
                               .then_inc(S["vec_chain"], 1)
                            c.up("vec_chain")
                    k = m - 1
                    if update and 0 <= k < 8:
                        src = f[:, k, 0:T]
                        if normed:
                            src = pair_a[:, k % 2, 0:T]
                            dve.wait_ge(S["vec_chain"], n_v + k + 1)
                        dve.scalar_tensor_tensor(h[:, k, off:off + T], src, gain[:, k:k + 1], h[:, k, off:off + T],
                                                 ALU.mult, ALU.add).then_inc(S["h_ready"], 1)
                    k = m - 2
                    if k >= 0 and nx is not None:
                        if deferred:
                            dve.wait_ge(S["x_hi_ready"], c.up("x_hi_ready"))
                            dve.scalar_tensor_tensor(x_lo[:, k, 0:T], h[:, k, off:off + T], next_gain[:, k:k + 1],
                                                     x_hi[:, k, 0:T].bitcast(F32), ALU.mult, ALU.subtract)\
                               .then_inc(S["x_ready"], 1)
                        add_square(k, T)
                if update:
                    c.up("h_ready", 8)
                if nx is None:
                    return
                squares_done()
                if deferred:
                    return
                root(T)
                for m in range(8 + 2):
                    if m < 8:
                        dve.tensor_tensor(f[:, m, 0:T], h[:, m, off:off + T], spread[:, 0:T], ALU.mult)\
                           .then_inc(S["vec_chain"], 1)
                        c.up("vec_chain")
                    k = m - 1
                    if 0 <= k < 8:
                        dve.wait_ge(S["vec_chain"], c.now("vec_chain") - (1 if m < 8 else 0))
                        dve.tensor_scalar(f[:, k, 0:T], f[:, k, 0:T], next_gain[:, k:k + 1], shift[:, k:k + 1],
                                          ALU.mult, ALU.add).then_inc(S["full_ready"], 1)
                    k = m - 2
                    if k >= 0:
                        dve.wait_ge(S["x_hi_ready"], c.up("x_hi_ready"))
                        dve.tensor_tensor(x_lo[:, k, 0:T], f[:, k, 0:T], x_hi[:, k, 0:T].bitcast(F32),
                                          ALU.subtract).then_inc(S["x_ready"], 1)

            def before_evictions(nx, deferred=True, part=None):
                split_to(nx.u0 + 5)
                if deferred:
                    root(nx.T)
                    dve.tensor_copy(rstd[:, 0:nx.T], ps[:, side_bank(nx), 0:nx.T]).then_inc(S["rstd_kept"], 1)
                    if part is not None:
                        mod_evict(part, 6 if nx.quad else nx.bank(nx.t0 + 6))
                    dve.wait_ge(S["rstd_kept"], c.up("rstd_kept"))

            def ln(layer, which):
                at_col = V_LN + 8 * (6 * layer + which)
                return vec[:, at_col:at_col + 8]

            def side_bank(st):
                return 7 if st.quad else st.bank(st.t0 + 7)

            dve.memset(eps[:, 0:1], EPS)
            dve.memset(eps[:, 1:2], SUBLN_EPS)
            dve.wait_ge(inputs_loaded, 48)
            for n in range(4):
                dve.tensor_scalar(g_out[:, 8 * n:8 * n + 8], ln(n // 2, 1 + 4 * (n % 2)), 0.5, None, ALU.mult)
            dve.tensor_scalar(g_out[:, 48:49], vec[:, V_SUB:V_SUB + 1], 1.0 - LAMBDA_INIT, None, ALU.mult)
            chain(dve.tensor_tensor(lam[:, 0:2], vec[:, V_LAM:V_LAM + 4:2], vec[:, V_LAM + 1:V_LAM + 4:2], ALU.mult))
            dve.wait_ge(mask_loaded, 16)
            dve.tensor_copy(ident_b[:, :], ident)
            dve.tensor_copy(mask[:, :], f[:, 0, :]).then_inc(S["lam_in"], 1)
            dve.wait_ge(S["lam_in"], 1)
            dve.wait_ge(S["lam_exp"], 1)
            chain(dve.tensor_tensor(lam[:, 4:5], lam[:, 2:3], lam[:, 3:4], ALU.subtract))
            chain(dve.tensor_scalar(lam[:, 5:6], lam[:, 4:5], LAMBDA_INIT, None, ALU.add))

            split_to(3)
            update_and_prepare(TOK, 0, None, ln(0, 0), None, False, stages["up", 0], update=False)
            before_evictions(stages["up", 0])
            gate_up(0)
            down(0, 0)
            conv = stages["conv_in"]
            tail(stages["down", 0], g_out[:, 0:8], conv, ln(0, 2))
            before_evictions(conv, part=0)
            for g in range(6):
                split_to(conv.u0 + 2 * g + 5)
                t = conv.t0 + GROUP * g
                b = t % 8
                if g < 4:
                    for q, dst in enumerate((pair_a, pair_b)):
                        dve.wait_ge(S["tile_done"], t + 2 + 2 * q)
                        dve.tensor_tensor(dst[:, :, :], ps[:, b + 2 * q:b + 2 * q + 2, 0:TOK], bcast(rstd, TOK),
                                          ALU.mult).then_inc(S["tile_evicted"], 2)
                    dve.wait_ge(S["tile_evicted"], conv.evicted(t + 4))
                    chain(dve.tensor_tensor(pair_a[:, :, :], pair_a[:, :, :], pair_b[:, :, :], ALU.mult))
                    taps = [V_CONV + 8 * j + 2 * g for j in range(3)]
                    for back in range(3):
                        for m in range(2):
                            y, w = f[:, 2 * g + m, back:TOK], vec[:, taps[2 - back] + m:taps[2 - back] + m + 1]
                            if back == 0:
                                ins = dve.tensor_scalar(y, pair_a[:, m, :], w, None, ALU.mult)
                            else:
                                ins = dve.scalar_tensor_tensor(y, pair_a[:, m, 0:TOK - back], w, y, ALU.mult, ALU.add)
                            if m == 0:
                                ins.then_inc(S["vec_chain"], 1)
                                c.up("vec_chain")
                            else:
                                chain(ins)
                else:
                    for q, dst in enumerate((pair_a, pair_b)):
                        k = 4 * (g - 4) + 2 * q
                        e = E0["conv_in"] + 2 * (g - 4) + q
                        dve.wait_ge(S["tile_done"], t + 2 + 2 * q)
                        if g == 5:
                            dve.wait_ge(S["a_ready"], A0["conv_in"] + 2 * q + 2)
                        dve.tensor_tensor(dst[:, :, :], ps[:, b + 2 * q:b + 2 * q + 2, 0:TOK], bcast(rstd, TOK),
                                          ALU.mult).then_inc(S["tile_evicted"], 2)
                        dve.wait_ge(S["tile_evicted"], conv.evicted(t + 2 + 2 * q))
                        dve.tensor_tensor(dst[:, :, :], dst[:, :, :], f[:, k:k + 2, :], ALU.mult)\
                           .then_inc(S["act_in_ready"], 1)
                    for q, src in enumerate((pair_a, pair_b)):
                        k = 4 * (g - 4) + 2 * q
                        dve.wait_ge(S["a_hi_ready"], E0["conv_in"] + 2 * (g - 4) + q + 1)
                        dve.tensor_tensor(a_lo[:, k:k + 2, :], src[:, :, :], a_hi[:, k:k + 2, :].bitcast(F32),
                                          ALU.subtract).then_inc(S["a_ready"], 2)
            tail(stages["conv_out"], ln(0, 3), stages["up", 1], ln(0, 4))
            before_evictions(stages["up", 1])
            gate_up(1)
            down(1, 1)
            up2 = stages["up", 2]
            tail(stages["down", 1], g_out[:, 8:16], up2, ln(1, 0))

            before_evictions(up2, part=1)
            gate_up(2)
            down(2, 2)
            qkv = stages["qkv"]
            tail(stages["down", 2], g_out[:, 16:24], qkv, ln(1, 2))
            before_evictions(qkv, part=2)

            def evict4(st, g, dst, T, scaled):
                t = st.t0 + GROUP * g + (4 if st.name == "w_in" else 0)
                dve.wait_ge(S["tile_done"], t + 4)
                if scaled:
                    ins = dve.tensor_tensor(dst, ps[:, 0:4, 0:T], bcast(rstd, T, 4), ALU.mult)
                else:
                    ins = dve.tensor_copy(dst, ps[:, 0:4, 0:T])
                ins.then_inc(S["tile_evicted"], 4)
                dve.wait_ge(S["tile_evicted"], st.evicted(t + 4))

            def maxima(n, scale):
                s = c.now("scored")
                c.up("scored")
                col = small[:, s % 4, :]
                dve.wait_ge(S["scored"], s + 1)
                chain(dve.tensor_reduce(col[:, 0:2], ps[:, 4:6, 0:n], AX.X, ALU.max))
                dve.tensor_scalar(col[:, 2:4], col[:, 0:2], -scale, None, ALU.mult).then_inc(S["max_ready"], 1)

            def factors():
                s = c.now("weights_ready")
                c.up("weights_ready")
                col = small[:, s % 4, :]
                dve.wait_ge(S["probs_ready"], 2 * s + 2)
                chain(dve.reciprocal(col[:, 6:8], col[:, 4:6]))
                return col

            def soften(n, scale):
                maxima(n, scale)
                return factors()

            def peak(s):
                maxima(META + P * (s % 2 + 1), 64 ** -0.5)

            def combine(s):
                n = META + P * (s % 2 + 1)
                col = factors()
                chain(dve.tensor_scalar(col[:, 7:8], col[:, 7:8], lam[:, 5:6], None, ALU.mult))
                chain(dve.tensor_scalar(pair_a[:, 1, 0:n], pair_a[:, 1, 0:n], col[:, 7:8], None, ALU.mult))
                if s:
                    dve.wait_ge(S["p_turned"], s)
                dve.scalar_tensor_tensor(pair_b[:, 0, 0:n], pair_a[:, 0, 0:n], col[:, 6:7], pair_a[:, 1, 0:n],
                                         ALU.mult, ALU.subtract).then_inc(S["weights_ready"], 1)
                c.up("p_turned")

            def rope(g, m):
                x, turned = qk1[:, g % 2, m, :], f[:, 4 + m, :]
                dve.wait_ge(S["rotated"], c.up("rotated"))
                dve.tensor_tensor(turned, ps[:, 7, 0:TOK], sin1, ALU.mult).then_inc(S["rotation_read"], 1)
                dve.tensor_tensor(x, x, cos1, ALU.mult).then_inc(S["vec_chain"], 1)
                dve.wait_ge(S["rotation_read"], c.up("rotation_read"))
                dve.wait_ge(S["vec_chain"], c.up("vec_chain"))
                dve.tensor_tensor(x, x, turned, ALU.add).then_inc(S["qk_ready"], 1)

            def head_roots():
                dve.wait_ge(S["head_std"], c.up("head_std"))
                dve.reciprocal(head_col[:, 8:16], head_col[:, 0:8]).then_inc(S["head_columns"], 1)

            def subln(r):
                x = o1[:, 2 * r:2 * r + 2, :].rearrange("p a n -> p (a n)")
                dve.wait_ge(S["head_spread"], c.up("head_spread"))
                dve.scalar_tensor_tensor(x, x, g_out[:, 48:49], ps[:, 7, :], ALU.mult, ALU.mult)\
                   .then_inc(S["act_in_ready"], 1)

            def subln_lo(r):
                heads = slice(2 * r, 2 * r + 2)
                dve.wait_ge(S["a_hi_ready"], E0["qkv"] + r + 1)
                dve.tensor_tensor(a_lo[:, heads, 0:SEQ], o1[:, heads, :], a_hi[:, heads, 0:SEQ].bitcast(F32),
                                  ALU.subtract).then_inc(S["a_ready"], 2)

            def evict_qk(g):
                evict4(qkv, QK_GROUP[g], qk1[:, g % 2, :, :], TOK, True)

            evict_qk(0)
            low_half(0)
            rope(0, 0)
            low_half(1)
            rope(0, 2)
            rope(0, 1)
            low_half(0)
            rope(0, 3)
            low_half(1)
            evict4(qkv, V_GROUP[0], v1_T[:, :, :], TOK, True)
            peak(0)
            low_half(0)
            combine(0)
            peak(1)
            low_half(1)
            combine(1)
            peak(2)
            combine(2)
            peak(3)
            low_half(0)
            combine(3)
            low_half(1)
            evict_qk(1)
            low_half(0)
            rope(1, 0)
            low_half(1)
            rope(1, 2)
            rope(1, 1)
            rope(1, 3)
            peak(4)
            low_half(0)
            combine(4)
            peak(5)
            low_half(1)
            evict_qk(2)
            combine(5)
            low_half(0)
            peak(6)
            rope(2, 0)
            combine(6)
            low_half(1)
            peak(7)
            rope(2, 2)
            combine(7)
            rope(2, 1)
            low_half(0)
            rope(2, 3)
            low_half(1)
            dve.wait_ge(S["turned"], 3)
            evict4(qkv, V_GROUP[1], v1_T[:, :, :], TOK, True)
            peak(8)
            head_roots()
            low_half(0)
            combine(8)
            peak(9)
            low_half(1)
            combine(9)
            peak(10)
            combine(10)
            subln(0)
            peak(11)
            low_half(0)
            combine(11)
            subln(1)
            subln_lo(0)
            subln_lo(1)
            low_half(1)
            evict_qk(3)
            rope(3, 0)
            rope(3, 2)
            peak(12)
            rope(3, 1)
            combine(12)
            rope(3, 3)
            for s in range(13, 16):
                peak(s)
                if s < 15:
                    low_half(s - 13)
                combine(s)
            head_roots()
            for r in (2, 3):
                subln(r)
            for r in (2, 3):
                subln_lo(r)
            tail(stages["attn_out"], ln(1, 3), stages["up", 3], ln(1, 4))
            before_evictions(stages["up", 3])
            gate_up(3)
            down(3, 3)
            w_in = stages["w_in"]
            tail(stages["down", 3], g_out[:, 24:32], w_in, gain2[:, 0:8], shift=mod[:, 0:8], part=3)

            def rope2(x, which, tiles, bank):
                cos, sin = tab[:, 2 * which, :], tab[:, 2 * which + 1, :]
                dve.wait_ge(S["rotated"], c.up("rotated"))
                if c.now("roped"):
                    dve.wait_ge(S["roped"], c.now("roped"))
                c.up("roped")
                if tiles == 1:
                    dve.tensor_tensor(work1[:, 0, :], ps[:, bank, 0:SEQ], sin, ALU.mult)
                    chain(dve.tensor_tensor(x, x, cos, ALU.mult))
                    ins = dve.tensor_tensor(x, x, work1[:, 0, :], ALU.add)
                else:
                    for m in range(2):
                        dve.tensor_tensor(work1[:, 2 * m:2 * m + 2, :], ps[:, bank + m, :].rearrange("p (a n) -> p a n", a=2),
                                          bcast(sin, SEQ, 2), ALU.mult)
                    chain(dve.tensor_tensor(x, x, bcast(cos, SEQ, 4), ALU.mult))
                    ins = dve.tensor_tensor(x, x, work1[:, :, :], ALU.add)
                ins.then_inc(S["roped"], 1)

            def qk2_job(n, name):
                x = qkv2[name][:, :, :]
                head_roots()
                dve.wait_ge(S["head_spread"], c.up("head_spread"))
                flat = x.rearrange("p (b a) n -> p b (a n)", b=2)
                dve.scalar_tensor_tensor(flat, flat, vec[:, V_GQK + n:V_GQK + n + 1], ps[:, 5:7, :], ALU.mult, ALU.mult)\
                   .then_inc(S["normed_heads"], 1)
                rope2(x, 0, 4, 6)

            def idx_scores(qt, batch):
                n = P * (qt + 1)
                e = c.up("idx_relu")
                dve.wait_ge(S["idx_relu"], e)
                src = (work1, work2)[(e - 1) % 2]
                for b in range(4):
                    i = 4 * batch + b
                    before = mask[:, META + P - P * qt:META + P - P * qt + n] if i == 0 else score[:, qt, 0:n]
                    ins = dve.scalar_tensor_tensor(score[:, qt, 0:n], src[:, b, 0:n], wi[:, qt, i:i + 1], before,
                                                   ALU.mult, ALU.add)
                    if b < 3:
                        chain(ins)
                ins.then_inc(S["idx_used"], 1)
                dve.wait_ge(S["idx_used"], e)

            def select(qt):
                n = P * (qt + 1)
                x = score[:, qt, 0:n]
                for _ in range(TOPK // 8):
                    chain(dve.max(top8[:, :], x))
                    chain(dve.match_replace(x, top8[:, :], x, TAKEN))
                chain(dve.tensor_scalar(x, x, TAKEN / 2, NEG, ALU.is_gt, ALU.mult))
                dve.tensor_tensor(sel[:, qt, 0:n], x, mask[:, META + P - P * qt:META + P - P * qt + n],
                                  ALU.add).then_inc(S["sel_ready"], 1)

            def attend2(which, pair, qt):
                n = P * (qt + 1)
                col = soften(n, P ** -0.5)
                dve.wait_ge(S["p_turned"], c.now("p_turned"))
                for comp in range(2):
                    ins = dve.tensor_scalar(pair_b[:, comp, 0:n], pair_a[:, comp, 0:n], col[:, 6 + comp:7 + comp],
                                            None, ALU.mult)
                ins.then_inc(S["weights_ready"], 1)
                c.up("p_turned")
                if qt == 1:
                    dve.wait_ge(S["pv_done"], 16 + c.up("pv_done"))
                    head = 4 * which + 2 * pair
                    dve.tensor_copy(f[:, head:head + 2, 0:SEQ], ps[:, 7, :].rearrange("p (a n) -> p a n", a=2))\
                       .then_inc(S["o_evicted"], 1)

            u0 = w_in.u0
            split_to(u0 + 5)
            dve.wait_ge(S["tile_done"], w_in.t0 + 4)
            dve.tensor_copy(ki[:, :], ps[:, 0, 0:SEQ])
            dve.tensor_copy(wi_T[:, :], ps[:, 1, 0:SEQ]).then_inc(S["tile_evicted"], 4)
            dve.wait_ge(S["tile_evicted"], w_in.evicted(w_in.t0 + 4))
            dests = [qi, qkv2["q_a"], qkv2["k_a"], v2_T, qkv2["q_b"], qkv2["k_b"], v2_T]
            dve.wait_ge(tables_loaded, 16)
            for g in range(11):
                split_to(u0 + 2 * g + 6)
                if g < 7:
                    if g == 6:
                        dve.wait_ge(S["turned"], 7)
                    evict4(w_in, g, dests[g][:, :, :], SEQ, False)
                else:
                    k = 4 * (g - 7)
                    evict4(w_in, g, gates[:, k:k + 4, :], SEQ, False)
                split_to(u0 + 2 * g + 7)
                if g == 0:
                    rope2(ki[:, :], 1, 1, 4)
                    dve.wait_ge(S["w_turned"], 1)
                    for qt in range(2):
                        ins = dve.tensor_scalar(wi[:, qt, :], ps[:, 5, qt * P:qt * P + 8], IDX_SCALE, None, ALU.mult)
                    ins.then_inc(S["wi_ready"], 1)
                    dve.wait_ge(S["wi_ready"], 1)
                elif g == 1:
                    rope2(qi[:, :, :], 1, 4, 6)
                    for qt in range(2):
                        for batch in range(2):
                            idx_scores(qt, batch)
                elif g == 2:
                    qk2_job(0, "q_a")
                    select(0)
                elif g == 3:
                    qk2_job(1, "k_a")
                    select(1)
                elif g == 5:
                    qk2_job(2, "q_b")
                    attend2(0, 0, 0)
                    attend2(0, 0, 1)
                elif g == 6:
                    qk2_job(3, "k_b")
                    attend2(0, 1, 0)
                    attend2(0, 1, 1)
                elif g in (8, 9):
                    attend2(1, g - 8, 0)
                    attend2(1, g - 8, 1)
            for which in range(2):
                heads = slice(4 * which, 4 * which + 4)
                dve.wait_ge(S["a_hi_ready"], E0["w_in"] + which + 1)
                dve.tensor_tensor(o2_lo[:, heads, :], f[:, heads, 0:SEQ], o2_hi[:, heads, :].bitcast(F32),
                                  ALU.subtract).then_inc(S["a_ready"], 4)
            dsa, moba, w_out = stages["br_dsa"], stages["br_moba"], stages["w_out"]
            split_to(end_of(dsa) + 3)
            dve.wait_ge(S["gate_ready"], 4)
            for m in range(0, 8, 2):
                t = dsa.t0 + m
                dve.wait_ge(S["tile_done"], t + 2)
                dve.tensor_tensor(gates[:, m:m + 2, :], ps[:, t % 8:t % 8 + 2, 0:SEQ], gates[:, m:m + 2, :],
                                  ALU.mult).then_inc(S["tile_evicted"], 2)
            split_to(end_of(moba) + 3)
            for m in range(0, 8, 2):
                t, e = moba.t0 + m, E0["br"] + m // 2
                x = (pair_a, pair_b)[m // 2 % 2][:, :, 0:SEQ]
                dve.wait_ge(S["tile_done"], t + 2)
                if m >= 4:
                    dve.wait_ge(S["a_ready"], A0["br"] + m - 2)
                dve.tensor_tensor(x, ps[:, t % 8:t % 8 + 2, 0:SEQ], gates[:, 8 + m:10 + m, :],
                                  ALU.mult).then_inc(S["tile_evicted"], 2)
                dve.wait_ge(S["tile_evicted"], moba.evicted(t + 2))
                dve.tensor_tensor(x, x, gates[:, m:m + 2, :], ALU.add).then_inc(S["act_in_ready"], 1)
                dve.wait_ge(S["a_hi_ready"], e + 1)
                dve.tensor_tensor(z_lo[:, m:m + 2, :], x, z_hi[:, m:m + 2, :].bitcast(F32), ALU.subtract)\
                   .then_inc(S["a_ready"], 2)
            tail(w_out, mod[:, 16:24], stages["up", 4], gain2[:, 8:16], shift=mod[:, 24:32], normed=False)
            before_evictions(stages["up", 4], deferred=False)
            gate_up(4)
            down(4)
            last = stages["down", 4]
            for m in range(8):
                dve.wait_ge(S["tile_done"], last.t0 + m + 1)
                dve.scalar_tensor_tensor(h[:, m, META:TOK], ps[:, last.bank(last.t0 + m), 0:SEQ], mod[:, 40 + m:41 + m],
                                         h[:, m, META:TOK], ALU.mult, ALU.add).then_inc(S["h_ready"], 1)

        @block.scalar
        def _(act):
            c = Count()
            nxt = [0]

            def high_part(u, i=0):
                act.wait_ge(raw_loaded[u % RING], 16 * (u // RING + 1) + 16 * i)
                if u >= RING:
                    name, n = used_by[u - RING]
                    act.wait_ge(S[name], n + (8 if name == "tile_done" else 2) * i)
                act.activation(w_hi[:, u % RING, :], raw[:, u % RING, :], ACT.Copy).then_inc(S["hi_ready"], 1)

            def split_to(u_end):
                while nxt[0] < min(u_end, n_units):
                    high_part(nxt[0])
                    nxt[0] += 1

            def gated(n, g, i=0):
                st = stages["up", n]
                T, t = st.T, st.t0 + GROUP * g
                act.wait_ge(S["tile_evicted"], st.evicted(t + 2) + 8 * i)
                act.activation(pair_a[:, :, 0:T], pair_a[:, :, 0:T], ACT.Silu).then_inc(S["silu_done"], 1)
                act.wait_ge(S["act_in_ready"], I0["up", n] + g + 1 + 2 * i)
                act.activation(a_hi[:, bass.ds(2 * g + 4 * i, 2), 0:T], pair_b[:, :, 0:T], ACT.Copy)\
                   .then_inc(S["a_hi_ready"], 1)

            def gate_up(n):
                st = stages["up", n]
                for g in range(2):
                    split_to(st.u0 + 2 * g + 5)
                    gated(n, g)
                split_to(st.u0 + 9)
                with act.Fori(0, 4) as i:
                    u = st.u0 + 9
                    gated(n, 2, i)
                    high_part(u, i)
                    high_part(u + 1, i)
                    gated(n, 3, i)
                    high_part(u + 2, i)
                    high_part(u + 3, i)
                nxt[0] = st.u0 + 25
                gated(n, 10)

            def square(m, src, T):
                if m >= 2:
                    act.wait_ge(S["sq_used"], c.now("sq_used") + max(1, m - 2))
                act.activation(sq[:, m % 2, 0:T], src, ACT.Square).then_inc(S["sq_ready"], 1)

            def root(T, bank):
                act.wait_ge(S["stats_done"], c.up("stats_done"))
                n = 2 if T == 2 * P else 3
                act.activation(std_col[:, 0:n], ps[:, bank, 0:n], ACT.Sqrt, bias=eps[:, 0:1], scale=1.0 / D)\
                   .then_inc(S["std_ready"], 1)

            def tail(st, nx, next_gain, full=False, normed=True, bank=None):
                T = st.T
                off = TOK - T
                split_to(nx.u0 + 3)
                act.activation(eps[:, 2:3], eps[:, 0:1], ACT.Sqrt)
                for m in range(8):
                    sums = ps[:, st.bank(st.t0 + m), 0:T]
                    act.wait_ge(S["tile_done"], st.t0 + m + 1)
                    act.activation(f[:, m, 0:T], sums, ACT.Copy).then_inc(S["f_ready"], 1)
                    if normed:
                        square(m, sums, T)
                if normed:
                    c.up("sq_used", 6)
                    root(T, bank)
                prepare(T, off, next_gain, full, bank)

            def prepare(T, off, next_gain, full, bank, update=True):
                for m in range(8):
                    if update:
                        act.wait_ge(S["h_ready"], c.up("h_ready"))
                    if not full:
                        act.activation(x_hi[:, m, 0:T], h[:, m, off:off + T], ACT.Identity,
                                       scale=next_gain[:, m:m + 1]).then_inc(S["x_hi_ready"], 1)
                    square(m, h[:, m, off:off + T], T)
                c.up("sq_used", 6)
                if full:
                    root(T, bank)
                    for m in range(8):
                        act.wait_ge(S["full_ready"], c.up("full_ready"))
                        act.activation(x_hi[:, m, 0:T], f[:, m, 0:T], ACT.Copy).then_inc(S["x_hi_ready"], 1)

            def before_evictions(nx, bank):
                split_to(nx.u0 + 5)
                root(nx.T, bank)

            def ln(layer, which):
                at_col = V_LN + 8 * (6 * layer + which)
                return vec[:, at_col:at_col + 8]

            def side_bank(st):
                return 7 if st.quad else st.bank(st.t0 + 7)

            act.wait_ge(inputs_loaded, 48)
            act.activation(silu_c[:, :], vec[:, V_C:V_C + 8], ACT.Silu).then_inc(S["silu_c_ready"], 1)
            act.wait_ge(S["lam_sums"], 1)
            act.activation(lam[:, 2:4], ps[:, 7, 0:2], ACT.Exp).then_inc(S["lam_exp"], 1)

            split_to(3)
            prepare(TOK, 0, ln(0, 0), False, None, update=False)
            before_evictions(stages["up", 0], side_bank(stages["up", 0]))
            gate_up(0)
            conv = stages["conv_in"]
            tail(stages["down", 0], conv, ln(0, 2), bank=side_bank(conv))
            before_evictions(conv, side_bank(conv))
            for g in range(6):
                split_to(conv.u0 + 2 * g + 5)
                if g >= 4:
                    for q, src in enumerate((pair_a, pair_b)):
                        k = 4 * (g - 4) + 2 * q
                        act.wait_ge(S["act_in_ready"], I0["conv_in"] + 2 * (g - 4) + q + 1)
                        act.activation(a_hi[:, k:k + 2, :], src[:, :, :], ACT.Copy).then_inc(S["a_hi_ready"], 1)
            up1, up2, qkv, up3, w_in = (stages["up", 1], stages["up", 2], stages["qkv"], stages["up", 3], stages["w_in"])
            tail(stages["conv_out"], up1, ln(0, 4), bank=side_bank(up1))
            before_evictions(up1, side_bank(up1))
            gate_up(1)
            tail(stages["down", 1], up2, ln(1, 0), bank=side_bank(up2))

            before_evictions(up2, side_bank(up2))
            gate_up(2)
            tail(stages["down", 2], qkv, ln(1, 2), bank=7)
            before_evictions(qkv, 7)

            def soften(n, scale):
                s = c.now("scored")
                c.up("scored")
                col = small[:, s % 4, :]
                act.wait_ge(S["max_ready"], s + 1)
                if s:
                    act.wait_ge(S["weights_ready"], s)
                for comp in range(2):
                    act.activation(pair_a[:, comp, 0:n], ps[:, 4 + comp, 0:n], ACT.Exp, bias=col[:, 2 + comp:3 + comp],
                                   scale=scale, accum_out=col[:, 4 + comp:5 + comp]).then_inc(S["probs_ready"], 1)

            def exps(s):
                soften(META + P * (s % 2 + 1), 64 ** -0.5)

            def store_p(s):
                w = s % 2 + 2
                act.wait_ge(S["p_turned"], c.up("p_turned"))
                act.activation(pT1[:, 0:w, :], ps[:, 6, 0:w * P].rearrange("p (w n) -> p w n", w=w), ACT.Copy)\
                   .then_inc(S["pT_ready"], 1)

            def store_o(s):
                head, cols = s // 2, slice(P * (s % 2), P * (s % 2) + P)
                act.wait_ge(S["pv_done"], s + 1)
                act.activation(o1[:, head, cols], ps[:, 6, 3 * P:4 * P], ACT.Copy).then_inc(S["o_evicted"], 1)
                if s == 8:
                    act.wait_ge(S["head_sums"], 1)
                act.activation(f[:, head % 4, cols], ps[:, 6, 3 * P:4 * P], ACT.Square).then_inc(S["head_sq"], 1)

            def store_v(n):
                g, w = n // 3, n % 3
                act.wait_ge(S["turned"], n + 1)
                act.activation(v1[:, w, 4 * g:4 * g + 4, :], ps[:, 7, :].rearrange("p (a n) -> p a n", a=4),
                               ACT.Copy).then_inc(S["v_stored"], 1)

            def subln_std(half):
                act.wait_ge(S["head_sums"], half + 1)
                if half:
                    act.wait_ge(S["head_columns"], 1)
                act.activation(head_col[:, 0:8], ps[:, 7, 0:8], ACT.Sqrt,
                               bias=eps[:, 1:2], scale=1.0 / P).then_inc(S["head_std"], 1)

            def subln_hi(r):
                heads = slice(2 * r, 2 * r + 2)
                act.wait_ge(S["act_in_ready"], I0["qkv"] + r + 1)
                act.activation(a_hi[:, heads, 0:SEQ], o1[:, heads, :], ACT.Copy).then_inc(S["a_hi_ready"], 1)

            def split():
                split_to(nxt[0] + 1)

            split()
            split()
            split()
            exps(0)
            store_v(0)
            store_v(1)
            store_p(0)
            exps(1)
            store_v(2)
            store_o(0)
            store_p(1)
            exps(2)
            split()
            store_o(1)
            store_p(2)
            exps(3)
            store_o(2)
            store_p(3)
            split()
            store_o(3)
            split()
            exps(4)
            store_p(4)
            exps(5)
            store_o(4)
            split()
            store_p(5)
            exps(6)
            store_o(5)
            store_p(6)
            exps(7)
            store_o(6)
            split()
            store_p(7)
            store_o(7)
            subln_std(0)
            split()
            exps(8)
            store_v(3)
            store_v(4)
            store_p(8)
            exps(9)
            store_v(5)
            store_o(8)
            store_p(9)
            exps(10)
            split()
            store_o(9)
            store_p(10)
            exps(11)
            subln_hi(0)
            store_o(10)
            subln_hi(1)
            store_p(11)
            split()
            store_o(11)
            exps(12)
            for s in range(12, 16):
                store_p(s)
                if s < 15:
                    exps(s + 1)
                store_o(s)
            subln_std(1)
            subln_hi(2)
            subln_hi(3)
            tail(stages["attn_out"], up3, ln(1, 4), bank=side_bank(up3))
            before_evictions(up3, side_bank(up3))
            gate_up(3)
            tail(stages["down", 3], w_in, None, full=True, bank=7)

            def qk2_job(n, name):
                act.wait_ge(S["tile_evicted"], w_in.evicted(w_in.t0 + GROUP * ((1, 2, 4, 5)[n] + 2)))
                act.wait_ge(S["roped"], c.now("roped"))
                act.activation(work1[:, :, :], qkv2[name][:, :, :], ACT.Square).then_inc(S["head_sq"], 1)
                act.wait_ge(S["head_sums"], 2 + n + 1)
                act.activation(head_col[:, 0:8], ps[:, 4, 0:8], ACT.Sqrt,
                               bias=eps[:, 0:1], scale=1.0 / P).then_inc(S["head_std"], 1)
                c.up("roped")

            def store_v2(n, dst):
                act.wait_ge(S["turned"], 6 + n + 1)
                act.activation(dst[:, :, :, :], ps[:, 4:6, :].rearrange("p k (a n) -> p k a n", a=4), ACT.Copy)\
                   .then_inc(S["v_stored"], 1)

            def attend2(qt):
                n = P * (qt + 1)
                soften(n, P ** -0.5)
                act.wait_ge(S["p_turned"], c.up("p_turned"))
                act.activation(pT2[:, 0:2 * (qt + 1), :], ps[:, 6, 0:2 * n].rearrange("p (w n) -> p w n", n=P),
                               ACT.Copy).then_inc(S["pT_ready"], 1)

            u0 = w_in.u0
            c.n["roped"] = 2
            split_to(u0 + 5)
            for g in range(11):
                split_to(u0 + 2 * g + 7)
                if g == 1:
                    act.wait_ge(S["roped"], 2)
                    for qt in range(2):
                        for _ in range(2):
                            e = c.up("idx_scored")
                            n = P * (qt + 1)
                            act.wait_ge(S["idx_scored"], e)
                            if e > 2:
                                act.wait_ge(S["idx_used"], e - 2)
                            act.activation((work1, work2)[(e - 1) % 2][:, :, 0:n], ps[:, 4:8, 0:n], ACT.Relu)\
                               .then_inc(S["idx_relu"], 1)
                elif g == 2:
                    act.wait_ge(S["idx_used"], 4)
                    qk2_job(0, "q_a")
                elif g == 3:
                    qk2_job(1, "k_a")
                elif g == 4:
                    store_v2(0, v_a)
                elif g == 5:
                    qk2_job(2, "q_b")
                    attend2(0)
                    attend2(1)
                elif g == 6:
                    qk2_job(3, "k_b")
                    attend2(0)
                    attend2(1)
                elif g == 7:
                    store_v2(1, v_b)
                elif g in (8, 9):
                    attend2(0)
                    attend2(1)
            for which in range(2):
                heads = slice(4 * which, 4 * which + 4)
                act.wait_ge(S["o_evicted"], 16 + 2 * which + 2)
                act.activation(o2_hi[:, heads, :], f[:, heads, 0:SEQ], ACT.Copy).then_inc(S["a_hi_ready"], 1)
            for k in range(4):
                act.wait_ge(S["tile_evicted"], w_in.evicted(w_in.t0 + GROUP * (k + 9)))
                act.activation(gates[:, 4 * k:4 * k + 4, :], gates[:, 4 * k:4 * k + 4, :], ACT.Sigmoid)\
                   .then_inc(S["gate_ready"], 1)
            dsa, moba = stages["br_dsa"], stages["br_moba"]
            split_to(end_of(dsa) + 3)
            split_to(end_of(moba) + 3)
            for m in range(0, 8, 2):
                x = (pair_a, pair_b)[m // 2 % 2][:, :, 0:SEQ]
                act.wait_ge(S["act_in_ready"], I0["br"] + m // 2 + 1)
                act.activation(z_hi[:, m:m + 2, :], x, ACT.Copy).then_inc(S["a_hi_ready"], 1)
            up4 = stages["up", 4]
            tail(stages["w_out"], up4, None, full=True, normed=False, bank=side_bank(up4))
            split_to(up4.u0 + 5)
            gate_up(4)
            split_to(n_units)
            n_h = c.now("h_ready")
            for m in range(KT):
                act.wait_ge(S["h_ready"], n_h + m + 1)
                act.dma_start(out[:, m, :], h[:, m, META:TOK]).then_inc(out_stored, 16)


def _constants():
    f32 = np.float32
    con = np.zeros((P, C_ALL), f32)
    con[:, C_ONES:C_ONES + P] = 1
    con[:, C_IDENT:C_IDENT + P] = np.eye(P)

    def swap(block, half):
        r = np.zeros((P, P), f32)
        for b in range(0, P, block):
            for i in range(half):
                r[b + half + i, b + i] = -1
                r[b + i, b + half + i] = 1
        return r

    con[:, C_ROT1:C_ROT1 + P] = swap(64, 8)
    con[:, C_ROT2:C_ROT2 + P] = swap(128, 64)
    con[:, C_ROTI:C_ROTI + P] = swap(64, 32)

    def table(tokens, dim, theta, block):
        half = dim // 2
        inv = (f32(theta) ** (-np.arange(0, dim, 2, dtype=f32) / f32(dim))).astype(f32)
        ang = (np.arange(tokens, dtype=f32)[None, :] * inv[:, None]).astype(f32)
        cos, sin = np.ones((P, tokens), f32), np.zeros((P, tokens), f32)
        for b in range(0, P, block):
            for part in range(2):
                cos[b + part * half:b + (part + 1) * half] = np.cos(ang)
                sin[b + part * half:b + (part + 1) * half] = np.sin(ang)
        return cos, sin

    con[:, C_COS1:C_COS1 + TOK], con[:, C_SIN1:C_SIN1 + TOK] = table(TOK, 16, 500000.0, 64)
    con[:, C_MASK:] = np.where(np.arange(TOK)[None, :] <= META + P + np.arange(P)[:, None], 0, NEG)
    tables2 = np.stack([*table(SEQ, 128, 10000.0, 128), *table(SEQ, 64, 10000.0, 64)], axis=1)
    return con, tables2.astype(f32)


def _layout(a):
    def grouped(w):
        k, m = w.shape
        return w.reshape(k // 512, 4, P, m // 512, 512).transpose(3, 0, 2, 1, 4).reshape(-1, P, UNIT)

    def pairs(w, starts):
        return np.concatenate([w[:, s:s + 256] for s in starts], axis=1)

    def k_outer(w):
        return w.reshape(-1, 2, P, D).transpose(0, 2, 1, 3).reshape(-1, P, UNIT)

    def gate_up(w):
        return grouped(pairs(w, [s for g in range(FT // 2) for s in (256 * g, FF + 256 * g)]))

    units = []
    for i in range(2):
        units += [gate_up(a["ffn1_w_gu"][i]), k_outer(a["ffn1_w_down"][i])]
        if i == 0:
            w = a["conv_w_in"][0]
            units += [grouped(np.concatenate([pairs(w, [s for g in range(4) for s in (D + 256 * g, 2 * D + 256 * g)]),
                                              w[:, 0:D]], axis=1)),
                      k_outer(a["conv_w_out"][0])]
        else:
            w = a["attn_w_qkv"][0]
            v = 2 * D
            units += [grouped(pairs(w, [0, D, v, v + 256, 256, D + 256, 512, D + 512, v + 512, v + 768, 768, D + 768])),
                      k_outer(a["attn_w_o"][0])]
        units += [gate_up(a["ffn2_w_gu"][i]), k_outer(a["ffn2_w_down"][i])]
    w = a["w_in_2"][0]
    key = w[:, 2048:2112]
    small = np.concatenate([key, key, w[:, 2112:2120], np.zeros((D, 120), np.float32)], axis=1)
    units.append(small.reshape(KT, P, 256).transpose(1, 0, 2).reshape(1, P, UNIT))
    units.append(grouped(np.concatenate([w[:, 1536:2048], w[:, 0:1536], w[:, 2120:]], axis=1)))
    units += [k_outer(a["w_br_dsa_2"][0]), k_outer(a["w_br_moba_2"][0]), k_outer(a["w_out_2"][0]),
              gate_up(a["w_gate_up_2"][0]), k_outer(a["w_down_2"][0])]

    mod_units = a["w_mod_2"][0].reshape(P, 8, MOD_UNITS, 256).transpose(2, 0, 1, 3)
    x = np.concatenate([a["meta_tokens"], a["x"][0]], axis=0).reshape(TOK, KT, P).transpose(2, 1, 0)

    def columns(v):
        return v.reshape(-1, P).T

    cols = []
    for i in range(2):
        for name in ("ln_ffn1", "ln_mix", "ln_ffn2"):
            cols += [columns(a[name][i, 0]), columns(a[name][i, 1])]
    cols += [columns(a["conv_w"][0]), columns(a["b_mod_2"][0]), columns(a["g_mix_norm_2"][0]),
             columns(a["g_ffn_norm_2"][0])]
    cols += [columns(a[n][0]) for n in ("g_q_dsa_2", "g_k_dsa_2", "g_q_moba_2", "g_k_moba_2", "attn_subln_g")]
    cols.append(a["c_2"][0].reshape(P, 8))
    cols.append(np.concatenate([a["attn_lambda"][0].T, np.zeros((P - 64, 4), np.float32)], axis=0))
    return np.concatenate(units, axis=0), mod_units, x, np.concatenate(cols, axis=1)


def kernel(**inputs):
    import concourse.bacc as bacc
    from concourse.bass_utils import run_bass_kernel_spmd

    a = {name: np.asarray(value) for name, value in inputs.items()}
    names = ("w_units", "mod_units", "x_in", "vectors", "constants", "tables2")
    arrays = dict(zip(names, (*_layout(a), *_constants())))
    arrays = {name: np.ascontiguousarray(v) for name, v in arrays.items()}
    nc = bacc.Bacc("TRN2", target_bir_lowering=False, num_devices=1)
    args = [nc.dram_tensor(name, v.shape, F32, kind="ExternalInput").ap() for name, v in arrays.items()]
    out = nc.dram_tensor("out", (P, KT, SEQ), F32, kind="ExternalOutput").ap()
    build(nc, *args, out)
    r = run_bass_kernel_spmd(nc, [arrays], core_ids=[0])
    got = r.results[0]["out"]
    return np.ascontiguousarray(got.transpose(2, 1, 0)).reshape(1, SEQ, D)
```

```python
import math
from contextlib import ExitStack

import numpy as np

import concourse.bass as bass
from concourse import mybir

F32, F32R, BF16 = mybir.dt.float32, mybir.dt.float32r, mybir.dt.bfloat16
ACT = mybir.ActivationFunctionType
ALU = mybir.AluOpType
AX = mybir.AxisListType

P = 128
D = 1024
KT = D // P
SEQ, META = 256, 16
TOK = SEQ + META
FF = 2816
FT = FF // P
UNIT = 2048
RING = 4
GROUP = 4
NEG = -1e30
TAKEN = -3e38
LAMBDA_INIT = 0.8 - 0.6 * math.exp(-0.3)
EPS, SUBLN_EPS = 1e-6, 1e-5
HEADS1, HEADS2, IDX_HEADS = 8, 4, 8
TOPK = min(256, SEQ // 4)
IDX_SCALE = (IDX_HEADS ** -0.5) * (64 ** -0.5)
MOD_UNITS = 24
MOD_PARTS = 4
MOD_PER = MOD_UNITS // MOD_PARTS

V_LN = 0
V_CONV = V_LN + 96
V_BMOD = V_CONV + 24
V_GMIX = V_BMOD + 48
V_GFFN = V_GMIX + 8
V_GQK = V_GFFN + 8
V_SUB = V_GQK + 4
V_C = V_SUB + 1
V_LAM = V_C + 8
V_ALL = V_LAM + 4
C_ONES, C_IDENT, C_ROT1, C_ROT2, C_ROTI, C_COS1, C_SIN1, C_MASK = 0, 128, 256, 384, 512, 640, 912, 1184
C_ALL = C_MASK + TOK


class Stage:

    def __init__(self, plan, name, units, tiles, tokens, k_outer, quad_banks=False, tail=False):
        self.name, self.units, self.tiles, self.T = name, units, tiles, tokens
        self.u0, self.t0 = plan["u"], plan["t"]
        self.tail = tail
        self.e_shift = plan["tails"]
        if tail:
            plan["tails"] += tiles
        self.quad = quad_banks
        self.after_tail = plan["after_tail"]
        self.first_fresh = plan["quad"] or quad_banks
        plan["after_tail"] = tail
        plan["u"] += units
        plan["t"] += tiles
        plan["quad"] = quad_banks
        done = self.t0
        for n in range(units):
            if k_outer:
                last = n == units - 1
            elif name == "w_in":
                last = n % 2 == 0
            else:
                last = n % 2 == 1
            if last:
                done += 8 if k_outer else GROUP
                plan["used"].append(("tile_done", done))
            else:
                plan["mid"] += 1
                plan["used"].append(("weights_used", plan["mid"]))

    def evicted(self, t):
        return t - self.e_shift

    def bank(self, t):
        return (t - self.t0) % 4 if self.quad else t % 8


def build(nc, w_units, mod_units, x_in, vectors, constants, tables2, out):
    ctx = ExitStack()
    with ctx:
        def sb(name, shape, dt=F32):
            return ctx.enter_context(nc.sbuf_tensor(name, shape, dt))

        def sem(name):
            return ctx.enter_context(nc.semaphore(name))

        plan = {"u": 0, "t": 0, "quad": False, "mid": 0, "used": [], "tails": 0, "after_tail": True}
        stages = {}

        def stage(name, key, units, tiles, tokens, k_outer, quad=False):
            stages[key] = Stage(plan, name, units, tiles, tokens, k_outer, quad,
                                tail=k_outer and key not in ("br_dsa", "br_moba"))

        for layer in range(2):
            stage("gate_up", ("up", 2 * layer), 22, 44, TOK, False)
            stage("down", ("down", 2 * layer), 11, 8, TOK, True)
            if layer == 0:
                stage("conv_in", "conv_in", 12, 24, TOK, False)
                stage("proj", "conv_out", 4, 8, TOK, True)
                stage("gate_up", ("up", 1), 22, 44, TOK, False)
                stage("down", ("down", 1), 11, 8, TOK, True)
            else:
                stage("qkv", "qkv", 12, 24, TOK, False, True)
                stage("proj", "attn_out", 4, 8, SEQ, True)
                stage("gate_up", ("up", 3), 22, 44, SEQ, False)
                stage("down", ("down", 3), 11, 8, SEQ, True)
        stage("w_in", "w_in", 23, 48, SEQ, False, True)
        stage("proj", "br_dsa", 2, 8, SEQ, True)
        stage("proj", "br_moba", 2, 8, SEQ, True)
        stage("proj", "w_out", 4, 8, SEQ, True)
        stage("gate_up", ("up", 4), 22, 44, SEQ, False)
        stage("down", ("down", 4), 11, 8, SEQ, True)
        n_units = plan["u"]
        assert n_units % RING == 0
        S0, I0, E0, A0, X0 = {}, {}, {}, {}, {}
        silus = given = events = a_tiles = x_tiles = 0
        for key, n_silu, n_event, n_tiles, x in (
                (("up", 0), 11, 11, FT, 8), ("conv_in", 0, 4, 8, 8), (("up", 1), 11, 11, FT, 8),
                (("up", 2), 11, 11, FT, 8), ("qkv", 0, 4, 8, 8), (("up", 3), 11, 11, FT, 8),
                ("w_in", 0, 2, 8, 8), ("br", 0, 4, 8, 0), (("up", 4), 11, 11, FT, 8)):
            S0[key], I0[key], E0[key], A0[key], X0[key] = silus, given, events, a_tiles, x_tiles
            given += n_event if key != "w_in" else 0
            silus, events, a_tiles, x_tiles = silus + n_silu, events + n_event, a_tiles + n_tiles, x_tiles + x
        used_by = plan["used"]

        a_bytes = FT * TOK * 4
        mod_bytes = 8 * 256 * 4
        acc_bytes = MOD_PER * 256 * 4
        arena_at = -(-nc.sbuf_base // 32) * 32
        sb("arena", [P, (2 * a_bytes + mod_bytes + acc_bytes + 64) // 4])

        def at(name, offset, shape, dt=F32):
            return nc.alloc_sbuf_tensor_at(name, shape, dt, offset=arena_at + offset)

        a_hi = at("a_hi", 0, [P, FT, TOK], F32R)
        a_lo = at("a_lo", a_bytes, [P, FT, TOK], F32R)
        mod_w = at("mod_w", 2 * a_bytes, [P, 8, 256])
        mod_acc = at("mod_acc", 2 * a_bytes + mod_bytes, [P, MOD_PER, 256])
        free1, free2 = 8 * TOK * 4, a_bytes + 8 * TOK * 4
        v1_T = at("v1_T", free1, [P, 4, TOK])
        qk1 = at("qk1", free1 + 4 * TOK * 4, [P, 2, 4, TOK])
        pT1 = at("pT1", free1 + 12 * TOK * 4, [P, 3, P])
        v1 = at("v1", free2, [P, 3, HEADS1, P])
        o1 = at("o1", 2 * a_bytes, [P, HEADS1, SEQ])
        KB = 1024
        qkv2 = {n: at(n, i * 4 * KB, [P, 4, SEQ]) for i, n in enumerate(("q_a", "k_a"))}
        v_a = at("v_a", 8 * KB, [P, 2, HEADS2, P])
        qkv2["q_b"] = at("q_b", 16 * KB, [P, 4, SEQ])
        qkv2["k_b"] = at("k_b", 20 * KB, [P, 4, SEQ])
        v_b = at("v_b", 24 * KB, [P, 2, HEADS2, P])
        v2_T = at("v2_T", 12 * KB, [P, 4, SEQ])
        qi = at("qi", 28 * KB, [P, 4, SEQ])
        gates = at("gates", 32 * KB, [P, 16, SEQ])
        work1 = at("work1", 48 * KB, [P, 4, SEQ])
        work2 = at("work2", 52 * KB, [P, 4, SEQ])
        tab = at("tab", 56 * KB, [P, 4, SEQ])
        o2_hi = at("o2_hi", 0, [P, 8, SEQ], F32R)
        o2_lo = at("o2_lo", 8 * KB, [P, 8, SEQ], F32R)
        z_hi = at("z_hi", 16 * KB, [P, 8, SEQ], F32R)
        z_lo = at("z_lo", 24 * KB, [P, 8, SEQ], F32R)

        raw = sb("raw_weights", [P, RING, UNIT])
        w_hi = sb("w_hi", [P, RING, UNIT], F32R)
        w_lo = sb("w_lo", [P, RING, UNIT], F32R)
        h = sb("h", [P, KT, TOK])
        x_hi = sb("x_hi", [P, KT, TOK], F32R)
        x_lo = sb("x_lo", [P, KT, TOK], F32R)
        f = sb("f", [P, KT, TOK])
        pair_a = sb("pair_a", [P, 2, TOK])
        pair_b = sb("pair_b", [P, 2, TOK])
        norm_at = -(-nc.sbuf_base // 32) * 32
        sb("norm_area", [P, 5 * TOK])

        def norm_part(name, offset, shape, dt=F32):
            return nc.alloc_sbuf_tensor_at(name, shape, dt, offset=norm_at + offset)

        sq = norm_part("sq", 0, [P, 2, TOK])
        sq_sum = norm_part("sq_sum", 8 * TOK, [P, TOK])
        std_col = norm_part("std_col", 12 * TOK, [P, 4])
        r_col = norm_part("r_col", 12 * TOK + 32, [P, 4])
        rstd = norm_part("rstd", 16 * TOK, [P, TOK])
        ki = norm_part("ki", 0, [P, SEQ])
        wi_T = norm_part("wi_T", KB, [P, SEQ])
        score = norm_part("score", 2 * KB, [P, 2, SEQ])
        pT2 = norm_part("pT2", 2 * KB, [P, 4, P])
        sel = norm_part("sel", 4 * KB, [P, 2, SEQ], BF16)
        vec = sb("vec", [P, V_ALL])
        g_out = sb("g_out", [P, 49])
        mod = sb("mod", [P, 48])
        gain2 = sb("gain2", [P, 16])
        silu_c = sb("silu_c", [P, KT])
        eps = sb("eps", [P, 3])
        small = sb("small", [P, 4, 8])
        lam = sb("lam", [P, 8])
        head_col = sb("head_col", [P, 16])
        con = sb("con", [P, C_MASK])
        mask = sb("mask", [P, TOK], BF16)
        ident_b = sb("ident_b", [P, P], BF16)
        wi = sb("wi", [P, 2, 8])
        top8 = sb("top8", [P, 8])
        ones, ident = con[:, C_ONES:C_ONES + P], con[:, C_IDENT:C_IDENT + P]
        rot1, rot2, rot_i = (con[:, c:c + P] for c in (C_ROT1, C_ROT2, C_ROTI))
        cos1, sin1 = con[:, C_COS1:C_COS1 + TOK], con[:, C_SIN1:C_SIN1 + TOK]
        ps = ctx.enter_context(nc.psum_tensor("ps", [P, 8, 512], F32))

        raw_loaded = [sem(f"raw_loaded{i}") for i in range(RING)]
        h_loaded, vectors_loaded, constants_loaded = sem("h_loaded"), sem("vectors_loaded"), sem("constants_loaded")
        mask_loaded, tables_loaded = sem("mask_loaded"), sem("tables_loaded")
        mod_loaded, out_stored = sem("mod_loaded"), sem("out_stored")
        S = {n: sem(n) for n in (
            "hi_ready", "lo_ready", "weights_used", "tile_done", "tile_evicted",
            "x_hi_ready", "x_ready", "act_in_ready", "a_hi_ready", "a_ready", "silu_done",
            "sq_ready", "sq_used", "sumsq_ready", "stats_done", "std_ready", "rstd_columns", "rstd_spread", "rstd_kept", "f_ready",
            "h_ready", "full_ready", "head_columns", "head_spread",
            "silu_c_ready", "mod_used", "mod_psum", "mod_evicted", "lam_in", "lam_sums", "lam_exp",
            "turned", "v_stored", "rotated", "rotation_read", "normed_heads", "roped", "qk_ready",
            "head_sq", "head_sums", "head_std",
            "scored", "max_ready", "probs_ready", "weights_ready", "p_turned", "pT_ready", "pv_done", "o_evicted",
            "idx_scored", "idx_relu", "idx_used", "sel_ready", "gate_ready",
            "vec_chain")}

        class Count:

            def __init__(self):
                self.n = {}

            def up(self, name, k=1):
                self.n[name] = self.n.get(name, 0) + k
                return self.n[name]

            def now(self, name):
                return self.n.get(name, 0)

        QK_GROUP, V_GROUP = (0, 2, 3, 5), (1, 4)
        V_GROUP2 = (1, 4)

        def end_of(st):
            return st.u0 + st.units

        block = ctx.enter_context(nc.Block())

        @block.sync
        def _(sp):
            sp.dma_start(vec[:, :], vectors).then_inc(vectors_loaded, 16)
            sp.dma_start(h[:, :, :], x_in).then_inc(h_loaded, 16)
            for s in range(RING):
                sp.dma_start(raw[:, s, :], w_units[s]).then_inc(raw_loaded[s], 16)
            with sp.Fori(1, n_units // RING) as i:
                for s in range(RING):
                    sp.wait_ge(S["lo_ready"], RING * i + (s - RING + 1))
                    sp.dma_start(raw[:, s, :], w_units[RING * i + s]).then_inc(raw_loaded[s], 16)
            sp.wait_ge(out_stored, 16 * KT)

        @block.gpsimd
        def _(gp):
            gp.wait_ge(raw_loaded[0], 16)
            gp.dma_start(con[:, :], constants[:, 0:C_MASK]).then_inc(constants_loaded, 16)
            gp.dma_start(f[:, 0, :], constants[:, C_MASK:C_ALL]).then_inc(mask_loaded, 16)
            for u in range(MOD_UNITS):
                if u:
                    gp.wait_ge(S["mod_used"], u)
                if u == 3 * MOD_PER:
                    gp.wait_ge(S["a_ready"], A0["up", 3])
                gp.dma_start(mod_w[:, :, :], mod_units[u]).then_inc(mod_loaded, 16)
            gp.wait_ge(S["mod_evicted"], MOD_PARTS)
            gp.dma_start(tab[:, :, :], tables2).then_inc(tables_loaded, 16)

        @block.tensor
        def _(pe):
            c = Count()

            def three_pass(dst, slot, col, hi, lo, start, stop):
                wh, wl = w_hi[:, slot, col:col + P], w_lo[:, slot, col:col + P]
                pe.matmul(dst, wh, hi, start=start, stop=False)
                pe.matmul(dst, wh, lo, start=False, stop=False)
                return pe.matmul(dst, wl, hi, start=False, stop=stop)

            def wait_bank(st, t, shift=0):
                n = st.evicted(t - (3 if st.quad else 7))
                if t < st.t0 + (4 if st.quad else 8):
                    if st.after_tail:
                        return
                    if st.first_fresh:
                        n = st.evicted(st.t0)
                pe.wait_ge(S["tile_evicted"], n + shift)

            def group(st, g, xs, i=0, x_base=None, bank_busy=None, between=None):
                for half in range(2):
                    u = st.u0 + 2 * g + half + (1 if st.name == "w_in" else 0)
                    pe.wait_ge(S["lo_ready"], u + 1 + 4 * i)
                    for kk in range(4):
                        k = 4 * half + kk
                        if x_base is not None:
                            pe.wait_ge(S["x_ready"], x_base + k + 1)
                        for m in range(GROUP):
                            t = st.t0 + GROUP * g + m + (4 if st.name == "w_in" else 0)
                            if k == 0:
                                wait_bank(st, t, 8 * i)
                                if bank_busy is not None:
                                    bank_busy(m)
                            ins = three_pass(ps[:, st.bank(t), 0:st.T], u % RING, (kk * GROUP + m) * P,
                                             xs[0][:, k, 0:st.T], xs[1][:, k, 0:st.T], k == 0, k == KT - 1)
                            if k == KT - 1:
                                ins.then_inc(S["tile_done"], 1)
                        if between is not None:
                            for job in between.get(k, ()):
                                job()
                    if half == 0:
                        ins.then_inc(S["weights_used"], 1)

            def slab(st, xs, a_base, n, kk, tiles):
                u, k = st.u0 + n, 2 * n + kk
                pe.wait_ge(S["lo_ready"], u + 1)
                pe.wait_ge(S["a_ready"], a_base + k + 1)
                for m in tiles:
                    three_pass(ps[:, st.bank(st.t0 + m), 0:st.T], u % RING, (kk * 8 + m) * P,
                               xs[0][:, k, 0:st.T], xs[1][:, k, 0:st.T], k == 0, False)

            def k_outer(st, xs, a_base, done=(), done_units=0, busy=None):
                for n in range(st.units):
                    u = st.u0 + n
                    pe.wait_ge(S["lo_ready"], u + 1)
                    last = n == st.units - 1
                    order = [(kk, m) for kk in range(2) for m in range(8)]
                    if last:
                        order = [(kk, m) for m in range(8) for kk in range(2)]
                    if n < done_units:
                        order = [(kk, m) for kk, m in order if m not in done]
                    for kk, m in order:
                        k = 2 * n + kk
                        if m == 0:
                            pe.wait_ge(S["a_ready"], a_base + k + 1)
                        if k == 0:
                            wait_bank(st, st.t0 + m)
                            if busy is not None and m in busy:
                                busy[m]()
                        ins = three_pass(ps[:, st.bank(st.t0 + m), 0:st.T], u % RING, (kk * 8 + m) * P,
                                         xs[0][:, k, 0:st.T], xs[1][:, k, 0:st.T], k == 0, k == 2 * st.units - 1)
                        if k == 2 * st.units - 1:
                            ins.then_inc(S["tile_done"], 1)
                    if not last:
                        ins.then_inc(S["weights_used"], 1)

            def starts(T):
                return [0, P] if T == 2 * P else [0, P, T - P]

            def column_sums(T, bank):
                pe.wait_ge(S["sumsq_ready"], c.up("sumsq_ready"))
                for n, at_token in enumerate(starts(T)):
                    ins = pe.matmul(ps[:, bank, n:n + 1], sq_sum[:, at_token:at_token + P], ones[:, 0:1],
                                    start=True, stop=True)
                ins.then_inc(S["stats_done"], 1)

            def spread(T, bank):
                pe.wait_ge(S["rstd_columns"], c.up("rstd_columns"))
                for n, at_token in enumerate(starts(T)):
                    ins = pe.matmul(ps[:, bank, at_token:at_token + P], r_col[:, n:n + 1].broadcast_to([P, P]), ident,
                                    start=True, stop=True)
                ins.then_inc(S["rstd_spread"], 1)

            def stats(T, bank, evict=True):
                if evict:
                    pe.wait_ge(S["f_ready"], c.up("f_ready", 8))
                column_sums(T, bank)
                spread(T, bank)

            def side_bank(st):
                return 7 if st.quad else st.bank(st.t0 + 7)

            def mod_bank(st):
                return 6 if st.quad else st.bank(st.t0 + 6)

            def mod_sums(part, bank):
                pe.wait_ge(S["mod_used"], MOD_PER * (part + 1))
                for n in range(2 * MOD_PER):
                    ins = pe.matmul(ps[:, bank, 288 + n:289 + n], mod_acc[:, n // 2, (n % 2) * P:(n % 2) * P + P],
                                    ones[:, 0:1], start=True, stop=True)
                ins.then_inc(S["mod_psum"], 1)

            def wait_side(part, m=None):
                if part is not None and m in (None, 2):
                    pe.wait_ge(S["mod_evicted"], part + 1)
                if m in (None, 3):
                    pe.wait_ge(S["rstd_kept"], c.now("rstd_kept"))

            def lambda_sums():
                pe.wait_ge(S["lam_in"], 1)
                pe.matmul(ps[:, 7, 0:2], ones, lam[:, 0:2], start=True, stop=True).then_inc(S["lam_sums"], 1)

            def group_0(st, x_base, part=None):
                between = {KT - 2: [lambda: column_sums(st.T, side_bank(st))]}
                if part is not None:
                    between[3] = [lambda: mod_sums(part, mod_bank(st))]
                if st.u0 == 0:
                    between[5] = [lambda: lambda_sums()]
                    between[6] = [lambda: pe.wait_ge(S["lam_exp"], 1)] + between[6]
                group(st, 0, (x_hi, x_lo), x_base=x_base, between=between)

            def first_groups(st, x_base, part=None):
                bank = side_bank(st)
                group_0(st, x_base, part)
                spread(st.T, bank)
                c.up("rstd_kept")
                group(st, 1, (x_hi, x_lo), bank_busy=lambda m: wait_side(part, m))

            def gate_up(n, x_base, part=None, deferred=True):
                st = stages["up", n]
                if deferred:
                    first_groups(st, x_base, part)
                else:
                    group(st, 0, (x_hi, x_lo), x_base=x_base)
                    group(st, 1, (x_hi, x_lo), bank_busy=lambda m: wait_side(part, m))
                with pe.Fori(0, 4) as i:
                    group(st, 2, (x_hi, x_lo), i)
                    group(st, 3, (x_hi, x_lo), i)
                group(st, 10, (x_hi, x_lo))

            gate_up(0, 0)
            k_outer(stages["down", 0], (a_hi, a_lo), A0["up", 0])
            conv = stages["conv_in"]
            stats(TOK, side_bank(conv))
            first_groups(conv, X0["conv_in"], 0)
            with pe.Fori(0, 2) as i:
                group(conv, 2, (x_hi, x_lo), i)
                group(conv, 3, (x_hi, x_lo), i)
            k_outer(stages["conv_out"], (a_hi, a_lo), A0["conv_in"])
            stats(TOK, side_bank(stages["up", 1]))
            gate_up(1, X0["up", 1])
            k_outer(stages["down", 1], (a_hi, a_lo), A0["up", 1])
            stats(TOK, side_bank(stages["up", 2]))
            gate_up(2, X0["up", 2], 1)
            k_outer(stages["down", 2], (a_hi, a_lo), A0["up", 2])
            qkv = stages["qkv"]
            stats(TOK, 7)

            def bank7_free():
                for name, n in (("v_stored", c.now("turned")), ("rotation_read", c.now("rotated")),
                                ("head_std", c.now("head_sums")), ("act_in_ready", I0["qkv"] + c.now("head_spread"))):
                    if n:
                        pe.wait_ge(S[name], n)

            def turn(g, w):
                at_token = (0, META, META + P)[w]
                bank7_free()
                pe.wait_ge(S["tile_evicted"], qkv.evicted(qkv.t0 + GROUP * (V_GROUP[g] + 1)))
                for m in range(4):
                    ins = pe.transpose(ps[:, 7, m * P:(m + 1) * P], v1_T[:, m, at_token:at_token + P], ident)
                ins.then_inc(S["turned"], 1)
                c.up("turned")

            def rot(g, m, bank=7):
                if bank == 7:
                    bank7_free()
                else:
                    pe.wait_ge(S["probs_ready"], 2 * c.now("scored"))
                pe.wait_ge(S["tile_evicted"], qkv.evicted(qkv.t0 + GROUP * (QK_GROUP[g] + 1)))
                pe.matmul(ps[:, bank, 0:TOK], rot1, qk1[:, g % 2, m, :], start=True, stop=True).then_inc(S["rotated"], 1)
                c.up("rotated")

            def scores(s):
                g, j, qt = s // 4, s // 2 % 2, s % 2
                n = META + P * (qt + 1)
                pe.wait_ge(S["qk_ready"], 4 * g + 2 + 2 * j)
                if s:
                    pe.wait_ge(S["probs_ready"], 2 * s)
                for comp in range(2):
                    rows = slice(64 * comp, 64 * comp + 64)
                    at_q = META + P * qt
                    pe.matmul(ps[:, 4 + comp, 0:n], qk1[rows, g % 2, j, at_q:at_q + P],
                              qk1[rows, g % 2, 2 + j, 0:n], start=True, stop=False)
                    ins = pe.matmul(ps[:, 4 + comp, 0:n], ident_b[:, :], mask[:, P - P * qt:P - P * qt + n],
                                    start=False, stop=True)
                ins.then_inc(S["scored"], 1)
                c.up("scored")

            def turn_p(s):
                pe.wait_ge(S["weights_ready"], c.up("weights_ready"))
                if s:
                    pe.wait_ge(S["head_sq"], s)
                for w, at_key in enumerate((0, META, META + P)[:s % 2 + 2]):
                    ins = pe.transpose(ps[:, 6, w * P:(w + 1) * P], pair_b[:, 0, at_key:at_key + P], ident)
                ins.then_inc(S["p_turned"], 1)
                c.up("p_turned")

            def values(s):
                pe.wait_ge(S["pT_ready"], s + 1)
                n = s % 2 + 2
                pe.wait_ge(S["v_stored"], 3 * (s // 8) + n)
                for w in range(n):
                    rows = slice(0, META if w == 0 else P)
                    ins = pe.matmul(ps[:, 6, 3 * P:4 * P], v1[rows, w, s // 2, :], pT1[rows, w, :],
                                    start=w == 0, stop=w == n - 1)
                ins.then_inc(S["pv_done"], 1)
                c.up("pv_done")

            def head_sums(squares, bank, columns=range(8)):
                for n in columns:
                    ins = pe.matmul(ps[:, bank, n:n + 1], squares[:, n // 2, (n % 2) * P:(n % 2) * P + P], ones[:, 0:1],
                                    start=True, stop=True)
                if columns[-1] == 7:
                    ins.then_inc(S["head_sums"], 1)
                    c.up("head_sums")

            def head_spread(heads, banks):
                pe.wait_ge(S["head_columns"], c.now("head_sums"))
                for h, bank in zip(heads, (b for b in banks for _ in range(2))):
                    for half in range(2):
                        n = 2 * h + half
                        ins = pe.matmul(ps[:, bank, (n % 4) * P:(n % 4) * P + P],
                                        head_col[:, 8 + n:9 + n].broadcast_to([P, P]), ident, start=True, stop=True)
                ins.then_inc(S["head_spread"], 1)
                c.up("head_spread")

            def subln_sums(half, columns=range(8)):
                bank7_free()
                pe.wait_ge(S["head_sq"], 8 * half + columns[-1] + 1)
                c.n["head_sq"] = 8 * half + columns[-1] + 1
                head_sums(f, 7, columns)

            def subln_spread(r, bank=7):
                if bank == 7:
                    bank7_free()
                head_spread((2 * r, 2 * r + 1), (bank,))

            xs = (x_hi, x_lo)
            group_0(qkv, X0["qkv"], 2)
            spread(TOK, 7)
            c.up("rstd_kept")
            group(qkv, 1, xs, between={
                0: [lambda: wait_side(2)],
                1: [lambda: rot(0, 0)], 2: [lambda: rot(0, 2)], 3: [lambda: rot(0, 1)], 4: [lambda: rot(0, 3)],
                7: [lambda: scores(0)]})
            group(qkv, 2, xs, between={
                0: [lambda: turn(0, 0)],
                1: [lambda: turn(0, 1), lambda: scores(1), lambda: turn_p(0)],
                2: [lambda: turn(0, 2), lambda: values(0)],
                3: [lambda: scores(2), lambda: turn_p(1)], 4: [lambda: values(1)],
                5: [lambda: scores(3), lambda: turn_p(2)], 6: [lambda: values(2)],
                7: [lambda: turn_p(3)]})
            group(qkv, 3, xs, between={
                0: [lambda: values(3)],
                1: [lambda: rot(1, 0)], 2: [lambda: rot(1, 2)], 3: [lambda: rot(1, 1)],
                4: [lambda: rot(1, 3), lambda: scores(4)],
                6: [lambda: scores(5), lambda: turn_p(4)], 7: [lambda: values(4)]})
            group(qkv, 4, xs, between={
                0: [lambda: scores(6), lambda: turn_p(5)],
                1: [lambda: values(5), lambda: rot(2, 0)],
                2: [lambda: scores(7), lambda: turn_p(6), lambda: rot(2, 2)],
                3: [lambda: values(6), lambda: rot(2, 1)],
                4: [lambda: turn_p(7), lambda: rot(2, 3)],
                5: [lambda: values(7)], 6: [lambda: subln_sums(0)], 7: [lambda: scores(8)]})
            group(qkv, 5, xs, between={
                0: [lambda: turn(1, 0)],
                1: [lambda: turn(1, 1), lambda: scores(9), lambda: turn_p(8)],
                2: [lambda: turn(1, 2), lambda: values(8)],
                3: [lambda: scores(10), lambda: turn_p(9)],
                4: [lambda: values(9), lambda: subln_spread(0)],
                5: [lambda: scores(11), lambda: turn_p(10)],
                6: [lambda: values(10), lambda: subln_spread(1)],
                7: [lambda: turn_p(11)]})
            rot(3, 0)
            rot(3, 2, bank=4)
            rot(3, 1, bank=5)
            values(11)
            rot(3, 3)
            pe.wait_ge(S["rotation_read"], 15)
            scores(12)
            attn_out = stages["attn_out"]
            early = [m for m in range(8) if attn_out.bank(attn_out.t0 + m) < 4]
            a_in = (a_hi, a_lo)

            def early_slab(k):
                slab(attn_out, a_in, A0["qkv"], k // 2, k % 2, early)

            pe.wait_ge(S["tile_evicted"], attn_out.evicted(attn_out.t0))
            for s in range(12, 16):
                if s < 15:
                    scores(s + 1)
                turn_p(s)
                if s == 15:
                    early_slab(1)
                values(s)
                if s == 13:
                    subln_sums(1, range(4))
                if s == 14:
                    subln_sums(1, range(4, 6))
                    early_slab(0)
            subln_sums(1, range(6, 8))
            early_slab(2)
            early_slab(3)
            subln_spread(0)
            subln_spread(1, bank=6)
            pe.wait_ge(S["o_evicted"], 16)
            last_reads = {m: (lambda n: lambda: pe.wait_ge(S["act_in_ready"], I0["qkv"] + n))(n)
                          for m in range(8) for bank, n in ((7, 3), (6, 4)) if attn_out.bank(attn_out.t0 + m) == bank}
            k_outer(attn_out, a_in, A0["qkv"], done=early, done_units=2, busy=last_reads)
            stats(SEQ, side_bank(stages["up", 3]))
            gate_up(3, X0["up", 3])
            k_outer(stages["down", 3], (a_hi, a_lo), A0["up", 3])
            w_in = stages["w_in"]
            stats(SEQ, 7)
            mod_sums(3, 6)
            stats(SEQ, 7, evict=False)

            def small_group():
                u = w_in.u0
                pe.wait_ge(S["lo_ready"], u + 1)
                for k in range(KT):
                    pe.wait_ge(S["x_ready"], X0["w_in"] + k + 1)
                    for m in range(2):
                        if k == 0:
                            wait_bank(w_in, w_in.t0 + m)
                        ins = three_pass(ps[:, m, 0:SEQ], u % RING, (k * 2 + m) * P, x_hi[:, k, 0:SEQ],
                                         x_lo[:, k, 0:SEQ], k == 0, k == KT - 1)
                        if k == KT - 1:
                            ins.then_inc(S["tile_done"], 2)

            def bank7_free():
                for name, n in (("v_stored", c.now("turned")), ("rotation_read", c.now("rotated")),
                                ("head_std", c.now("head_sums")), ("normed_heads", c.now("head_spread") - 4),
                                ("o_evicted", c.now("pv_done"))):
                    if n:
                        pe.wait_ge(S[name], n)

            def key_and_weights():
                pe.wait_ge(S["mod_evicted"], 4)
                bank7_free()
                pe.wait_ge(S["tile_evicted"], w_in.evicted(w_in.t0 + GROUP))
                pe.matmul(ps[:, 7, 0:SEQ], rot_i, ki[:, :], start=True, stop=True)
                for qt in range(2):
                    ins = pe.transpose(ps[:, 7, SEQ + qt * P:SEQ + (qt + 1) * P], wi_T[:, qt * P:(qt + 1) * P], ident)
                ins.then_inc(S["rotated"], 1)
                c.up("rotated")

            def rotate(matrix, src, r):
                bank7_free()
                pe.matmul(ps[:, 7, :], matrix, src[:, 2 * r:2 * r + 2, :], start=True, stop=True).then_inc(S["rotated"], 1)
                c.up("rotated")

            def rotate_qi(r):
                pe.wait_ge(S["tile_evicted"], w_in.evicted(w_in.t0 + GROUP * 2))
                rotate(rot_i, qi, r)

            def idx_scores(r):
                qt, heads = ((0, range(8)), (1, range(4)), (1, range(4, 8)))[r]
                n = P * (qt + 1)
                pe.wait_ge(S["roped"], 3)
                if r:
                    pe.wait_ge(S["idx_relu"], r)
                for b, i in enumerate(heads):
                    rows = slice(64 * (i % 2), 64 * (i % 2) + 64)
                    col = b // 2 * n
                    ins = pe.matmul(ps[:, 4 + i % 2, col:col + n],
                                    qi[rows, i // 2, P * qt:P * qt + P], ki[rows, 0:n], start=True, stop=True)
                ins.then_inc(S["idx_scored"], 1)

            def turn_v(g, kt):
                bank7_free()
                pe.wait_ge(S["tile_evicted"], w_in.evicted(w_in.t0 + GROUP * (V_GROUP2[g] + 2)))
                for m in range(4):
                    ins = pe.transpose(ps[:, 7, m * P:(m + 1) * P], v2_T[:, m, kt * P:(kt + 1) * P], ident)
                ins.then_inc(S["turned"], 1)
                c.up("turned")

            def qk_sums():
                bank7_free()
                pe.wait_ge(S["head_sq"], c.up("head_sq"))
                head_sums(f[:, 4:8, :], 7)

            def qk_spread(r):
                bank7_free()
                head_spread((2 * r, 2 * r + 1), (7,))

            def qk_rotate(name, r):
                pe.wait_ge(S["normed_heads"], c.now("head_spread") - 4 - 1 + r)
                rotate(rot2, qkv2[name], r)

            def scores2(s):
                which, pair, qt = s // 4, s // 2 % 2, s % 2
                q, k = (qkv2["q_a"], qkv2["k_a"]) if which == 0 else (qkv2["q_b"], qkv2["k_b"])
                n = P * (qt + 1)
                bias = sel[:, qt, 0:n] if which == 0 else mask[:, META + P - P * qt:META + P - P * qt + n]
                pe.wait_ge(S["roped"], 7 if which == 0 else 11)
                pe.wait_ge(S["sel_ready"], 2)
                pe.wait_ge(S["idx_relu"], 3)
                pe.wait_ge(S["probs_ready"], 2 * c.now("scored"))
                for comp in range(2):
                    head = 2 * pair + comp
                    pe.matmul(ps[:, 4 + comp, 0:n], q[:, head, P * qt:P * qt + P], k[:, head, 0:n],
                              start=True, stop=False)
                    ins = pe.matmul(ps[:, 4 + comp, 0:n], ident_b[:, :], bias, start=False, stop=True)
                ins.then_inc(S["scored"], 1)
                c.up("scored")

            def turn_p2(s):
                n = s % 2 + 1
                pe.wait_ge(S["weights_ready"], c.up("weights_ready"))
                pe.wait_ge(S["pT_ready"], c.now("p_turned"))
                for comp in range(2):
                    for kt in range(n):
                        col = (comp * n + kt) * P
                        ins = pe.transpose(ps[:, 6, col:col + P], pair_b[:, comp, kt * P:(kt + 1) * P], ident)
                ins.then_inc(S["p_turned"], 1)
                c.up("p_turned")

            def values2(s):
                which, pair, n = s // 4, s // 2 % 2, s % 2 + 1
                v = (v_a, v_b)[which]
                bank7_free()
                pe.wait_ge(S["v_stored"], 6 + 2 * which + n)
                pe.wait_ge(S["pT_ready"], 16 + s + 1)
                for comp in range(2):
                    for kt in range(n):
                        ins = pe.matmul(ps[:, 7, comp * P:comp * P + P], v[:, kt, 2 * pair + comp, :],
                                        pT2[:, comp * n + kt, :], start=kt == 0, stop=kt == n - 1)
                ins.then_inc(S["pv_done"], 1)
                c.up("pv_done")

            def qk_jobs(name):
                return {0: [lambda: qk_sums()], 2: [lambda: qk_spread(0)], 3: [lambda: qk_spread(1)],
                        4: [lambda: qk_rotate(name, 0)], 5: [lambda: qk_rotate(name, 1)]}

            small_group()
            group(w_in, 0, xs, between={1: [lambda: key_and_weights()]})
            group(w_in, 1, xs, between={
                0: [lambda: rotate_qi(0)], 1: [lambda: rotate_qi(1)],
                3: [lambda: idx_scores(0)], 6: [lambda: idx_scores(1)]})
            group(w_in, 2, xs, between={
                0: [lambda: turn_v(0, 0)], 1: [lambda: turn_v(0, 1)], 2: [lambda: idx_scores(2)]})
            group(w_in, 3, xs, between=qk_jobs("q_a"))
            group(w_in, 4, xs, between=qk_jobs("k_a"))
            group(w_in, 5, xs, between={
                0: [lambda: turn_v(1, 0)], 1: [lambda: turn_v(1, 1)],
                2: [lambda: scores2(0)],
                4: [lambda: scores2(1), lambda: turn_p2(0)], 5: [lambda: values2(0)],
                6: [lambda: scores2(2), lambda: turn_p2(1)], 7: [lambda: values2(1)]})
            group(w_in, 6, xs, between={
                0: [lambda: scores2(3), lambda: turn_p2(2)],
                1: [lambda: values2(2), lambda: qk_sums()],
                2: [lambda: turn_p2(3)],
                3: [lambda: values2(3), lambda: qk_spread(0)], 4: [lambda: qk_spread(1)],
                5: [lambda: qk_rotate("q_b", 0)], 6: [lambda: qk_rotate("q_b", 1)]})
            group(w_in, 7, xs, between=qk_jobs("k_b"))
            group(w_in, 8, xs, between={
                0: [lambda: scores2(4)],
                2: [lambda: scores2(5), lambda: turn_p2(4)], 3: [lambda: values2(4)],
                4: [lambda: scores2(6), lambda: turn_p2(5)], 5: [lambda: values2(5)],
                6: [lambda: scores2(7), lambda: turn_p2(6)], 7: [lambda: values2(6)]})
            group(w_in, 9, xs, between={1: [lambda: turn_p2(7)], 2: [lambda: values2(7)]})
            group(w_in, 10, xs)
            bank7_free()
            k_outer(stages["br_dsa"], (o2_hi, o2_lo), A0["w_in"])
            k_outer(stages["br_moba"], (o2_hi[:, 4:8, :], o2_lo[:, 4:8, :]), A0["w_in"] + 4)
            k_outer(stages["w_out"], (z_hi, z_lo), A0["br"])
            stats(SEQ, side_bank(stages["up", 4]), evict=False)
            gate_up(4, X0["up", 4], deferred=False)
            k_outer(stages["down", 4], (a_hi, a_lo), A0["up", 4])

        @block.vector
        def _(dve):
            c = Count()
            nxt = [0]

            def chain(ins):
                ins.then_inc(S["vec_chain"], 1)
                dve.wait_ge(S["vec_chain"], c.up("vec_chain"))

            def low_part(u, i=0):
                dve.wait_ge(S["hi_ready"], u + 1 + 4 * i)
                dve.tensor_tensor(w_lo[:, u % RING, :], raw[:, u % RING, :], w_hi[:, u % RING, :].bitcast(F32),
                                  ALU.subtract).then_inc(S["lo_ready"], 1)

            halves = [0]

            def split_to(u_end):
                while nxt[0] < min(u_end, n_units):
                    if halves[0]:
                        low_half()
                    else:
                        low_part(nxt[0])
                        nxt[0] += 1

            def low_half():
                u, half = nxt[0], halves[0]
                halves[0] = 1 - half
                cols = slice(half * UNIT // 2, (half + 1) * UNIT // 2)
                if half == 0:
                    dve.wait_ge(S["hi_ready"], u + 1)
                ins = dve.tensor_tensor(w_lo[:, u % RING, cols], raw[:, u % RING, cols],
                                        w_hi[:, u % RING, cols].bitcast(F32), ALU.subtract)
                if half == 1:
                    ins.then_inc(S["lo_ready"], 1)
                    nxt[0] += 1

            def bcast(row, T, n=2):
                return row[:, 0:T].unsqueeze(1).broadcast_to([P, n, T])

            def gated_eviction(n, g, i=0):
                st = stages["up", n]
                T, t, e = st.T, st.t0 + GROUP * g, E0["up", n] + g
                b = t % 8
                gate, up = pair_a[:, :, 0:T], pair_b[:, :, 0:T]
                if A0["up", n] + g > 0:
                    dve.wait_ge(S["a_ready"], A0["up", n] + 2 * g + 4 * i)
                dve.wait_ge(S["tile_done"], t + 2 + 8 * i)
                if n < 4:
                    dve.tensor_tensor(gate, ps[:, b:b + 2, 0:T], bcast(rstd, T), ALU.mult).then_inc(S["tile_evicted"], 2)
                else:
                    dve.tensor_copy(gate, ps[:, b:b + 2, 0:T]).then_inc(S["tile_evicted"], 2)
                dve.wait_ge(S["tile_done"], t + 4 + 8 * i)
                if n < 4:
                    dve.tensor_tensor(up, ps[:, b + 2:b + 4, 0:T], bcast(rstd, T), ALU.mult).then_inc(S["tile_evicted"], 2)
                else:
                    dve.tensor_copy(up, ps[:, b + 2:b + 4, 0:T]).then_inc(S["tile_evicted"], 2)
                dve.wait_ge(S["tile_evicted"], st.evicted(t + 4) + 8 * i)
                dve.wait_ge(S["silu_done"], S0["up", n] + g + 1 + 2 * i)
                dve.tensor_tensor(up, gate, up, ALU.mult).then_inc(S["act_in_ready"], 1)
                dve.wait_ge(S["a_hi_ready"], e + 1 + 2 * i)
                k = bass.ds(2 * g + 4 * i, 2)
                dve.tensor_tensor(a_lo[:, k, 0:T], up, a_hi[:, k, 0:T].bitcast(F32), ALU.subtract).then_inc(S["a_ready"], 2)

            def gate_up(n):
                st = stages["up", n]
                for g in range(2):
                    split_to(st.u0 + 2 * g + 5)
                    gated_eviction(n, g)
                split_to(st.u0 + 9)
                with dve.Fori(0, 4) as i:
                    u = st.u0 + 9
                    gated_eviction(n, 2, i)
                    low_part(u, i)
                    low_part(u + 1, i)
                    gated_eviction(n, 3, i)
                    low_part(u + 2, i)
                    low_part(u + 3, i)
                nxt[0] = st.u0 + 25
                gated_eviction(n, 10)

            def mod_part(part):
                for n in range(MOD_PER):
                    dve.wait_ge(mod_loaded, 16 * (MOD_PER * part + n + 1))
                    if part == 0 and n == 0:
                        dve.wait_ge(S["silu_c_ready"], 1)
                    elif n == 0:
                        dve.wait_ge(S["mod_psum"], part)
                    acc = mod_acc[:, n, :]
                    chain(dve.tensor_scalar(acc, mod_w[:, 0, :], silu_c[:, 0:1], None, ALU.mult))
                    for j in range(1, 8):
                        ins = dve.scalar_tensor_tensor(acc, mod_w[:, j, :], silu_c[:, j:j + 1], acc, ALU.mult, ALU.add)
                        if j < 7:
                            chain(ins)
                    ins.then_inc(S["mod_used"], 1)
                    yield

            def mod_evict(part, bank):
                cols = slice(2 * MOD_PER * part, 2 * MOD_PER * (part + 1))
                dve.wait_ge(S["mod_psum"], part + 1)
                dve.tensor_tensor(mod[:, cols], ps[:, bank, 288:288 + 2 * MOD_PER],
                                  vec[:, V_BMOD + 2 * MOD_PER * part:V_BMOD + 2 * MOD_PER * (part + 1)],
                                  ALU.add).then_inc(S["mod_evicted"], 1)

            def down(n, mod_work=iter(())):
                st = stages["down", n]
                for n, u in enumerate(range(nxt[0], end_of(st) + 1)):
                    if n in (0, 1, 3, 4, 6, 7):
                        next(mod_work, None)
                    split_to(u + 1)

            def add_square(m, T):
                if m == 0:
                    return
                dve.wait_ge(S["sq_ready"], c.now("sq_ready") + m + 1)
                first = sq[:, 0, 0:T] if m == 1 else sq_sum[:, 0:T]
                if m > 1:
                    dve.wait_ge(S["sq_used"], c.now("sq_used") + m - 1)
                dve.tensor_tensor(sq_sum[:, 0:T], first, sq[:, m % 2, 0:T], ALU.add)\
                   .then_inc(S["sq_used" if m < 7 else "sumsq_ready"], 1)

            def squares_done():
                c.up("sq_ready", 8)
                c.up("sq_used", 6)

            def root(T, between=None):
                n = 2 if T == 2 * P else 3
                dve.wait_ge(S["std_ready"], c.up("std_ready"))
                dve.reciprocal(r_col[:, 0:n], std_col[:, 0:n]).then_inc(S["rstd_columns"], 1)
                if between is not None:
                    between()
                dve.wait_ge(S["rstd_spread"], c.up("rstd_spread"))

            def tail(st, gain, nx, next_gain, shift=None, normed=True, part=None):
                T = st.T
                off = TOK - T
                split_to(nx.u0 + 1)
                if normed:
                    for m in range(8):
                        add_square(m, T)
                    squares_done()
                    low_half()
                    root(T, between=lambda: low_half())
                update_and_prepare(T, off, gain, next_gain, shift, normed, nx, spread=ps[:, side_bank(nx), :], part=part,
                                   src=None if normed else st)

            def second_gains(part):
                mod_evict(part, 6)
                dve.wait_ge(S["mod_evicted"], MOD_PARTS)
                for w in range(2):
                    dve.tensor_scalar(gain2[:, 8 * w:8 * w + 8], mod[:, 8 + 24 * w:16 + 24 * w], 1.0, None, ALU.add)\
                       .then_inc(S["vec_chain"], 1)
                dve.wait_ge(S["vec_chain"], c.up("vec_chain", 2))
                for w in range(2):
                    chain(dve.tensor_tensor(gain2[:, 8 * w:8 * w + 8], gain2[:, 8 * w:8 * w + 8],
                                            vec[:, V_GMIX + 8 * w:V_GMIX + 8 * w + 8], ALU.mult))

            def update_and_prepare(T, off, gain, next_gain, shift, normed, nx, update=True, spread=None, part=None, src=None, between=None):
                n_h = c.now("h_ready")
                n_v = c.now("vec_chain")
                deferred = shift is None
                for m in range(8 + 2):
                    if update and m < 8:
                        if normed:
                            if m >= 2:
                                dve.wait_ge(S["h_ready"], n_h + m - 1)
                            dve.tensor_tensor(pair_a[:, m % 2, 0:T], f[:, m, 0:T], spread[:, 0:T], ALU.mult)\
                               .then_inc(S["vec_chain"], 1)
                            c.up("vec_chain")
                    k = m - 1
                    if update and 0 <= k < 8:
                        if normed:
                            scaled = pair_a[:, k % 2, 0:T]
                            dve.wait_ge(S["vec_chain"], n_v + k + 1)
                        else:
                            scaled = ps[:, src.bank(src.t0 + k), 0:T]
                            dve.wait_ge(S["tile_done"], src.t0 + k + 1)
                        dve.scalar_tensor_tensor(h[:, k, off:off + T], scaled, gain[:, k:k + 1], h[:, k, off:off + T],
                                                 ALU.mult, ALU.add).then_inc(S["h_ready"], 1)
                    k = m - 2
                    if k >= 0 and nx is not None:
                        if deferred:
                            dve.wait_ge(S["x_hi_ready"], c.up("x_hi_ready"))
                            dve.scalar_tensor_tensor(x_lo[:, k, 0:T], h[:, k, off:off + T], next_gain[:, k:k + 1],
                                                     x_hi[:, k, 0:T].bitcast(F32), ALU.mult, ALU.subtract)\
                               .then_inc(S["x_ready"], 1)
                        add_square(k, T)
                    if between is not None and m in between:
                        between[m]()
                if update:
                    c.up("h_ready", 8)
                if nx is None:
                    return
                squares_done()
                if deferred:
                    return
                if part is not None:
                    second_gains(part)
                else:
                    low_half()
                root(T, between=low_half)
                for m in range(8 + 2):
                    if m < 8:
                        dve.tensor_tensor(f[:, m, 0:T], h[:, m, off:off + T], spread[:, 0:T], ALU.mult)\
                           .then_inc(S["vec_chain"], 1)
                        c.up("vec_chain")
                    k = m - 1
                    if 0 <= k < 8:
                        dve.wait_ge(S["vec_chain"], c.now("vec_chain") - (1 if m < 8 else 0))
                        dve.tensor_scalar(f[:, k, 0:T], f[:, k, 0:T], next_gain[:, k:k + 1], shift[:, k:k + 1],
                                          ALU.mult, ALU.add).then_inc(S["full_ready"], 1)
                    k = m - 2
                    if k >= 0:
                        dve.wait_ge(S["x_hi_ready"], c.up("x_hi_ready"))
                        dve.tensor_tensor(x_lo[:, k, 0:T], f[:, k, 0:T], x_hi[:, k, 0:T].bitcast(F32),
                                          ALU.subtract).then_inc(S["x_ready"], 1)

            def before_evictions(nx, deferred=True, part=None):
                split_to(nx.u0 + 4)
                if deferred:
                    root(nx.T, between=lambda: split_to(nx.u0 + 5))
                    dve.tensor_copy(rstd[:, 0:nx.T], ps[:, side_bank(nx), 0:nx.T]).then_inc(S["rstd_kept"], 1)
                    if part is not None:
                        mod_evict(part, 6 if nx.quad else nx.bank(nx.t0 + 6))
                    dve.wait_ge(S["rstd_kept"], c.up("rstd_kept"))
                split_to(nx.u0 + 5)

            def ln(layer, which):
                at_col = V_LN + 8 * (6 * layer + which)
                return vec[:, at_col:at_col + 8]

            def side_bank(st):
                return 7 if st.quad else st.bank(st.t0 + 7)

            dve.memset(eps[:, 0:1], EPS)
            dve.memset(eps[:, 1:2], SUBLN_EPS)
            dve.wait_ge(vectors_loaded, 16)
            for n in range(4):
                dve.tensor_scalar(g_out[:, 8 * n:8 * n + 8], ln(n // 2, 1 + 4 * (n % 2)), 0.5, None, ALU.mult)
            dve.tensor_scalar(g_out[:, 48:49], vec[:, V_SUB:V_SUB + 1], 1.0 - LAMBDA_INIT, None, ALU.mult)
            dve.tensor_tensor(lam[:, 0:2], vec[:, V_LAM:V_LAM + 4:2], vec[:, V_LAM + 1:V_LAM + 4:2], ALU.mult)
            dve.wait_ge(h_loaded, 16)

            update_and_prepare(TOK, 0, None, ln(0, 0), None, False, stages["up", 0], update=False,
                               between={5: lambda: split_to(1)})
            split_to(2)
            dve.wait_ge(mask_loaded, 16)
            dve.wait_ge(constants_loaded, 16)
            dve.tensor_copy(ident_b[:, :], ident)
            dve.tensor_copy(mask[:, :], f[:, 0, :]).then_inc(S["lam_in"], 1)
            split_to(3)
            dve.wait_ge(S["lam_exp"], 1)
            chain(dve.tensor_tensor(lam[:, 4:5], lam[:, 2:3], lam[:, 3:4], ALU.subtract))
            chain(dve.tensor_scalar(lam[:, 5:6], lam[:, 4:5], LAMBDA_INIT, None, ALU.add))
            before_evictions(stages["up", 0])
            gate_up(0)
            down(0, mod_part(0))
            conv = stages["conv_in"]
            tail(stages["down", 0], g_out[:, 0:8], conv, ln(0, 2))
            before_evictions(conv, part=0)
            for g in range(6):
                split_to(conv.u0 + 2 * g + 5)
                t = conv.t0 + GROUP * g
                b = t % 8
                if g < 4:
                    for q, dst in enumerate((pair_a, pair_b)):
                        dve.wait_ge(S["tile_done"], t + 2 + 2 * q)
                        dve.tensor_tensor(dst[:, :, :], ps[:, b + 2 * q:b + 2 * q + 2, 0:TOK], bcast(rstd, TOK),
                                          ALU.mult).then_inc(S["tile_evicted"], 2)
                    dve.wait_ge(S["tile_evicted"], conv.evicted(t + 4))
                    chain(dve.tensor_tensor(pair_a[:, :, :], pair_a[:, :, :], pair_b[:, :, :], ALU.mult))
                    taps = [V_CONV + 8 * j + 2 * g for j in range(3)]
                    for back in range(3):
                        for m in range(2):
                            y, w = f[:, 2 * g + m, back:TOK], vec[:, taps[2 - back] + m:taps[2 - back] + m + 1]
                            if back == 0:
                                ins = dve.tensor_scalar(y, pair_a[:, m, :], w, None, ALU.mult)
                            else:
                                ins = dve.scalar_tensor_tensor(y, pair_a[:, m, 0:TOK - back], w, y, ALU.mult, ALU.add)
                            if m == 0:
                                ins.then_inc(S["vec_chain"], 1)
                                c.up("vec_chain")
                            else:
                                chain(ins)
                else:
                    for q, dst in enumerate((pair_a, pair_b)):
                        k = 4 * (g - 4) + 2 * q
                        e = E0["conv_in"] + 2 * (g - 4) + q
                        dve.wait_ge(S["tile_done"], t + 2 + 2 * q)
                        if g == 5:
                            dve.wait_ge(S["a_ready"], A0["conv_in"] + 2 * q + 2)
                        dve.tensor_tensor(dst[:, :, :], ps[:, b + 2 * q:b + 2 * q + 2, 0:TOK], bcast(rstd, TOK),
                                          ALU.mult).then_inc(S["tile_evicted"], 2)
                        dve.wait_ge(S["tile_evicted"], conv.evicted(t + 2 + 2 * q))
                        dve.tensor_tensor(dst[:, :, :], dst[:, :, :], f[:, k:k + 2, :], ALU.mult)\
                           .then_inc(S["act_in_ready"], 1)
                    for q, src in enumerate((pair_a, pair_b)):
                        k = 4 * (g - 4) + 2 * q
                        dve.wait_ge(S["a_hi_ready"], E0["conv_in"] + 2 * (g - 4) + q + 1)
                        dve.tensor_tensor(a_lo[:, k:k + 2, :], src[:, :, :], a_hi[:, k:k + 2, :].bitcast(F32),
                                          ALU.subtract).then_inc(S["a_ready"], 2)
            tail(stages["conv_out"], ln(0, 3), stages["up", 1], ln(0, 4))
            before_evictions(stages["up", 1])
            gate_up(1)
            down(1, mod_part(1))
            up2 = stages["up", 2]
            tail(stages["down", 1], g_out[:, 8:16], up2, ln(1, 0))

            before_evictions(up2, part=1)
            gate_up(2)
            down(2, mod_part(2))
            qkv = stages["qkv"]
            tail(stages["down", 2], g_out[:, 16:24], qkv, ln(1, 2))
            before_evictions(qkv, part=2)

            def evict4(st, g, dst, T, scaled):
                t = st.t0 + GROUP * g + (4 if st.name == "w_in" else 0)
                for m in (0, 2):
                    dve.wait_ge(S["tile_done"], t + m + 2)
                    if scaled:
                        ins = dve.tensor_tensor(dst[:, m:m + 2, :], ps[:, m:m + 2, 0:T], bcast(rstd, T), ALU.mult)
                    else:
                        ins = dve.tensor_copy(dst[:, m:m + 2, :], ps[:, m:m + 2, 0:T])
                    ins.then_inc(S["tile_evicted"], 2)
                dve.wait_ge(S["tile_evicted"], st.evicted(t + 4))

            def maxima(n, scale):
                s = c.now("scored")
                c.up("scored")
                col = small[:, s % 4, :]
                dve.wait_ge(S["scored"], s + 1)
                chain(dve.tensor_reduce(col[:, 0:2], ps[:, 4:6, 0:n], AX.X, ALU.max))
                dve.tensor_scalar(col[:, 2:4], col[:, 0:2], -scale, None, ALU.mult).then_inc(S["max_ready"], 1)

            def factors():
                s = c.now("weights_ready")
                c.up("weights_ready")
                col = small[:, s % 4, :]
                dve.wait_ge(S["probs_ready"], 2 * s + 2)
                chain(dve.reciprocal(col[:, 6:8], col[:, 4:6]))
                return col

            def peak(s):
                maxima(META + P * (s % 2 + 1), 64 ** -0.5)

            def combine(s):
                n = META + P * (s % 2 + 1)
                col = factors()
                chain(dve.tensor_scalar(pair_a[:, 1, 0:n], pair_a[:, 1, 0:n], col[:, 7:8], lam[:, 5:6], ALU.mult, ALU.mult))
                if s:
                    dve.wait_ge(S["p_turned"], s)
                dve.scalar_tensor_tensor(pair_b[:, 0, 0:n], pair_a[:, 0, 0:n], col[:, 6:7], pair_a[:, 1, 0:n],
                                         ALU.mult, ALU.subtract).then_inc(S["weights_ready"], 1)
                c.up("p_turned")

            def rope(g, m, bank=7):
                x, turned = qk1[:, g % 2, m, :], f[:, 4 + m, :]
                dve.wait_ge(S["rotated"], c.up("rotated"))
                dve.tensor_tensor(turned, ps[:, bank, 0:TOK], sin1, ALU.mult).then_inc(S["rotation_read"], 1)
                dve.tensor_tensor(x, x, cos1, ALU.mult).then_inc(S["vec_chain"], 1)
                dve.wait_ge(S["rotation_read"], c.up("rotation_read"))
                dve.wait_ge(S["vec_chain"], c.up("vec_chain"))
                dve.tensor_tensor(x, x, turned, ALU.add).then_inc(S["qk_ready"], 1)

            def head_roots():
                dve.wait_ge(S["head_std"], c.up("head_std"))
                dve.reciprocal(head_col[:, 8:16], head_col[:, 0:8]).then_inc(S["head_columns"], 1)

            def subln(r, bank=7):
                x = o1[:, 2 * r:2 * r + 2, :].rearrange("p a n -> p (a n)")
                dve.wait_ge(S["head_spread"], c.up("head_spread"))
                dve.scalar_tensor_tensor(x, x, g_out[:, 48:49], ps[:, bank, :], ALU.mult, ALU.mult)\
                   .then_inc(S["act_in_ready"], 1)

            def subln_lo(r):
                heads = slice(2 * r, 2 * r + 2)
                dve.wait_ge(S["a_hi_ready"], E0["qkv"] + r + 1)
                dve.tensor_tensor(a_lo[:, heads, 0:SEQ], o1[:, heads, :], a_hi[:, heads, 0:SEQ].bitcast(F32),
                                  ALU.subtract).then_inc(S["a_ready"], 2)

            def evict_qk(g):
                evict4(qkv, QK_GROUP[g], qk1[:, g % 2, :, :], TOK, True)

            evict_qk(0)
            low_half()
            rope(0, 0)
            low_half()
            rope(0, 2)
            rope(0, 1)
            low_half()
            rope(0, 3)
            low_half()
            evict4(qkv, V_GROUP[0], v1_T[:, :, :], TOK, True)
            peak(0)
            low_half()
            combine(0)
            peak(1)
            low_half()
            combine(1)
            peak(2)
            combine(2)
            peak(3)
            low_half()
            combine(3)
            low_half()
            evict_qk(1)
            low_half()
            rope(1, 0)
            low_half()
            rope(1, 2)
            rope(1, 1)
            rope(1, 3)
            peak(4)
            low_half()
            combine(4)
            peak(5)
            low_half()
            evict_qk(2)
            combine(5)
            low_half()
            peak(6)
            rope(2, 0)
            combine(6)
            low_half()
            peak(7)
            rope(2, 2)
            combine(7)
            rope(2, 1)
            low_half()
            rope(2, 3)
            low_half()
            dve.wait_ge(S["turned"], 3)
            evict4(qkv, V_GROUP[1], v1_T[:, :, :], TOK, True)
            peak(8)
            head_roots()
            low_half()
            combine(8)
            peak(9)
            low_half()
            combine(9)
            peak(10)
            combine(10)
            subln(0)
            peak(11)
            low_half()
            combine(11)
            subln(1)
            evict_qk(3)
            rope(3, 0)
            rope(3, 2, bank=4)
            rope(3, 1, bank=5)
            rope(3, 3)
            peak(12)
            low_half()
            combine(12)
            for s in range(13, 16):
                peak(s)
                if s < 15:
                    low_half()
                combine(s)
                if s < 15:
                    subln_lo(s - 13)
            head_roots()
            subln(2)
            subln(3, bank=6)
            for r in (2, 3):
                subln_lo(r)
            tail(stages["attn_out"], ln(1, 3), stages["up", 3], ln(1, 4))
            before_evictions(stages["up", 3])
            gate_up(3)
            down(3, mod_part(3))
            w_in = stages["w_in"]
            tail(stages["down", 3], g_out[:, 24:32], w_in, gain2[:, 0:8], shift=mod[:, 0:8], part=3)

            def rotation(dst, which, x, r=None):
                cos, sin = tab[:, 2 * which, :], tab[:, 2 * which + 1, :]
                dve.wait_ge(S["rotated"], c.up("rotated"))
                if r is None:
                    swapped = ps[:, 7, 0:SEQ]
                else:
                    x, dst = x[:, 2 * r:2 * r + 2, :], dst[:, 2 * r:2 * r + 2, :]
                    cos, sin = bcast(cos, SEQ), bcast(sin, SEQ)
                    swapped = ps[:, 7, :].rearrange("p (a n) -> p a n", a=2)
                ins = dve.tensor_tensor(dst, swapped, sin, ALU.mult)
                if r is None:
                    for qt in range(2):
                        ins = dve.tensor_scalar(wi[:, qt, :], ps[:, 7, SEQ + qt * P:SEQ + qt * P + 8], IDX_SCALE,
                                                None, ALU.mult)
                ins.then_inc(S["rotation_read"], 1)
                dve.tensor_tensor(x, x, cos, ALU.mult).then_inc(S["vec_chain"], 1)
                dve.wait_ge(S["rotation_read"], c.up("rotation_read"))
                dve.wait_ge(S["vec_chain"], c.up("vec_chain"))
                dve.tensor_tensor(x, x, dst, ALU.add).then_inc(S["roped"], 1)
                c.up("roped")

            def idx_add(r):
                qt, heads = ((0, range(8)), (1, range(4)), (1, range(4, 8)))[r]
                n = P * (qt + 1)
                dve.wait_ge(S["idx_relu"], r + 1)
                src = (work1, work2)[r % 2][:, :, :].rearrange("p a n -> p (a n)")
                for b, i in enumerate(heads):
                    before = mask[:, META + P - P * qt:META + P - P * qt + n] if i == 0 else score[:, qt, 0:n]
                    at_col = 512 * (i % 2) + b // 2 * n
                    ins = dve.scalar_tensor_tensor(score[:, qt, 0:n], src[:, at_col:at_col + n], wi[:, qt, i:i + 1], before,
                                                   ALU.mult, ALU.add)
                    if i < heads[-1]:
                        chain(ins)
                ins.then_inc(S["idx_used"], 1)
                dve.wait_ge(S["idx_used"], r + 1)

            def take_best(qt, times):
                x = score[:, qt, 0:P * (qt + 1)]
                for _ in range(times):
                    chain(dve.max(top8[:, :], x))
                    chain(dve.match_replace(x, top8[:, :], x, TAKEN))

            def select(qt):
                n = P * (qt + 1)
                x = score[:, qt, 0:n]
                chain(dve.tensor_scalar(x, x, TAKEN / 2, NEG, ALU.is_gt, ALU.mult))
                dve.tensor_tensor(sel[:, qt, 0:n], x, mask[:, META + P - P * qt:META + P - P * qt + n],
                                  ALU.add).then_inc(S["sel_ready"], 1)

            def qk_norm(n, name, r):
                x = qkv2[name][:, 2 * r:2 * r + 2, :].rearrange("p a n -> p (a n)")
                dve.wait_ge(S["head_spread"], c.up("head_spread"))
                dve.scalar_tensor_tensor(x, x, vec[:, V_GQK + n:V_GQK + n + 1], ps[:, 7, :], ALU.mult, ALU.mult)\
                   .then_inc(S["normed_heads"], 1)
                dve.wait_ge(S["normed_heads"], c.up("normed_heads"))

            def peak2(s):
                maxima(P * (s % 2 + 1), P ** -0.5)

            def normalise(s):
                n = P * (s % 2 + 1)
                col = factors()
                dve.wait_ge(S["p_turned"], c.now("p_turned"))
                for comp in range(2):
                    ins = dve.tensor_scalar(pair_b[:, comp, 0:n], pair_a[:, comp, 0:n], col[:, 6 + comp:7 + comp],
                                            None, ALU.mult)
                ins.then_inc(S["weights_ready"], 1)
                c.up("p_turned")

            def store(g, dst):
                evict4(w_in, g, dst[:, :, :], SEQ, False)

            def qk_jobs(n, name, best=0):
                low_half()
                low_half()
                if best:
                    take_best(1, 1)
                head_roots()
                low_half()
                if best > 1:
                    take_best(1, 1)
                qk_norm(n, name, 0)
                if best > 2:
                    take_best(1, 1)
                qk_norm(n, name, 1)
                if best > 3:
                    take_best(1, best - 3)
                rotation(work1, 0, qkv2[name], 0)
                rotation(work1, 0, qkv2[name], 1)

            u0 = w_in.u0
            split_to(u0 + 4)
            dve.wait_ge(S["tile_done"], w_in.t0 + 4)
            dve.tensor_copy(ki[:, :], ps[:, 0, 0:SEQ])
            dve.tensor_copy(wi_T[:, :], ps[:, 1, 0:SEQ]).then_inc(S["tile_evicted"], 4)
            dve.wait_ge(S["tile_evicted"], w_in.evicted(w_in.t0 + 4))
            split_to(u0 + 5)
            dve.wait_ge(tables_loaded, 16)
            rotation(work1[:, 0, :], 1, ki[:, :])
            split_to(u0 + 6)
            store(0, qi)
            rotation(work1, 1, qi, 0)
            low_half()
            rotation(work1, 1, qi, 1)
            low_half()
            idx_add(0)
            store(1, v2_T)
            low_half()
            low_half()
            idx_add(1)
            low_half()
            low_half()
            idx_add(2)
            take_best(0, TOPK // 8 - 3)
            store(2, qkv2["q_a"])
            low_half()
            qk_jobs(0, "q_a", 4)
            store(3, qkv2["k_a"])
            low_half()
            qk_jobs(1, "k_a", TOPK // 8 - 4)
            dve.wait_ge(S["turned"], 8)
            store(4, v2_T)
            take_best(0, 3)
            for qt in range(2):
                select(qt)
            low_half()
            low_half()
            low_half()
            peak2(0)
            normalise(0)
            peak2(1)
            low_half()
            normalise(1)
            peak2(2)
            low_half()
            store(5, qkv2["q_b"])
            normalise(2)
            peak2(3)
            low_half()
            normalise(3)
            head_roots()
            low_half()
            qk_norm(2, "q_b", 0)
            qk_norm(2, "q_b", 1)
            rotation(work1, 0, qkv2["q_b"], 0)
            rotation(work1, 0, qkv2["q_b"], 1)
            store(6, qkv2["k_b"])
            low_half()
            low_half()
            qk_jobs(3, "k_b")
            store(7, gates[:, 0:4, :])
            low_half()
            low_half()
            peak2(4)
            normalise(4)
            peak2(5)
            low_half()
            normalise(5)
            peak2(6)
            low_half()
            normalise(6)
            peak2(7)
            store(8, gates[:, 4:8, :])
            normalise(7)
            split_to(u0 + 24)
            store(9, gates[:, 8:12, :])
            split_to(u0 + 26)
            for which in range(2):
                heads = slice(4 * which, 4 * which + 4)
                dve.wait_ge(S["a_hi_ready"], E0["w_in"] + which + 1)
                dve.tensor_tensor(o2_lo[:, heads, :], f[:, heads, 0:SEQ], o2_hi[:, heads, :].bitcast(F32),
                                  ALU.subtract).then_inc(S["a_ready"], 4)
            store(10, gates[:, 12:16, :])
            dsa, moba, w_out = stages["br_dsa"], stages["br_moba"], stages["w_out"]
            split_to(end_of(dsa) + 3)
            dve.wait_ge(S["gate_ready"], 4)
            for m in range(0, 8, 2):
                t = dsa.t0 + m
                dve.wait_ge(S["tile_done"], t + 2)
                dve.tensor_tensor(gates[:, m:m + 2, :], ps[:, t % 8:t % 8 + 2, 0:SEQ], gates[:, m:m + 2, :],
                                  ALU.mult).then_inc(S["tile_evicted"], 2)
            split_to(end_of(moba) + 2)
            for n in range(4 + 2):
                if n < 4:
                    m = 2 * n
                    t = moba.t0 + m
                    dve.wait_ge(S["tile_done"], t + 2)
                    dve.tensor_tensor(gates[:, 8 + m:10 + m, :], ps[:, t % 8:t % 8 + 2, 0:SEQ], gates[:, 8 + m:10 + m, :],
                                      ALU.mult).then_inc(S["tile_evicted"], 2)
                if 1 <= n < 5:
                    m = 2 * (n - 1)
                    dve.wait_ge(S["tile_evicted"], moba.evicted(moba.t0 + m + 2))
                    dve.tensor_tensor(gates[:, m:m + 2, :], gates[:, m:m + 2, :], gates[:, 8 + m:10 + m, :],
                                      ALU.add).then_inc(S["act_in_ready"], 1)
                if n >= 2:
                    m = 2 * (n - 2)
                    dve.wait_ge(S["a_hi_ready"], E0["br"] + n - 2 + 1)
                    dve.tensor_tensor(z_lo[:, m:m + 2, :], gates[:, m:m + 2, :], z_hi[:, m:m + 2, :].bitcast(F32),
                                      ALU.subtract).then_inc(S["a_ready"], 2)
            tail(w_out, mod[:, 16:24], stages["up", 4], gain2[:, 8:16], shift=mod[:, 24:32], normed=False)
            before_evictions(stages["up", 4], deferred=False)
            gate_up(4)
            down(4)
            last = stages["down", 4]
            for m in range(8):
                dve.wait_ge(S["tile_done"], last.t0 + m + 1)
                dve.scalar_tensor_tensor(h[:, m, META:TOK], ps[:, last.bank(last.t0 + m), 0:SEQ], mod[:, 40 + m:41 + m],
                                         h[:, m, META:TOK], ALU.mult, ALU.add).then_inc(S["h_ready"], 1)

        @block.scalar
        def _(act):
            c = Count()
            nxt = [0]

            def high_part(u, i=0):
                act.wait_ge(raw_loaded[u % RING], 16 * (u // RING + 1) + 16 * i)
                if u >= RING:
                    name, n = used_by[u - RING]
                    act.wait_ge(S[name], n + (8 if name == "tile_done" else 2) * i)
                act.activation(w_hi[:, u % RING, :], raw[:, u % RING, :], ACT.Copy).then_inc(S["hi_ready"], 1)

            def split_to(u_end):
                while nxt[0] < min(u_end, n_units):
                    high_part(nxt[0])
                    nxt[0] += 1

            def gated(n, g, i=0):
                st = stages["up", n]
                T, t = st.T, st.t0 + GROUP * g
                act.wait_ge(S["tile_evicted"], st.evicted(t + 2) + 8 * i)
                act.activation(pair_a[:, :, 0:T], pair_a[:, :, 0:T], ACT.Silu).then_inc(S["silu_done"], 1)
                act.wait_ge(S["act_in_ready"], I0["up", n] + g + 1 + 2 * i)
                act.activation(a_hi[:, bass.ds(2 * g + 4 * i, 2), 0:T], pair_b[:, :, 0:T], ACT.Copy)\
                   .then_inc(S["a_hi_ready"], 1)

            def gate_up(n):
                st = stages["up", n]
                for g in range(2):
                    split_to(st.u0 + 2 * g + 5)
                    gated(n, g)
                split_to(st.u0 + 9)
                with act.Fori(0, 4) as i:
                    u = st.u0 + 9
                    gated(n, 2, i)
                    high_part(u, i)
                    high_part(u + 1, i)
                    gated(n, 3, i)
                    high_part(u + 2, i)
                    high_part(u + 3, i)
                nxt[0] = st.u0 + 25
                gated(n, 10)

            def square(m, src, T):
                if m >= 2:
                    act.wait_ge(S["sq_used"], c.now("sq_used") + max(1, m - 2))
                act.activation(sq[:, m % 2, 0:T], src, ACT.Square).then_inc(S["sq_ready"], 1)

            def root(T, bank):
                act.wait_ge(S["stats_done"], c.up("stats_done"))
                n = 2 if T == 2 * P else 3
                act.activation(std_col[:, 0:n], ps[:, bank, 0:n], ACT.Sqrt, bias=eps[:, 0:1], scale=1.0 / D)\
                   .then_inc(S["std_ready"], 1)

            def tail(st, nx, next_gain, full=False, normed=True, bank=None):
                T = st.T
                off = TOK - T
                split_to(nx.u0 + 2)
                act.activation(eps[:, 2:3], eps[:, 0:1], ACT.Sqrt)
                if normed:
                    for m in range(8):
                        sums = ps[:, st.bank(st.t0 + m), 0:T]
                        act.wait_ge(S["tile_done"], st.t0 + m + 1)
                        square(m, sums, T)
                        act.activation(f[:, m, 0:T], sums, ACT.Copy).then_inc(S["f_ready"], 1)
                    c.up("sq_used", 6)
                    root(T, bank)
                    split_to(nx.u0 + 3)
                prepare(T, off, next_gain, full, bank)

            def prepare(T, off, next_gain, full, bank, update=True, split_after=None):
                for m in range(8):
                    if update:
                        act.wait_ge(S["h_ready"], c.up("h_ready"))
                    if not full:
                        act.activation(x_hi[:, m, 0:T], h[:, m, off:off + T], ACT.Identity,
                                       scale=next_gain[:, m:m + 1]).then_inc(S["x_hi_ready"], 1)
                    square(m, h[:, m, off:off + T], T)
                    if m == split_after:
                        split_to(1)
                c.up("sq_used", 6)
                if full:
                    root(T, bank)
                    for m in range(8):
                        act.wait_ge(S["full_ready"], c.up("full_ready"))
                        act.activation(x_hi[:, m, 0:T], f[:, m, 0:T], ACT.Copy).then_inc(S["x_hi_ready"], 1)

            def before_evictions(nx, bank):
                split_to(nx.u0 + 5)
                root(nx.T, bank)

            def ln(layer, which):
                at_col = V_LN + 8 * (6 * layer + which)
                return vec[:, at_col:at_col + 8]

            def side_bank(st):
                return 7 if st.quad else st.bank(st.t0 + 7)

            act.wait_ge(vectors_loaded, 16)
            act.wait_ge(h_loaded, 16)

            prepare(TOK, 0, ln(0, 0), False, None, update=False, split_after=3)
            split_to(3)
            act.wait_ge(S["lam_sums"], 1)
            act.activation(lam[:, 2:4], ps[:, 7, 0:2], ACT.Exp).then_inc(S["lam_exp"], 1)
            before_evictions(stages["up", 0], side_bank(stages["up", 0]))
            act.activation(silu_c[:, :], vec[:, V_C:V_C + 8], ACT.Silu).then_inc(S["silu_c_ready"], 1)
            gate_up(0)
            conv = stages["conv_in"]
            tail(stages["down", 0], conv, ln(0, 2), bank=side_bank(conv))
            before_evictions(conv, side_bank(conv))
            for g in range(6):
                split_to(conv.u0 + 2 * g + 5)
                if g >= 4:
                    for q, src in enumerate((pair_a, pair_b)):
                        k = 4 * (g - 4) + 2 * q
                        act.wait_ge(S["act_in_ready"], I0["conv_in"] + 2 * (g - 4) + q + 1)
                        act.activation(a_hi[:, k:k + 2, :], src[:, :, :], ACT.Copy).then_inc(S["a_hi_ready"], 1)
            up1, up2, qkv, up3, w_in = (stages["up", 1], stages["up", 2], stages["qkv"], stages["up", 3], stages["w_in"])
            tail(stages["conv_out"], up1, ln(0, 4), bank=side_bank(up1))
            before_evictions(up1, side_bank(up1))
            gate_up(1)
            tail(stages["down", 1], up2, ln(1, 0), bank=side_bank(up2))

            before_evictions(up2, side_bank(up2))
            gate_up(2)
            tail(stages["down", 2], qkv, ln(1, 2), bank=7)
            before_evictions(qkv, 7)

            def soften(n, scale):
                s = c.now("scored")
                c.up("scored")
                col = small[:, s % 4, :]
                act.wait_ge(S["max_ready"], s + 1)
                if s:
                    act.wait_ge(S["weights_ready"], s)
                for comp in range(2):
                    act.activation(pair_a[:, comp, 0:n], ps[:, 4 + comp, 0:n], ACT.Exp, bias=col[:, 2 + comp:3 + comp],
                                   scale=scale, accum_out=col[:, 4 + comp:5 + comp]).then_inc(S["probs_ready"], 1)

            def exps(s):
                soften(META + P * (s % 2 + 1), 64 ** -0.5)

            def store_p(s):
                w = s % 2 + 2
                act.wait_ge(S["p_turned"], c.up("p_turned"))
                act.activation(pT1[:, 0:w, :], ps[:, 6, 0:w * P].rearrange("p (w n) -> p w n", w=w), ACT.Copy)\
                   .then_inc(S["pT_ready"], 1)

            def store_o(s):
                head, cols = s // 2, slice(P * (s % 2), P * (s % 2) + P)
                act.wait_ge(S["pv_done"], s + 1)
                act.activation(o1[:, head, cols], ps[:, 6, 3 * P:4 * P], ACT.Copy).then_inc(S["o_evicted"], 1)
                if s == 8:
                    act.wait_ge(S["head_sums"], 1)
                act.activation(f[:, head % 4, cols], ps[:, 6, 3 * P:4 * P], ACT.Square).then_inc(S["head_sq"], 1)

            def store_v(n):
                g, w = n // 3, n % 3
                act.wait_ge(S["turned"], n + 1)
                act.activation(v1[:, w, 4 * g:4 * g + 4, :], ps[:, 7, :].rearrange("p (a n) -> p a n", a=4),
                               ACT.Copy).then_inc(S["v_stored"], 1)

            def subln_std(half):
                act.wait_ge(S["head_sums"], half + 1)
                if half:
                    act.wait_ge(S["head_columns"], 1)
                act.activation(head_col[:, 0:8], ps[:, 7, 0:8], ACT.Sqrt,
                               bias=eps[:, 1:2], scale=1.0 / P).then_inc(S["head_std"], 1)

            def subln_hi(r):
                heads = slice(2 * r, 2 * r + 2)
                act.wait_ge(S["act_in_ready"], I0["qkv"] + r + 1)
                act.activation(a_hi[:, heads, 0:SEQ], o1[:, heads, :], ACT.Copy).then_inc(S["a_hi_ready"], 1)

            def split():
                split_to(nxt[0] + 1)

            split()
            split()
            split()
            exps(0)
            store_v(0)
            store_v(1)
            store_p(0)
            exps(1)
            store_v(2)
            store_o(0)
            store_p(1)
            exps(2)
            split()
            store_o(1)
            store_p(2)
            exps(3)
            store_o(2)
            store_p(3)
            split()
            store_o(3)
            split()
            exps(4)
            store_p(4)
            exps(5)
            store_o(4)
            split()
            store_p(5)
            exps(6)
            store_o(5)
            store_p(6)
            exps(7)
            store_o(6)
            split()
            store_p(7)
            store_o(7)
            subln_std(0)
            split()
            exps(8)
            store_v(3)
            store_v(4)
            store_p(8)
            exps(9)
            store_v(5)
            store_o(8)
            store_p(9)
            exps(10)
            split()
            store_o(9)
            store_p(10)
            exps(11)
            subln_hi(0)
            store_o(10)
            subln_hi(1)
            store_p(11)
            split()
            store_o(11)
            exps(12)
            for s in range(12, 16):
                store_p(s)
                if s < 15:
                    exps(s + 1)
                store_o(s)
            subln_std(1)
            subln_hi(2)
            subln_hi(3)
            tail(stages["attn_out"], up3, ln(1, 4), bank=side_bank(up3))
            before_evictions(up3, side_bank(up3))
            gate_up(3)
            tail(stages["down", 3], w_in, None, full=True, bank=7)

            def qk_squares(group, name):
                act.wait_ge(S["tile_evicted"], w_in.evicted(w_in.t0 + GROUP * (group + 2)))
                act.activation(f[:, 4:8, 0:SEQ], qkv2[name][:, :, :], ACT.Square).then_inc(S["head_sq"], 1)

            def qk_std(n):
                act.wait_ge(S["head_sums"], 2 + n + 1)
                act.wait_ge(S["head_columns"], 2 + n)
                act.activation(head_col[:, 0:8], ps[:, 7, 0:8], ACT.Sqrt,
                               bias=eps[:, 0:1], scale=1.0 / P).then_inc(S["head_std"], 1)

            def relu(r):
                act.wait_ge(S["idx_scored"], r + 1)
                if r == 2:
                    act.wait_ge(S["idx_used"], 1)
                dst = (work1, work2)[r % 2][:, :, :].rearrange("p (b a) n -> p b (a n)", b=2)
                act.activation(dst, ps[:, 4:6, :], ACT.Relu).then_inc(S["idx_relu"], 1)

            def store_v2(n):
                act.wait_ge(S["turned"], 6 + n + 1)
                act.activation((v_a, v_b)[n // 2][:, n % 2, :, :], ps[:, 7, :].rearrange("p (a n) -> p a n", a=4),
                               ACT.Copy).then_inc(S["v_stored"], 1)

            def exps2(s):
                soften(P * (s % 2 + 1), P ** -0.5)

            def store_p2(s):
                w = 2 * (s % 2 + 1)
                act.wait_ge(S["p_turned"], c.up("p_turned"))
                act.activation(pT2[:, 0:w, :], ps[:, 6, 0:w * P].rearrange("p (w n) -> p w n", w=w), ACT.Copy)\
                   .then_inc(S["pT_ready"], 1)

            def store_o2(s):
                head = 4 * (s // 4) + 2 * (s // 2 % 2)
                cols = slice(P * (s % 2), P * (s % 2) + P)
                act.wait_ge(S["pv_done"], 16 + s + 1)
                act.activation(f[:, head:head + 2, cols], ps[:, 7, 0:2 * P].rearrange("p (a n) -> p a n", a=2), ACT.Copy)\
                   .then_inc(S["o_evicted"], 1)

            def branch_hi(which):
                heads = slice(4 * which, 4 * which + 4)
                act.wait_ge(S["o_evicted"], 16 + 4 * which + 4)
                act.activation(o2_hi[:, heads, :], f[:, heads, 0:SEQ], ACT.Copy).then_inc(S["a_hi_ready"], 1)

            split_to(w_in.u0 + 6)
            split()
            relu(0)
            split()
            relu(1)
            split()
            store_v2(0)
            store_v2(1)
            relu(2)
            split()
            for n, (group, name) in enumerate(((2, "q_a"), (3, "k_a"))):
                split()
                qk_squares(group, name)
                qk_std(n)
                split()
            split()
            store_v2(2)
            store_v2(3)
            exps2(0)
            split()
            store_p2(0)
            exps2(1)
            store_o2(0)
            store_p2(1)
            exps2(2)
            store_o2(1)
            split()
            qk_squares(5, "q_b")
            store_p2(2)
            exps2(3)
            store_o2(2)
            qk_std(2)
            store_p2(3)
            store_o2(3)
            split()
            split()
            qk_squares(6, "k_b")
            qk_std(3)
            split()
            split()
            exps2(4)
            store_p2(4)
            exps2(5)
            store_o2(4)
            split()
            store_p2(5)
            exps2(6)
            store_o2(5)
            store_p2(6)
            exps2(7)
            store_o2(6)
            split()
            store_p2(7)
            store_o2(7)
            for which in range(2):
                branch_hi(which)
            split()
            split()
            split()
            for k in range(4):
                act.wait_ge(S["tile_evicted"], w_in.evicted(w_in.t0 + GROUP * (k + 9)))
                act.activation(gates[:, 4 * k:4 * k + 4, :], gates[:, 4 * k:4 * k + 4, :], ACT.Sigmoid)\
                   .then_inc(S["gate_ready"], 1)
            dsa, moba = stages["br_dsa"], stages["br_moba"]
            split_to(end_of(dsa) + 3)
            split_to(end_of(moba) + 3)
            for m in range(0, 8, 2):
                act.wait_ge(S["act_in_ready"], I0["br"] + m // 2 + 1)
                act.activation(z_hi[:, m:m + 2, :], gates[:, m:m + 2, :], ACT.Copy).then_inc(S["a_hi_ready"], 1)
            up4 = stages["up", 4]
            tail(stages["w_out"], up4, None, full=True, normed=False, bank=side_bank(up4))
            split_to(up4.u0 + 5)
            gate_up(4)
            split_to(n_units)
            n_h = c.now("h_ready")
            for m in range(KT):
                act.wait_ge(S["h_ready"], n_h + m + 1)
                act.dma_start(out[:, m, :], h[:, m, META:TOK]).then_inc(out_stored, 16)


def _constants():
    f32 = np.float32
    con = np.zeros((P, C_ALL), f32)
    con[:, C_ONES:C_ONES + P] = 1
    con[:, C_IDENT:C_IDENT + P] = np.eye(P)

    def swap(block, half):
        r = np.zeros((P, P), f32)
        for b in range(0, P, block):
            for i in range(half):
                r[b + half + i, b + i] = -1
                r[b + i, b + half + i] = 1
        return r

    con[:, C_ROT1:C_ROT1 + P] = swap(64, 8)
    con[:, C_ROT2:C_ROT2 + P] = swap(128, 64)
    con[:, C_ROTI:C_ROTI + P] = swap(64, 32)

    def table(tokens, dim, theta, block):
        half = dim // 2
        inv = (f32(theta) ** (-np.arange(0, dim, 2, dtype=f32) / f32(dim))).astype(f32)
        ang = (np.arange(tokens, dtype=f32)[None, :] * inv[:, None]).astype(f32)
        cos, sin = np.ones((P, tokens), f32), np.zeros((P, tokens), f32)
        for b in range(0, P, block):
            for part in range(2):
                cos[b + part * half:b + (part + 1) * half] = np.cos(ang)
                sin[b + part * half:b + (part + 1) * half] = np.sin(ang)
        return cos, sin

    con[:, C_COS1:C_COS1 + TOK], con[:, C_SIN1:C_SIN1 + TOK] = table(TOK, 16, 500000.0, 64)
    con[:, C_MASK:] = np.where(np.arange(TOK)[None, :] <= META + P + np.arange(P)[:, None], 0, NEG)
    tables2 = np.stack([*table(SEQ, 128, 10000.0, 128), *table(SEQ, 64, 10000.0, 64)], axis=1)
    return con, tables2.astype(f32)


def _layout(a):
    def grouped(w):
        k, m = w.shape
        return w.reshape(k // 512, 4, P, m // 512, 512).transpose(3, 0, 2, 1, 4).reshape(-1, P, UNIT)

    def pairs(w, starts):
        return np.concatenate([w[:, s:s + 256] for s in starts], axis=1)

    def k_outer(w):
        return w.reshape(-1, 2, P, D).transpose(0, 2, 1, 3).reshape(-1, P, UNIT)

    def gate_up(w):
        return grouped(pairs(w, [s for g in range(FT // 2) for s in (256 * g, FF + 256 * g)]))

    units = []
    for i in range(2):
        units += [gate_up(a["ffn1_w_gu"][i]), k_outer(a["ffn1_w_down"][i])]
        if i == 0:
            w = a["conv_w_in"][0]
            units += [grouped(np.concatenate([pairs(w, [s for g in range(4) for s in (D + 256 * g, 2 * D + 256 * g)]),
                                              w[:, 0:D]], axis=1)),
                      k_outer(a["conv_w_out"][0])]
        else:
            w = a["attn_w_qkv"][0]
            v = 2 * D
            units += [grouped(pairs(w, [0, D, v, v + 256, 256, D + 256, 512, D + 512, v + 512, v + 768, 768, D + 768])),
                      k_outer(a["attn_w_o"][0])]
        units += [gate_up(a["ffn2_w_gu"][i]), k_outer(a["ffn2_w_down"][i])]
    w = a["w_in_2"][0]
    key = w[:, 2048:2112]
    small = np.concatenate([key, key, w[:, 2112:2120], np.zeros((D, 120), np.float32)], axis=1)
    units.append(small.reshape(KT, P, 256).transpose(1, 0, 2).reshape(1, P, UNIT))
    starts = (1536, 1024, 0, 512, 3144, 2120, 2632, 3656, 4168, 4680, 5192)
    units.append(grouped(np.concatenate([w[:, s:s + 512] for s in starts], axis=1)))
    units += [k_outer(a["w_br_dsa_2"][0]), k_outer(a["w_br_moba_2"][0]), k_outer(a["w_out_2"][0]),
              gate_up(a["w_gate_up_2"][0]), k_outer(a["w_down_2"][0])]

    mod_units = a["w_mod_2"][0].reshape(P, 8, MOD_UNITS, 256).transpose(2, 0, 1, 3)
    x = np.concatenate([a["meta_tokens"], a["x"][0]], axis=0).reshape(TOK, KT, P).transpose(2, 1, 0)

    def columns(v):
        return v.reshape(-1, P).T

    cols = []
    for i in range(2):
        for name in ("ln_ffn1", "ln_mix", "ln_ffn2"):
            cols += [columns(a[name][i, 0]), columns(a[name][i, 1])]
    cols += [columns(a["conv_w"][0]), columns(a["b_mod_2"][0]), columns(a["g_mix_norm_2"][0]),
             columns(a["g_ffn_norm_2"][0])]
    cols += [columns(a[n][0]) for n in ("g_q_dsa_2", "g_k_dsa_2", "g_q_moba_2", "g_k_moba_2", "attn_subln_g")]
    cols.append(a["c_2"][0].reshape(P, 8))
    cols.append(np.concatenate([a["attn_lambda"][0].T, np.zeros((P - 64, 4), np.float32)], axis=0))
    return np.concatenate(units, axis=0), mod_units, x, np.concatenate(cols, axis=1)


def kernel(**inputs):
    import concourse.bacc as bacc
    from concourse.bass_utils import run_bass_kernel_spmd

    a = {name: np.asarray(value) for name, value in inputs.items()}
    names = ("w_units", "mod_units", "x_in", "vectors", "constants", "tables2")
    arrays = dict(zip(names, (*_layout(a), *_constants())))
    arrays = {name: np.ascontiguousarray(v) for name, v in arrays.items()}
    nc = bacc.Bacc("TRN2", target_bir_lowering=False, num_devices=1)
    args = [nc.dram_tensor(name, v.shape, F32, kind="ExternalInput").ap() for name, v in arrays.items()]
    out = nc.dram_tensor("out", (P, KT, SEQ), F32, kind="ExternalOutput").ap()
    build(nc, *args, out)
    r = run_bass_kernel_spmd(nc, [arrays], core_ids=[0])
    got = r.results[0]["out"]
    return np.ascontiguousarray(got.transpose(2, 1, 0)).reshape(1, SEQ, D)
```
